# Optimizing a Trainium2 kernel written in Bass

```python
import math
import jax
import jax.numpy as jnp
from jax import lax
import numpy as np

D_MODEL = 1024
BATCH = 1
SEQ = 256
DEPTH = 2

N_MIXERS = 2
HEAD_DIM = 64
N_HEADS = D_MODEL // HEAD_DIM
ATTN_WIDTH = N_HEADS * HEAD_DIM
ROPE_THETA = 10000.0
NORM_EPS = 1e-6

NSA_KV_HEADS = 2
NSA_GROUP = N_HEADS // NSA_KV_HEADS
NSA_KV_WIDTH = NSA_KV_HEADS * HEAD_DIM
NSA_BRANCHES = 3
CMP_LEN = 32
CMP_STRIDE = 16
CMP_HIDDEN = 256
SLC_LEN = 64
SLC_TOP = 16
WIN_LEN = 512
NSA_IN = ATTN_WIDTH + 6 * NSA_KV_WIDTH + ATTN_WIDTH + NSA_BRANCHES * N_HEADS
SLC_Q_BLOCK = 32
WIN_Q_BLOCK = 128

DIL_PATTERNS = ((128, 1), (512, 4), (2048, 16))
DIL_GROUP_HEADS = (N_HEADS - 2 * (N_HEADS // 3), N_HEADS // 3, N_HEADS // 3)
DIL_IN = 4 * ATTN_WIDTH
DIL_Q_BLOCK = 32


def rms_norm(x, g):
    xf = x.astype(jnp.float32)
    y = xf * lax.rsqrt(jnp.mean(xf * xf, axis=-1, keepdims=True) + NORM_EPS)
    return (y * g.astype(jnp.float32)).astype(x.dtype)

def rope(x):
    T = x.shape[1]
    half = x.shape[-1] // 2
    inv = ROPE_THETA ** (-jnp.arange(half, dtype=jnp.float32) / half)
    ang = jnp.arange(T, dtype=jnp.float32)[:, None] * inv[None, :]
    cos = jnp.cos(ang)[None, :, None, :]
    sin = jnp.sin(ang)[None, :, None, :]
    xf = x.astype(jnp.float32)
    x1, x2 = xf[..., :half], xf[..., half:]
    return jnp.concatenate([x1 * cos - x2 * sin, x2 * cos + x1 * sin], axis=-1).astype(x.dtype)

def masked_softmax(s, mask):
    s = jnp.where(mask, s.astype(jnp.float32), -jnp.inf)
    m = jnp.max(s, axis=-1, keepdims=True)
    m = jnp.where(jnp.isfinite(m), m, 0.0)
    e = jnp.exp(s - m)
    den = jnp.sum(e, axis=-1, keepdims=True)
    return e / jnp.where(den > 0, den, 1.0)

def adaln_norm(x, c, g, w_ada, b_ada):
    mod = jax.nn.silu(c) @ w_ada + b_ada
    shift, scale, gate = jnp.split(mod, 3, axis=-1)
    h = rms_norm(x, g) * (1.0 + scale[:, None, :]) + shift[:, None, :]
    return h, gate[:, None, :]

def nsa_mixer(h, w_in, pe_k, pe_v, ck_w1, ck_w2, cv_w1, cv_w2, w_out):
    B, T, _ = h.shape
    G, HG, DH = NSA_KV_HEADS, NSA_GROUP, HEAD_DIM
    scale = DH ** -0.5
    u = h @ w_in
    cuts = np.cumsum([ATTN_WIDTH] + [NSA_KV_WIDTH] * 6 + [ATTN_WIDTH]).tolist()
    q, k_c, v_c, k_s, v_s, k_w, v_w, z, g_logit = jnp.split(u, cuts, axis=-1)
    k_c, v_c, k_s, v_s, k_w, v_w = [a.reshape(B, T, G, DH) for a in (k_c, v_c, k_s, v_s, k_w, v_w)]
    gates = jax.nn.sigmoid(g_logit.astype(jnp.float32)).reshape(B, T, G, HG, NSA_BRANCHES).astype(h.dtype)
    t = jnp.arange(T)

    q_plain = q.reshape(B, T, G, HG, DH)
    n_cmp = (T - CMP_LEN) // CMP_STRIDE + 1
    cmp_idx = CMP_STRIDE * np.arange(n_cmp)[:, None] + np.arange(CMP_LEN)[None, :]

    def compress(a, pe, w1, w2):
        blk = a[:, cmp_idx] + pe[:, None, :]
        blk = jnp.moveaxis(blk, 3, 2).reshape(B, n_cmp, G, CMP_LEN * DH)
        return jax.nn.silu(blk @ w1) @ w2

    k_cmp = compress(k_c, pe_k, ck_w1, ck_w2)
    v_cmp = compress(v_c, pe_v, cv_w1, cv_w2)
    cmp_end = CMP_STRIDE * jnp.arange(n_cmp) + CMP_LEN - 1
    cmask = cmp_end[None, :] <= t[:, None]
    s_cmp = jnp.einsum('btghd,bngd->btghn', q_plain, k_cmp) * scale
    p_cmp = masked_softmax(s_cmp, cmask[None, :, None, None, :])
    o_cmp = jnp.einsum('btghn,bngd->btghd', p_cmp.astype(v_cmp.dtype), v_cmp)

    n_slc = T // SLC_LEN
    c_start = CMP_STRIDE * np.arange(n_cmp)
    s_start = SLC_LEN * np.arange(n_slc)
    overlap = ((c_start[:, None] < s_start[None, :] + SLC_LEN)
               & (c_start[:, None] + CMP_LEN > s_start[None, :])).astype(np.float32)
    p_slc = jnp.einsum('btghn,nj->btgj', p_cmp, overlap)
    jblk = jnp.arange(n_slc)[None, :]
    cur = (t // SLC_LEN)[:, None]
    visible = jblk <= cur
    forced = (jblk == 0) | (jblk == cur) | (jblk == cur - 1)
    rank = jnp.where(forced[None, :, None, :], jnp.inf,
                     jnp.where(visible[None, :, None, :], p_slc, -jnp.inf))
    n_top = min(SLC_TOP, n_slc)
    top_val, top_idx = lax.top_k(rank, n_top)
    top_ok = top_val > -jnp.inf

    q_r = rope(q.reshape(B, T, N_HEADS, DH)).reshape(B, T, G, HG, DH)
    k_s = rope(k_s)
    k_w = rope(k_w)

    k_blk = k_s.reshape(B, n_slc, SLC_LEN, G, DH).transpose(0, 3, 1, 2, 4)
    v_blk = v_s.reshape(B, n_slc, SLC_LEN, G, DH).transpose(0, 3, 1, 2, 4)
    C = SLC_Q_BLOCK
    n_qb = T // C
    q_sb = jnp.moveaxis(q_r.reshape(B, n_qb, C, G, HG, DH), 1, 0)
    idx_sb = jnp.moveaxis(top_idx.reshape(B, n_qb, C, G, n_top), 1, 0)
    ok_sb = jnp.moveaxis(top_ok.reshape(B, n_qb, C, G, n_top), 1, 0)
    gather_blocks = jax.vmap(jax.vmap(lambda blk, ix: blk[ix]))

    def slc_block(args):
        s0, qq, ii, ok = args
        ii_g = jnp.swapaxes(ii, 1, 2)
        kg = gather_blocks(k_blk, ii_g)
        vg = gather_blocks(v_blk, ii_g)
        s = jnp.einsum('bcghd,bgcnld->bcghnl', qq, kg) * scale
        tq = s0 + jnp.arange(C)
        kpos = ii[..., None] * SLC_LEN + jnp.arange(SLC_LEN)
        mask = (kpos <= tq[None, :, None, None, None]) & ok[..., None]
        p = masked_softmax(s.reshape(B, C, G, HG, n_top * SLC_LEN),
                           mask.reshape(B, C, G, 1, n_top * SLC_LEN))
        return jnp.einsum('bcghnl,bgcnld->bcghd', p.reshape(s.shape).astype(vg.dtype), vg)

    o_slc = lax.map(slc_block, (jnp.arange(n_qb) * C, q_sb, idx_sb, ok_sb))
    o_slc = jnp.moveaxis(o_slc, 0, 1).reshape(B, T, G, HG, DH)

    span = WIN_LEN + WIN_Q_BLOCK
    n_wb = T // WIN_Q_BLOCK
    k_pad = jnp.pad(k_w, ((0, 0), (WIN_LEN, 0), (0, 0), (0, 0)))
    v_pad = jnp.pad(v_w, ((0, 0), (WIN_LEN, 0), (0, 0), (0, 0)))
    q_wb = jnp.moveaxis(q_r.reshape(B, n_wb, WIN_Q_BLOCK, G, HG, DH), 1, 0)

    def win_block(args):
        s0, qq = args
        kk = lax.dynamic_slice_in_dim(k_pad, s0, span, axis=1)
        vv = lax.dynamic_slice_in_dim(v_pad, s0, span, axis=1)
        s = jnp.einsum('bcghd,bkgd->bcghk', qq, kk) * scale
        tq = s0 + jnp.arange(WIN_Q_BLOCK)
        kpos = s0 - WIN_LEN + jnp.arange(span)
        mask = ((kpos[None, :] <= tq[:, None]) & (kpos[None, :] > tq[:, None] - WIN_LEN)
                & (kpos[None, :] >= 0))
        p = masked_softmax(s, mask[None, :, None, None, :])
        return jnp.einsum('bcghk,bkgd->bcghd', p.astype(vv.dtype), vv)

    o_win = lax.map(win_block, (jnp.arange(n_wb) * WIN_Q_BLOCK, q_wb))
    o_win = jnp.moveaxis(o_win, 0, 1).reshape(B, T, G, HG, DH)

    o = gates[..., 0:1] * o_cmp + gates[..., 1:2] * o_slc + gates[..., 2:3] * o_win
    o = o.reshape(B, T, ATTN_WIDTH)
    return (o * jax.nn.silu(z)) @ w_out

def dilated_mixer(h, w_in, w_out):
    B, T, _ = h.shape
    DH = HEAD_DIM
    scale = DH ** -0.5
    n_grp = len(DIL_PATTERNS)
    q, k, v, z = jnp.split(h @ w_in, 4, axis=-1)
    q = rope(q.reshape(B, T, N_HEADS, DH))
    k = rope(k.reshape(B, T, N_HEADS, DH))
    v = v.reshape(B, T, N_HEADS, DH)
    offs = np.cumsum((0,) + DIL_GROUP_HEADS).tolist()
    k_grp = [k[:, :, offs[i]:offs[i + 1]] for i in range(n_grp)]
    v_grp = [v[:, :, offs[i]:offs[i + 1]] for i in range(n_grp)]
    C = DIL_Q_BLOCK
    n_qb = T // C
    q_blocks = jnp.moveaxis(q.reshape(B, n_qb, C, N_HEADS, DH), 1, 0)

    def block(args):
        s0, qb = args
        tq = s0 + jnp.arange(C)
        outs, lses = [], []
        for gi, (win, dil) in enumerate(DIL_PATTERNS):
            n_k = win // dil + 1
            kpos = tq[:, None] - dil * jnp.arange(n_k)[None, :]
            ok = kpos >= 0
            kidx = jnp.maximum(kpos, 0)
            kg = k_grp[gi][:, kidx]
            vg = v_grp[gi][:, kidx]
            qg = qb[:, :, offs[gi]:offs[gi + 1]]
            s = jnp.einsum('bchd,bckhd->bchk', qg, kg).astype(jnp.float32) * scale
            s = jnp.where(ok[None, :, None, :], s, -jnp.inf)
            m = jnp.max(s, axis=-1, keepdims=True)
            e = jnp.exp(s - m)
            den = jnp.sum(e, axis=-1, keepdims=True)
            outs.append(jnp.einsum('bchk,bckhd->bchd', (e / den).astype(vg.dtype), vg))
            lse = (m + jnp.log(den))[..., 0]
            lses.append(jax.nn.logsumexp(lse, axis=-1) - math.log(DIL_GROUP_HEADS[gi]))
        alpha = jax.nn.softmax(jnp.stack(lses, axis=-1), axis=-1) * n_grp
        return jnp.concatenate(
            [outs[i] * alpha[:, :, i, None, None].astype(outs[i].dtype) for i in range(n_grp)], axis=2)

    o = lax.map(block, (jnp.arange(n_qb) * C, q_blocks))
    o = jnp.moveaxis(o, 0, 1).reshape(B, T, ATTN_WIDTH)
    return (o * jax.nn.silu(z)) @ w_out

def first_inputs(seed: int = 0) -> dict:
    key = jax.random.key(seed)
    ks = jax.random.split(key, 16)
    n_a = len(range(0, DEPTH, N_MIXERS))
    n_b = len(range(1, DEPTH, N_MIXERS))
    D = D_MODEL

    def nrm(k, shape, s):
        return jax.random.normal(k, shape, jnp.float32) * s

    return {
        "x": nrm(ks[0], (BATCH, SEQ, D), 1.0),
        "c": nrm(ks[1], (BATCH, D), 1.0),
        "norm_g": 1.0 + nrm(ks[2], (DEPTH, D), 0.05),
        "ada_w": nrm(ks[3], (DEPTH, D, 3 * D), 0.5 * D ** -0.5),
        "ada_b": nrm(ks[4], (DEPTH, 3 * D), 0.02),
        "nsa_w_in": nrm(ks[5], (n_a, D, NSA_IN), D ** -0.5),
        "nsa_pe_k": nrm(ks[6], (n_a, CMP_LEN, HEAD_DIM), 0.1),
        "nsa_pe_v": nrm(ks[7], (n_a, CMP_LEN, HEAD_DIM), 0.1),
        "nsa_ck_w1": nrm(ks[8], (n_a, CMP_LEN * HEAD_DIM, CMP_HIDDEN), (CMP_LEN * HEAD_DIM) ** -0.5),
        "nsa_ck_w2": nrm(ks[9], (n_a, CMP_HIDDEN, HEAD_DIM), CMP_HIDDEN ** -0.5),
        "nsa_cv_w1": nrm(ks[10], (n_a, CMP_LEN * HEAD_DIM, CMP_HIDDEN), (CMP_LEN * HEAD_DIM) ** -0.5),
        "nsa_cv_w2": nrm(ks[11], (n_a, CMP_HIDDEN, HEAD_DIM), CMP_HIDDEN ** -0.5),
        "nsa_w_out": nrm(ks[12], (n_a, ATTN_WIDTH, D), ATTN_WIDTH ** -0.5),
        "dil_w_in": nrm(ks[13], (n_b, D, DIL_IN), D ** -0.5),
        "dil_w_out": nrm(ks[14], (n_b, ATTN_WIDTH, D), ATTN_WIDTH ** -0.5),
        "final_g": 1.0 + nrm(ks[15], (D,), 0.05),
    }

def first_block(x, c, norm_g, ada_w, ada_b, nsa_w_in, nsa_pe_k, nsa_pe_v, nsa_ck_w1, nsa_ck_w2,
              nsa_cv_w1, nsa_cv_w2, nsa_w_out, dil_w_in, dil_w_out, final_g):
    for i in range(DEPTH):
        h, gate = adaln_norm(x, c, norm_g[i], ada_w[i], ada_b[i])
        j = i // N_MIXERS
        if i % N_MIXERS == 0:
            y = nsa_mixer(h, nsa_w_in[j], nsa_pe_k[j], nsa_pe_v[j], nsa_ck_w1[j], nsa_ck_w2[j],
                          nsa_cv_w1[j], nsa_cv_w2[j], nsa_w_out[j])
        else:
            y = dilated_mixer(h, dil_w_in[j], dil_w_out[j])
        x = x + gate * y
    return rms_norm(x, final_g)


CHUNK = 64
Q_BLOCK = 128
NEG_INF = -1e30
LN_EPS = 1e-5
RMS_EPS = 1e-6

MLA_HEADS = 8
MLA_Q_RANK = 384
MLA_KV_RANK = 256
MLA_NOPE = 64
MLA_ROPE = 32
MLA_V = 64

SWA_HEADS = 8
SWA_KV_HEADS = 2
SWA_WINDOW = 128
SWA_LEFT_CHUNKS = SWA_WINDOW // CHUNK

FOX_HEADS = 8

CK_HEADS = 8
CK_LEFT_CHUNKS = 8
REL_MAX = 256
REL_TABLE = REL_MAX + CHUNK

D_FF = -(-8 * D_MODEL // (3 * 256)) * 256

DEEPNORM_ALPHA = (2 * DEPTH) ** 0.25
DEEPNORM_BETA = (8 * DEPTH) ** -0.25

AB_SPLITS = (MLA_Q_RANK, MLA_KV_RANK, MLA_ROPE, SWA_HEADS * HEAD_DIM, SWA_KV_HEADS * HEAD_DIM, SWA_KV_HEADS * HEAD_DIM)
CD_SPLITS = (FOX_HEADS * HEAD_DIM,) * 3 + (FOX_HEADS,) + (CK_HEADS * HEAD_DIM,) * 3
AB_MIX = MLA_HEADS * MLA_V + SWA_HEADS * HEAD_DIM
CD_MIX = (FOX_HEADS + CK_HEADS) * HEAD_DIM


def _split_cols(x, widths):
    return jnp.split(x, [int(i) for i in np.cumsum(widths)[:-1]], axis=-1)

def _layer_norm(x, g, b):
    xf = x.astype(jnp.float32)
    mu = jnp.mean(xf, -1, keepdims=True)
    var = jnp.mean(jnp.square(xf - mu), -1, keepdims=True)
    y = (xf - mu) * lax.rsqrt(var + LN_EPS) * g.astype(jnp.float32) + b.astype(jnp.float32)
    return y.astype(x.dtype)

def _rms_norm(x, g):
    xf = x.astype(jnp.float32)
    y = xf * lax.rsqrt(jnp.mean(xf * xf, -1, keepdims=True) + RMS_EPS)
    return (y * g.astype(jnp.float32)).astype(x.dtype)

def _rope_tables(S):
    inv = ROPE_THETA ** (-jnp.arange(0, MLA_ROPE, 2, dtype=jnp.float32) / MLA_ROPE)
    ang = jnp.arange(S, dtype=jnp.float32)[:, None] * inv[None, :]
    return jnp.cos(ang), jnp.sin(ang)

def _apply_rope(x, cos, sin):
    x1, x2 = jnp.split(x.astype(jnp.float32), 2, axis=-1)
    return jnp.concatenate([x1 * cos - x2 * sin, x1 * sin + x2 * cos], -1).astype(x.dtype)

def _alibi_slopes(n):
    return jnp.exp2(-8.0 * jnp.arange(1, n + 1, dtype=jnp.float32) / n)

def _sweep_query_blocks(block_fn, *q_parts):
    B, S = q_parts[0].shape[:2]
    nb = S // Q_BLOCK
    blocked = tuple(jnp.moveaxis(p.reshape(B, nb, Q_BLOCK, *p.shape[2:]), 1, 0) for p in q_parts)
    out = lax.map(lambda a: block_fn(a[0], *a[1]), (jnp.arange(nb), blocked))
    return jnp.moveaxis(out, 0, 1).reshape(B, S, *out.shape[3:])

def _band(x, n_left):
    B, S = x.shape[:2]
    nc = S // CHUNK
    pad = [(0, 0), (n_left * CHUNK, 0)] + [(0, 0)] * (x.ndim - 2)
    xp = jnp.pad(x, pad).reshape(B, nc + n_left, CHUNK, *x.shape[2:])
    return jnp.concatenate([xp[:, j:j + nc] for j in range(n_left + 1)], axis=2)

def _band_geometry(nc, n_left):
    band = jnp.arange((n_left + 1) * CHUNK)
    key_off = band // CHUNK - n_left
    dist = jnp.arange(CHUNK)[:, None] - (key_off * CHUNK + band % CHUNK)[None, :]
    valid = (jnp.arange(nc)[:, None] + key_off[None, :]) >= 0
    return dist, valid

def _mla_attention(q_nope, q_rope, k_nope, k_rope, v):
    S = k_nope.shape[1]
    scale = (MLA_NOPE + MLA_ROPE) ** -0.5
    key_chunk = jnp.arange(S) // CHUNK

    def block(i, qn, qr):
        q_chunk = (i * Q_BLOCK + jnp.arange(Q_BLOCK)) // CHUNK
        logits = (jnp.einsum('bqhd,bkhd->bhqk', qn, k_nope, preferred_element_type=jnp.float32)
                  + jnp.einsum('bqhr,bkr->bhqk', qr, k_rope, preferred_element_type=jnp.float32)) * scale
        logits = jnp.where(key_chunk[None, :] <= q_chunk[:, None], logits, NEG_INF)
        p = jax.nn.softmax(logits, axis=-1).astype(v.dtype)
        return jnp.einsum('bhqk,bkhd->bqhd', p, v)

    return _sweep_query_blocks(block, q_nope, q_rope)

def _swa_sink_attention(q, k, v, sinks):
    B, S, _, d = q.shape
    nc = S // CHUNK
    G = SWA_HEADS // SWA_KV_HEADS
    qc = q.reshape(B, nc, CHUNK, SWA_KV_HEADS, G, d)
    kb, vb = _band(k, SWA_LEFT_CHUNKS), _band(v, SWA_LEFT_CHUNKS)
    dist, valid = _band_geometry(nc, SWA_LEFT_CHUNKS)
    alibi = -_alibi_slopes(SWA_HEADS).reshape(SWA_KV_HEADS, G, 1, 1) * jnp.abs(dist).astype(jnp.float32)
    logits = jnp.einsum('bcqkgd,bcskd->bckgqs', qc, kb, preferred_element_type=jnp.float32) * d ** -0.5 + alibi
    logits = jnp.where(valid[None, :, None, None, None, :], logits, NEG_INF)
    sink = jnp.broadcast_to(sinks.astype(jnp.float32).reshape(SWA_KV_HEADS, G, 1, 1), logits.shape[:-1] + (1,))
    p = jax.nn.softmax(jnp.concatenate([logits, sink], -1), axis=-1)[..., :-1].astype(v.dtype)
    return jnp.einsum('bckgqs,bcskd->bcqkgd', p, vb).reshape(B, S, SWA_HEADS, d)

def _forgetting_attention(q, k, v, f_logit, b_forget):
    S = k.shape[1]
    scale = q.shape[-1] ** -0.5
    cum_log_f = jnp.cumsum(jax.nn.log_sigmoid(f_logit.astype(jnp.float32) + b_forget.astype(jnp.float32)), axis=1)
    cum_k = jnp.swapaxes(cum_log_f, 1, 2)[:, :, None, :]
    key_pos = jnp.arange(S)

    def block(i, qb, cum_q):
        q_pos = i * Q_BLOCK + jnp.arange(Q_BLOCK)
        decay = jnp.swapaxes(cum_q, 1, 2)[..., None] - cum_k
        logits = jnp.einsum('bqhd,bkhd->bhqk', qb, k, preferred_element_type=jnp.float32) * scale + decay
        logits = jnp.where(key_pos[None, :] <= q_pos[:, None], logits, NEG_INF)
        p = jax.nn.softmax(logits, axis=-1).astype(v.dtype)
        return jnp.einsum('bhqk,bkhd->bqhd', p, v)

    return _sweep_query_blocks(block, q, cum_log_f)

def _chunk_relpos_attention(q, k, v, rel_bias):
    B, S, H, d = q.shape
    nc = S // CHUNK
    qc = q.reshape(B, nc, CHUNK, H, d)
    kb, vb = _band(k, CK_LEFT_CHUNKS), _band(v, CK_LEFT_CHUNKS)
    dist, valid = _band_geometry(nc, CK_LEFT_CHUNKS)
    idx = jnp.clip(dist, -(CHUNK - 1), REL_MAX) + (CHUNK - 1)
    bias = jnp.moveaxis(rel_bias[idx], -1, 0).astype(jnp.float32)
    logits = jnp.einsum('bcqhd,bcshd->bchqs', qc, kb, preferred_element_type=jnp.float32) * d ** -0.5 + bias
    logits = jnp.where(valid[None, :, None, None, :], logits, NEG_INF)
    p = jax.nn.softmax(logits, axis=-1).astype(v.dtype)
    return jnp.einsum('bchqs,bcshd->bcqhd', p, vb).reshape(B, S, H, d)

def _mixer_ab(h, w_in, q_norm, w_uq, kv_norm, w_ukv, sinks, w_out, cos, sin):
    B, S, _ = h.shape
    proj = jnp.einsum('bsd,df->bsf', h, w_in)
    c_q, c_kv, k_r, q_s, k_s, v_s = _split_cols(proj, AB_SPLITS)
    q = jnp.einsum('bsr,rf->bsf', _rms_norm(c_q, q_norm), w_uq).reshape(B, S, MLA_HEADS, MLA_NOPE + MLA_ROPE)
    q_nope = q[..., :MLA_NOPE]
    q_rope = _apply_rope(q[..., MLA_NOPE:], cos[None, :, None], sin[None, :, None])
    kv = jnp.einsum('bsr,rf->bsf', _rms_norm(c_kv, kv_norm), w_ukv).reshape(B, S, MLA_HEADS, MLA_NOPE + MLA_V)
    k_rope = _apply_rope(k_r, cos[None], sin[None])
    o_a = _mla_attention(q_nope, q_rope, kv[..., :MLA_NOPE], k_rope, kv[..., MLA_NOPE:])
    o_b = _swa_sink_attention(q_s.reshape(B, S, SWA_HEADS, HEAD_DIM),
                              k_s.reshape(B, S, SWA_KV_HEADS, HEAD_DIM),
                              v_s.reshape(B, S, SWA_KV_HEADS, HEAD_DIM), sinks)
    o = jnp.concatenate([o_a.reshape(B, S, -1), o_b.reshape(B, S, -1)], -1)
    return jnp.einsum('bsf,fd->bsd', o, w_out)

def _mixer_cd(h, w_in, b_forget, rel_bias, w_out):
    B, S, _ = h.shape
    proj = jnp.einsum('bsd,df->bsf', h, w_in)
    q_f, k_f, v_f, f_logit, q_c, k_c, v_c = _split_cols(proj, CD_SPLITS)
    o_c = _forgetting_attention(q_f.reshape(B, S, FOX_HEADS, HEAD_DIM), k_f.reshape(B, S, FOX_HEADS, HEAD_DIM),
                                v_f.reshape(B, S, FOX_HEADS, HEAD_DIM), f_logit, b_forget)
    o_d = _chunk_relpos_attention(q_c.reshape(B, S, CK_HEADS, HEAD_DIM), k_c.reshape(B, S, CK_HEADS, HEAD_DIM),
                                  v_c.reshape(B, S, CK_HEADS, HEAD_DIM), rel_bias)
    o = jnp.concatenate([o_c.reshape(B, S, -1), o_d.reshape(B, S, -1)], -1)
    return jnp.einsum('bsf,fd->bsd', o, w_out)

def _swiglu(x, w_gate, w_up, w_down):
    g = jnp.einsum('bsd,df->bsf', x, w_gate)
    u = jnp.einsum('bsd,df->bsf', x, w_up)
    return jnp.einsum('bsf,fd->bsd', jax.nn.silu(g) * u, w_down)

def second_inputs(seed: int = 0) -> dict:
    key = jax.random.key(seed)
    ks = jax.random.split(key, 20)
    ne, no = (DEPTH + 1) // 2, DEPTH // 2
    f32 = jnp.float32

    def normal(k, shape, scale):
        return jax.random.normal(k, shape, f32) * scale

    def gain(k, shape):
        return 1.0 + normal(k, shape, 0.02)

    return {
        'x': normal(ks[0], (BATCH, SEQ, D_MODEL), 1.0),
        'ab_w_in': normal(ks[1], (ne, D_MODEL, sum(AB_SPLITS)), D_MODEL ** -0.5),
        'ab_q_norm': gain(ks[2], (ne, MLA_Q_RANK)),
        'ab_w_uq': normal(ks[3], (ne, MLA_Q_RANK, MLA_HEADS * (MLA_NOPE + MLA_ROPE)), MLA_Q_RANK ** -0.5),
        'ab_kv_norm': gain(ks[4], (ne, MLA_KV_RANK)),
        'ab_w_ukv': normal(ks[5], (ne, MLA_KV_RANK, MLA_HEADS * (MLA_NOPE + MLA_V)), MLA_KV_RANK ** -0.5),
        'ab_sinks': normal(ks[6], (ne, SWA_HEADS), 0.5),
        'ab_w_out': normal(ks[7], (ne, AB_MIX, D_MODEL), DEEPNORM_BETA * AB_MIX ** -0.5),
        'cd_w_in': normal(ks[8], (no, D_MODEL, sum(CD_SPLITS)), D_MODEL ** -0.5),
        'cd_b_forget': jax.random.uniform(ks[9], (no, FOX_HEADS), dtype=f32, minval=1.0, maxval=5.0),
        'cd_rel_bias': normal(ks[10], (no, REL_TABLE, CK_HEADS), 0.2),
        'cd_w_out': normal(ks[11], (no, CD_MIX, D_MODEL), DEEPNORM_BETA * CD_MIX ** -0.5),
        'ln1_g': gain(ks[12], (DEPTH, D_MODEL)),
        'ln1_b': normal(ks[13], (DEPTH, D_MODEL), 0.02),
        'ffn_w_gate': normal(ks[14], (DEPTH, D_MODEL, D_FF), D_MODEL ** -0.5),
        'ffn_w_up': normal(ks[15], (DEPTH, D_MODEL, D_FF), D_MODEL ** -0.5),
        'ffn_w_down': normal(ks[16], (DEPTH, D_FF, D_MODEL), DEEPNORM_BETA * D_FF ** -0.5),
        'ln2_g': gain(ks[17], (DEPTH, D_MODEL)),
        'ln2_b': normal(ks[18], (DEPTH, D_MODEL), 0.02),
    }

def second_block(x, ab_w_in, ab_q_norm, ab_w_uq, ab_kv_norm, ab_w_ukv, ab_sinks, ab_w_out,
              cd_w_in, cd_b_forget, cd_rel_bias, cd_w_out,
              ln1_g, ln1_b, ffn_w_gate, ffn_w_up, ffn_w_down, ln2_g, ln2_b):
    cos, sin = _rope_tables(x.shape[1])
    for layer in range(DEPTH):
        i = layer // 2
        if layer % 2 == 0:
            mix = _mixer_ab(x, ab_w_in[i], ab_q_norm[i], ab_w_uq[i], ab_kv_norm[i], ab_w_ukv[i],
                            ab_sinks[i], ab_w_out[i], cos, sin)
        else:
            mix = _mixer_cd(x, cd_w_in[i], cd_b_forget[i], cd_rel_bias[i], cd_w_out[i])
        x = _layer_norm(DEEPNORM_ALPHA * x + mix, ln1_g[layer], ln1_b[layer])
        ffn = _swiglu(x, ffn_w_gate[layer], ffn_w_up[layer], ffn_w_down[layer])
        x = _layer_norm(DEEPNORM_ALPHA * x + ffn, ln2_g[layer], ln2_b[layer])
    return x


def setup_inputs(seed=0):
    out = dict(first_inputs(seed))
    for name, value in second_inputs(seed + 1).items():
        if name != "x":
            out[name + "_2"] = value
    return out


def reference(
    x, c, norm_g, ada_w, ada_b, nsa_w_in, nsa_pe_k, nsa_pe_v, nsa_ck_w1, nsa_ck_w2, nsa_cv_w1,
    nsa_cv_w2, nsa_w_out, dil_w_in, dil_w_out, final_g, ab_w_in_2, ab_q_norm_2, ab_w_uq_2,
    ab_kv_norm_2, ab_w_ukv_2, ab_sinks_2, ab_w_out_2, cd_w_in_2, cd_b_forget_2, cd_rel_bias_2,
    cd_w_out_2, ln1_g_2, ln1_b_2, ffn_w_gate_2, ffn_w_up_2, ffn_w_down_2, ln2_g_2, ln2_b_2,
):
    x = first_block(
        x, c, norm_g, ada_w, ada_b, nsa_w_in, nsa_pe_k, nsa_pe_v, nsa_ck_w1, nsa_ck_w2,
        nsa_cv_w1, nsa_cv_w2, nsa_w_out, dil_w_in, dil_w_out, final_g,
    )
    return second_block(
        x, ab_w_in_2, ab_q_norm_2, ab_w_uq_2, ab_kv_norm_2, ab_w_ukv_2, ab_sinks_2, ab_w_out_2,
        cd_w_in_2, cd_b_forget_2, cd_rel_bias_2, cd_w_out_2, ln1_g_2, ln1_b_2, ffn_w_gate_2,
        ffn_w_up_2, ffn_w_down_2, ln2_g_2, ln2_b_2,
    )


_drawn_inputs = setup_inputs


def setup_inputs(seed=0):
    import zlib

    import numpy as np

    out = dict(_drawn_inputs(seed))
    spreads = {}
    factors = {'norm_g': 4.83,
     'ada_b': 4.11,
     'nsa_pe_k': 8.0,
     'nsa_pe_v': 8.0,
     'nsa_ck_w1': 3.87,
     'nsa_ck_w2': 3.81,
     'ab_q_norm_2': 8.0,
     'ab_kv_norm_2': 8.0,
     'ab_sinks_2': 8.0,
     'cd_rel_bias_2': 7.991}
    for name, (base, spread) in spreads.items():
        noise = np.random.default_rng([zlib.crc32(name.encode()), seed]).standard_normal(out[name].shape)
        drawn = base * np.exp(spread * noise) if base else spread * noise
        out[name] = jnp.asarray(drawn.astype(out[name].dtype))
    for name, factor in factors.items():
        out[name] = (out[name] * factor).astype(out[name].dtype)
    return out
```

```python
from contextlib import ExitStack

import numpy as np

import concourse.bass as bass
from concourse import mybir

P = 128
D = 1024
T = 256
NT = T // P
KT = D // P
H = 16
DH = 64
HALF = DH // 2
SLOTS = 4
SLOT = 3080
ADA_C, ADA_W = 8, 384
NSA_C, NSA_W = 8, 358
DIL_C, DIL_W = 16, 256
AB_C, AB_W = 4, 360
CD_C, CD_W = 8, 385
OUT_C, OUT_W = 4, 256
FF_STEPS = 22
NCMP = 15
EPS_RMS = 1e-6
EPS_LN = 1e-5
ALPHA = 4.0 ** 0.25
SCALE = DH ** -0.5
MLA_SCALE = 96 ** -0.5
SW = 3 * P
FOXW = DH + 2

ALU = mybir.AluOpType
ACT = mybir.ActivationFunctionType
F32 = mybir.dt.float32
AX = mybir.AxisListType

TAB = {}
_at = 0
for _name, _n in (("ident", P), ("flip", P), ("tri", P), ("cos", NT * HALF), ("sin", NT * HALF), ("cos_m", NT * 16),
                  ("sin_m", NT * 16), ("causal", SW), ("dil0", SW), ("dil1", SW), ("dil2", SW),
                  ("chunk", SW), ("cneg", NT * NCMP), ("cone", NT * NCMP)):
    TAB[_name] = (_at, _at + _n)
    _at += _n
TAB_W = _at

VECS = ("norm_g0", "norm_g1", "final_g", "ln1_g0", "ln1_b0", "ln2_g0", "ln2_b0", "ln1_g1", "ln1_b1", "ln2_g1", "ln2_b1")


class Tally:

    def __init__(self, eng, own):
        self.eng, self.own, self.n, self.turns = eng, own, {}, None

    def mark(self, ins, sem):
        ins.then_inc(sem, 1)
        self.n[sem.name] = self.n.get(sem.name, 0) + 1

    def done(self, ins, sem=None):
        sem = self.own if sem is None else sem
        self.mark(ins, sem)
        self.eng.wait_ge(sem, self.n[sem.name] + (0 if self.turns is None else self.turns * self.per[sem.name]))

    def enter(self, turns, per):
        self.turns, self.per = turns, {k.name: v for k, v in per.items()}

    def leave(self, times):
        for name, per in self.per.items():
            self.n[name] += per * (times - 1)
        self.turns = None


SMALL_LOADS = 9


class Signals:

    def __init__(self, ctx, nc, stage, names):
        self.s = {n: ctx.enter_context(nc.semaphore(f"{stage}_{n}")) for n in names.split()}

    def __getitem__(self, n):
        return self.s[n]


def over(ap, axis, n):
    a = ap.unsqueeze(axis)
    shape = list(a.shape)
    shape[axis] = n
    return a.broadcast_to(shape)


def two_stacks(nc, a, out):
    with ExitStack() as ctx:
        def sb(name, shape, dt=F32):
            return ctx.enter_context(nc.sbuf_tensor(name, shape, dt))

        def sem(name):
            return ctx.enter_context(nc.semaphore(name))

        def stage(name, names):
            return Signals(ctx, nc, name, names)

        x = sb("x", [P, NT, D])
        tok = sb("tok", [P, NT, D])
        rotk = sb("rotk", [P, NT, D])
        hT = sb("hT", [P, KT, T])
        u = sb("u", [P, NT, 4 * D])
        qT = sb("qT", [P, 8, T])
        kT = sb("kT", [P, 8, T])
        q2T = sb("q2T", [P, 8, T])
        ring = sb("ring", [P, SLOTS, SLOT])
        tab = sb("tab", [P, TAB_W])
        mod0 = sb("mod0", [P, 3 * D])
        bias8 = sb("bias8", [P, 8 * SW])
        vec = sb("vec", [P, 2, D])
        small = sb("small", [P, 384 + 256 + 8 + 8 + KT])
        acc = sb("acc", [P, 2, ADA_W])
        tmp = sb("tmp", [P, 2, 512])
        scr = sb("scr", [P, 2, SW + 2])
        prob = sb("prob", [P, 2, SW + 2])
        probT = sb("probT", [P, 2, SW])
        negmax = sb("negmax", [P, H, 2])
        den = sb("den", [P, 2 * H, 2])
        rden = sb("rden", [P, 2 * H, 2])
        gate = sb("gate", [P, NT, 48])
        bstat = sb("bstat", [P, 4, 6])
        mv = sb("mv", [P, NT, 2])
        var = sb("var", [P, NT])
        rstd = sb("rstd", [P, NT])
        mhalf = sb("mhalf", [P, NT])
        ones = sb("ones", [P, P])
        peT = sb("peT", [P, 2, 16])
        pe_rows = sb("pe_rows", [16, 2, P])
        hid = sb("hid", [P, 2, 2, 2 * NCMP])
        hid8 = sb("hid8", [P, 2, 2, 8 * NCMP])
        w2 = sb("w2", [P, 2, 3 * DH])
        kcT = sb("kcT", [P, 2 * NCMP])
        bdmask = sb("bdmask", [8 * NCMP, 8 * DH])
        scm = sb("scm", [P, NT * H])
        lse = sb("lse", [P, 8, NT * H])
        glse = sb("glse", [P, 8, NT * 3])
        fox = sb("fox", [P, 6, NT * 8])

        G = [ctx.enter_context(nc.psum_tensor(f"G{i}", [P, 512], F32)) for i in range(4)]
        S = [ctx.enter_context(nc.psum_tensor(f"S{i}", [P, 512], F32)) for i in range(2)]
        TB = [ctx.enter_context(nc.psum_tensor(f"T{i}", [P, 512], F32)) for i in range(2)]

        def table(name):
            lo, hi = TAB[name]
            return tab[:, lo:hi]

        ident = table("ident")
        cos = table("cos").rearrange("p (t d) -> p t d", t=NT)
        sin = table("sin").rearrange("p (t d) -> p t d", t=NT)
        cos_m = table("cos_m").rearrange("p (t d) -> p t d", t=NT)
        sin_m = table("sin_m").rearrange("p (t d) -> p t d", t=NT)
        cneg = table("cneg").rearrange("p (t n) -> p t n", t=NT)
        cone = table("cone").rearrange("p (t n) -> p t n", t=NT)
        q_gain, kv_gain = small[:, 0:384], small[:, 384:640]
        sinks, forget = small[:, 640:648], small[:, 648:656]
        csil = small[:, 656:656 + KT]
        mod1 = bias8
        a2 = u[:, 0, 2864:2864 + 4 * T].rearrange("p (v g t) -> p v g t", v=2, g=2)
        blkT = u[:, 1, 2864:2864 + 960].rearrange("p (v c g n) -> p v c g n", v=2, c=16, g=2)

        vbd = rotk[0:8 * NCMP, :, 512:1024]
        sc = kT[:, 4:6, :].rearrange("p a t -> p (a t)")[:, 0:NT * H * NCMP].rearrange("p (h n) -> p h n", n=NCMP)
        pcT = kT[0:8 * NCMP, 6:8, :].rearrange("p a t -> p (a t)").rearrange("p (b c) -> p b c", b=4)
        sil, actT = probT[:, :, 0:T], prob[:, :, 0:T]

        landed = [sem(f"slot{i}_landed") for i in range(SLOTS)]
        freed = [sem(f"slot{i}_freed") for i in range(SLOTS)]
        x_loaded, tab_loaded, small_loaded = sem("x_loaded"), sem("tab_loaded"), sem("small_loaded")
        c_loaded, c_ready = sem("c_loaded"), sem("c_ready")
        mod0_loaded, mod1_loaded, swa_loaded, ck_loaded = (sem(n) for n in ("mod0_loaded", "mod1_loaded", "swa_loaded", "ck_loaded"))
        vec_loaded, vec_used = [sem("vec0_loaded"), sem("vec1_loaded")], sem("vec_used")
        consts_set, stored = sem("consts_set"), sem("stored")
        mod1_used, swa_used = sem("mod1_used"), sem("swa_used")
        dve_step, act_step, pool_step = sem("dve_step"), sem("act_step"), sem("pool_step")
        ada = [stage(f"ada{i}", "summed full taken") for i in range(2)]
        norm = stage("norm", "var rstd ready")
        turn = stage("turn", "turned taken")
        out_ready = sem("out_ready")
        proj = {n: stage(n, "full taken") for n in ("nsa_in", "dil_in", "ab_in", "uq", "ukv", "cd_in")}
        outp = stage("outp", "full taken")
        ffn = [stage(f"ffn{i}", "gu_full silu_done act_ready down_full") for i in range(2)]
        att = stage("att", "scores read maxes probs turns turned pv outs")
        nsa_s = stage("nsa", "pos_turned pos_taken cmp_sub cmp_summed kc_ready blocks hidden hidden_act hid8 kv_full kcT_ready vbd scored cmp_exp cmp_prob cmp_turned cmp_taken cmp_out rot_ready gates_exp silu")
        dil_s = stage("dil", "rot_ready lse_in lse_out silu")
        ab_s = stage("ab", "c_ready nope rot_ready")
        cd_s = stage("cd", "f_in f_exp f_ln f_ready cum aug_ready flipped bias_ready")

        first, n_items = {}, 0
        for name, count in (("ada0", ADA_C), ("nsa_ada1", 2 * NSA_C), ("w1", 4), ("nsa_out", OUT_C),
                            ("dil_in", DIL_C), ("dil_out", OUT_C), ("ab_in", AB_C), ("uq", 1), ("ukv", 1),
                            ("ab_out", OUT_C), ("ffn0", FF_STEPS), ("cd_in", CD_C), ("cd_out", OUT_C), ("ffn1", FF_STEPS)):
            first[name] = n_items
            n_items += count

        def slot_of(n, cols):
            return ring[:, n % SLOTS, 0:cols]

        def tiles_of(n, k, w):
            return slot_of(n, k * w).rearrange("p (k w) -> p k w", k=k)

        def wait_landed(eng, n, more=0):
            eng.wait_ge(landed[n % SLOTS], more * 16 + 16 * (n // SLOTS + 1))

        def norm_ready(i):
            return 2 * (i + 1 if i < 3 else i - 1)

        block = ctx.enter_context(nc.Block())

        group_of = {}
        for name, n0 in first.items():
            for n in range(n0, n_items):
                group_of[n] = name

        def used(n):
            name = group_of[n]
            m = n - first[name]
            if name == "ada0":
                return ada[0]["full"], m + 1
            if name == "nsa_ada1":
                return (ada[1]["full"], m // 2 + 1) if m % 2 else (proj["nsa_in"]["full"], m // 2 * 2 + 2)
            if name == "w1":
                return nsa_s["hidden"], m + 1
            if name in proj:
                return proj[name]["full"], 4 if name in ("uq", "ukv") else 2 * m + 2
            if name.endswith("out"):
                return outp["full"], ("nsa_out", "dil_out", "ab_out", "cd_out").index(name) * 2 * OUT_C + 2 * m + 2
            return ffn[int(name[3:])]["down_full"], m + 1

        @block.sync
        def _(sp):
            def fetch(n, src, cols):
                if n >= SLOTS:
                    sp.wait_ge(*used(n - SLOTS))
                sp.dma_start(slot_of(n, cols), src).then_inc(landed[n % SLOTS], 16)

            def group(name, srcs, cols):
                n0, count = first[name], srcs.shape[0]
                rounds = count // SLOTS
                for j in range(min(SLOTS, count)):
                    fetch(n0 + j, srcs[j], cols)
                if rounds == 2:
                    for j in range(SLOTS, 2 * SLOTS):
                        fetch(n0 + j, srcs[j], cols)
                if rounds > 2:
                    per = used(n0 + 1)[1] - used(n0)[1]
                    with sp.Fori(1, rounds) as i:
                        for j in range(SLOTS):
                            done, value = used(n0 + j)
                            sp.wait_ge(done, (i - 1) * (per * SLOTS) + value)
                            sp.dma_start(slot_of(n0 + j, cols), srcs[i * SLOTS + j]).then_inc(landed[(n0 + j) % SLOTS], 16)
                for j in range(max(rounds * SLOTS, SLOTS), count):
                    fetch(n0 + j, srcs[j], cols)

            group("ada0", a["ada_w0"], KT * ADA_W)
            n0 = first["nsa_ada1"]
            for j in range(2):
                fetch(n0 + 2 * j, a["nsa_w_in"][j], KT * NSA_W)
                fetch(n0 + 2 * j + 1, a["ada_w1"][j], KT * ADA_W)
            with sp.Fori(1, NSA_C // 2) as i:
                for j in range(2):
                    sp.wait_ge(proj["nsa_in"]["full"], (i - 1) * 4 + 2 * j + 2)
                    sp.dma_start(slot_of(n0 + 2 * j, KT * NSA_W), a["nsa_w_in"][i * 2 + j]).then_inc(landed[(n0 + 2 * j) % SLOTS], 16)
                    sp.wait_ge(ada[1]["full"], (i - 1) * 2 + j + 1)
                    sp.dma_start(slot_of(n0 + 2 * j + 1, KT * ADA_W), a["ada_w1"][i * 2 + j]).then_inc(landed[(n0 + 2 * j + 1) % SLOTS], 16)
            group("w1", a["cmp_w1"], 2048)
            group("nsa_out", a["nsa_w_out"], KT * OUT_W)
            group("dil_in", a["dil_w_in"], KT * DIL_W)
            group("dil_out", a["dil_w_out"], KT * OUT_W)
            group("ab_in", a["ab_w_in"], KT * AB_W)
            group("uq", a["ab_w_uq"], 3 * 768)
            group("ukv", a["ab_w_ukv"], 2 * 1024)
            group("ab_out", a["ab_w_out"], KT * OUT_W)
            group("ffn0", a["ffn0"], 3072)
            group("cd_in", a["cd_w_in"], KT * CD_W)
            group("cd_out", a["cd_w_out"], KT * OUT_W)
            group("ffn1", a["ffn1"], 3072)
            sp.wait_ge(norm["ready"], norm_ready(8))
            sp.dma_start(out.rearrange("b (t p) d -> p (b t) d", p=P), x[:]).then_inc(stored, 16)
            sp.wait_ge(stored, 16)

        @block.gpsimd
        def _(pool):
            pool.memset(mhalf[:], -0.5).then_inc(consts_set, 1)
            pool.memset(ones[:], 1.0).then_inc(consts_set, 1)
            pool.wait_ge(consts_set, 2)

            def load_vec(v):
                if v >= 2:
                    pool.wait_ge(vec_used, v - 1)
                pool.dma_start(vec[:, v % 2, :], a["vecs"][v:v + 1, :].rearrange("a d -> (a d)").partition_broadcast(P)).then_inc(vec_loaded[v % 2], 16)

            def rstd_of(i):
                pool.wait_ge(norm["var"], i + 1)
                pool.tensor_tensor(rstd[:], var[:], mhalf[:], ALU.pow).then_inc(norm["rstd"], 1)

            load_vec(0)
            load_vec(1)
            rstd_of(0)
            load_vec(2)
            rstd_of(1)
            rstd_of(2)
            load_vec(3)
            load_vec(4)
            pool.wait_ge(mod1_used, 1)
            pool.dma_start(bias8[:], a["swa_bias"]).then_inc(swa_loaded, 16)
            rstd_of(3)
            rstd_of(4)
            rstd_of(5)
            load_vec(5)
            load_vec(6)
            pool.wait_ge(swa_used, 1)
            b8 = bias8[:].rearrange("p (h w) -> p h w", h=8)
            rev = a["rel_rev"]
            for lo, base in ((0, P), (P, 0), (2 * P, P)):
                pool.dma_start(b8[:, :, lo:lo + P], bass.AP(tensor=rev.tensor, offset=base, ap=[[1, P], [rev.shape[1], 8], [1, P]])).then_inc(ck_loaded, 16)
            rstd_of(6)
            load_vec(7)
            load_vec(8)
            rstd_of(7)
            load_vec(9)
            load_vec(10)
            rstd_of(8)

        turns = {}
        turn_n = [0, 0]

        def plan_turn(name, groups):
            turns[name] = (groups, *turn_n)
            turn_n[0] += len(groups)
            turn_n[1] += sum(len(takes) for _, takes in groups)

        def turned_all(name):
            groups, _, t0 = turns[name]
            return t0 + sum(len(takes) for _, takes in groups)

        def turn_pe(pe, name):
            groups, _, t0 = turns[name]
            for g, (srcs, takes) in enumerate(groups):
                if g >= 2:
                    pe.wait_ge(turn["taken"], t0 + (g - 1) * len(takes))
                for n, (src, width) in enumerate(srcs):
                    ins = pe.transpose(TB[g % 2][0:width, n * P:(n + 1) * P], src, ident)
                ins.then_inc(turn["turned"], 1)

        def turn_act(act, name):
            groups, g0, _ = turns[name]
            for g, (srcs, takes) in enumerate(groups):
                act.wait_ge(turn["turned"], g0 + g + 1)
                for rows, cols, dst, split in takes:
                    src = TB[g % 2][rows[0]:rows[1], cols[0]:cols[1]]
                    if split:
                        src = src.rearrange("p (n c) -> p n c", n=split)
                        src = src[:, :, src.shape[2] - dst.shape[2]:]
                    act.copy(dst, src).then_inc(turn["taken"], 1)

        def rows_to(dst, src, per=4, width=P, t_n=NT):
            groups = []
            for t in range(t_n):
                n_all = src[t].shape[1]
                for n in range(0, n_all, per):
                    m = min(per, n_all - n)
                    groups.append(([(src[t][:, n + j, :], width) for j in range(m)],
                                   [((0, width), (0, m * P), dst[0:width, n:n + m, t * P:(t + 1) * P], m)]))
            return groups

        def blocks_of(ap2, w=P):
            return [ap2[:, t, :].rearrange("p (n w) -> p n w", w=w) for t in range(NT)]

        turn_full = rows_to(hT, blocks_of(tok))
        turn_resid = rows_to(hT, blocks_of(x))

        def att_pe(pe, name):
            st, jobs, b0 = att, att_jobs[name], att_base[name]
            n = len(jobs)
            for i in range(n + 2):
                if i < n:
                    q, k, v, _ = jobs[i]
                    if i >= 2:
                        pe.wait_ge(st["read"], b0 + i - 1)
                    pe.matmul(S[i % 2][:, 0:P], q[:, 0:P], k[:, 0:P], start=True, stop=True)
                    pe.matmul(S[i % 2][:, P:SW], q[:, P:T], k[:, 0:T], start=True, stop=True).then_inc(st["scores"], 1)
                if 1 <= i <= n:
                    j = i - 1
                    pe.wait_ge(st["probs"], 2 * b0 + 2 * j + 2)
                    if j >= 2:
                        pe.wait_ge(st["turned"], b0 + j - 1)
                    for b in range(3):
                        ins = pe.transpose(TB[j % 2][:, b * P:(b + 1) * P], prob[:, j % 2, 1 + b * P:1 + (b + 1) * P], ident)
                    ins.then_inc(st["turns"], 1)
                if i >= 2:
                    j = i - 2
                    v = jobs[j][2]
                    pe.wait_ge(st["turned"], b0 + j + 1)
                    if j >= 4:
                        pe.wait_ge(st["outs"], b0 + j - 3)
                    o = G[j % 4]
                    pt = probT[:, j % 2, :]
                    pe.matmul(o[:, 0:DH], pt[:, 0:P], v[0], start=True, stop=True)
                    pe.matmul(o[:, DH:2 * DH], pt[:, P:2 * P], v[0], start=True, stop=False)
                    pe.matmul(o[:, DH:2 * DH], pt[:, 2 * P:SW], v[1], start=False, stop=True).then_inc(st["pv"], 1)

        def att_dve(dve, tl, name, bias_of, scale, take, sink=None):
            st, n, b0 = att, len(att_jobs[name]), att_base[name]
            for i in range(n + 3):
                if i < n:
                    dve.wait_ge(st["scores"], b0 + i + 1)
                    if i >= 2:
                        dve.wait_ge(st["probs"], 2 * b0 + 2 * i - 2)
                    s = scr[:, i % 2, :]
                    if sink is not None:
                        tl.done(dve.tensor_copy(s[:, 0:SW + 2:SW + 1], sink(i)))
                    tl.done(dve.scalar_tensor_tensor(s[:, 1:1 + SW], S[i % 2][:, 0:SW], scale, bias_of(i), ALU.mult, ALU.add), st["read"])
                    lo, hi = (0, SW + 2) if sink is not None else (1, SW + 1)
                    h = i % H
                    if i >= H:
                        dve.wait_ge(st["probs"], 2 * b0 + 2 * (i - H) + 2)
                    tl.mark(dve.tensor_reduce(negmax[:, h, 0:1], s[:, lo:1 + P], AX.X, ALU.max, negate=True), st["maxes"])
                    tl.mark(dve.tensor_reduce(negmax[:, h, 1:2], s[:, 1 + P:hi], AX.X, ALU.max, negate=True), st["maxes"])
                if i >= 3:
                    j = i - 3
                    dve.wait_ge(st["pv"], b0 + j + 1)
                    tl.done(dve.reciprocal(rden[:, j, :], den[:, j, :]))
                    take(j, G[j % 4][:, 0:2 * DH].rearrange("p (t d) -> p t d", t=NT), rden[:, j, :])

        def att_act(act, name, sink=False):
            st, n, b0 = att, len(att_jobs[name]), att_base[name]
            lo, hi = (0, SW + 2) if sink else (1, SW + 1)
            for i in range(n + 1):
                if i < n:
                    act.wait_ge(st["maxes"], 2 * b0 + 2 * i + 2)
                    if i >= 2:
                        act.wait_ge(st["turns"], b0 + i - 1)
                    h = i % H
                    act.activation(prob[:, i % 2, lo:1 + P], scr[:, i % 2, lo:1 + P], ACT.Exp, bias=negmax[:, h, 0:1],
                                   accum_out=den[:, i, 0:1]).then_inc(st["probs"], 1)
                    act.activation(prob[:, i % 2, 1 + P:hi], scr[:, i % 2, 1 + P:hi], ACT.Exp, bias=negmax[:, h, 1:2],
                                   accum_out=den[:, i, 1:2]).then_inc(st["probs"], 1)
                if i >= 1:
                    j = i - 1
                    act.wait_ge(st["turns"], b0 + j + 1)
                    if j >= 2:
                        act.wait_ge(st["pv"], b0 + j - 1)
                    act.copy(probT[:, j % 2, :], TB[j % 2][:, 0:SW]).then_inc(st["turned"], 1)

        def pair(tile, h):
            return tile[(h % 2) * DH:(h % 2) * DH + DH, h // 2, :]

        def v_of(lo):
            return [u[:, t, lo:lo + DH] for t in range(NT)]

        def twin(tile, h, g):
            return tile[(h % 2) * DH:(h % 2) * DH + DH, g, :]

        nsa_jobs = [(pair(qT, h), twin(kT, h, br * 2 + h // 8), v_of(1408 + 256 * br + DH * (h // 8)), None)
                    for br in range(2) for h in range(H)]
        dil_jobs = [(pair(qT, h), pair(kT, h), v_of(2 * D + DH * h), None) for h in range(H)]
        mla_jobs = [(qT[0:96, h, :], kT[0:96, h, :], v_of(2560 + P * h + DH), None) for h in range(8)]
        swa_jobs = [(pair(q2T, h), twin(q2T, h, 4 + h // 4), v_of(1312 + DH * (h // 4)), None) for h in range(8)]
        fox_jobs = [(qT[0:FOXW, h, :], kT[0:FOXW, h, :], v_of(1024 + DH * h), None) for h in range(8)]
        ck_jobs = [(pair(q2T, h), twin(q2T, h, 4 + h // 2), v_of(2568 + DH * h), None) for h in range(8)]

        att_jobs = {"nsa": nsa_jobs, "dil": dil_jobs, "mla": mla_jobs, "swa": swa_jobs, "fox": fox_jobs, "ck": ck_jobs}
        att_base, heads_n = {}, 0
        for name, jobs in att_jobs.items():
            att_base[name] = heads_n
            heads_n += len(jobs)

        nsa_plain = rows_to(q2T, blocks_of(u[:, :, 0:D]))
        kdup = rotk[:, :, 0:512]
        kcdup = rotk[:, :, 512:1024]
        nsa_rot = rows_to(qT, blocks_of(tok)) + rows_to(kT, blocks_of(kdup))
        a2f = a2.rearrange("p v g t -> p (v g) t")
        nsa_kc = [([(kcdup[:, t, n * P:(n + 1) * P], P) for n in range(4)],
                   [((0, DH), (0, 4 * P), a2f[0:DH, :, t * P:(t + 1) * P], 4),
                    ((DH, P), (0, 4 * P), a2f[DH:P, :, max(t * P - 1, 0):(t + 1) * P - 1], 4)]) for t in range(NT)]
        dil_rot = rows_to(qT, blocks_of(tok)) + rows_to(kT, blocks_of(rotk))
        ab_c = rows_to(hT, blocks_of(tok[:, :, 0:640]))
        qcat = tok[:, :, 0:768]
        kcat = rotk[:, :, 0:768]
        kswa = tok[:, :, 768:1024]
        ab_rot = (rows_to(qT, blocks_of(qcat, 96), width=96) + rows_to(kT, blocks_of(kcat, 96), width=96)
                  + rows_to(q2T, blocks_of(u[:, :, 672:1184])) + rows_to(q2T[:, 4:6, :], blocks_of(kswa)))
        qaug = tok[:, :, 0:8 * FOXW]
        kaug = rotk[:, :, 0:8 * FOXW]
        cd_rot = (rows_to(qT, blocks_of(qaug, FOXW), width=FOXW) + rows_to(kT, blocks_of(kaug, FOXW), width=FOXW)
                  + rows_to(q2T, blocks_of(u[:, :, 1544:2056])) + rows_to(q2T[:, 4:8, :], blocks_of(u[:, :, 2056:2568])))

        for name, groups in (("h0", turn_full), ("nsa_plain", nsa_plain), ("nsa_kc", nsa_kc), ("nsa_rot", nsa_rot), ("o0", turn_full),
                             ("h1", turn_full), ("dil_rot", dil_rot), ("o1", turn_full), ("x0", turn_resid), ("ab_c", ab_c),
                             ("ab_rot", ab_rot), ("o2", turn_full), ("f0", turn_resid), ("x1", turn_resid), ("cd_rot", cd_rot),
                             ("o3", turn_full), ("f1", turn_resid)):
            plan_turn(name, groups)

        @block.tensor
        def _(pe):
            def ada_chunk(layer, j, m):
                pe.wait_ge(ada[layer]["summed"], m + 1)
                pe.matmul(S[j % 2][:, 0:ADA_W], ones[:], acc[:, j % 2, :], start=True, stop=True).then_inc(ada[layer]["full"], 1)

            def gemm_chunk(st, n, more, j, m, w, k_n=KT):
                wait_landed(pe, n, more)
                wt = tiles_of(n, k_n, w)
                for t in range(NT):
                    for k in range(k_n):
                        ins = pe.matmul(G[(j % 2) * 2 + t][:, 0:w], hT[:, k, t * P:(t + 1) * P], wt[:, k, :],
                                        start=(k == 0), stop=(k == k_n - 1))
                    ins.then_inc(st["full"], 1)

            def gemm(name, st, count, w, before=0):
                n0 = first[name]
                for j in range(SLOTS):
                    if j >= 2:
                        pe.wait_ge(st["taken"], before + 2 * (j - 1))
                    gemm_chunk(st, n0 + j, 0, j, j, w)
                if count > SLOTS:
                    with pe.Fori(1, count // SLOTS) as i:
                        for j in range(SLOTS):
                            pe.wait_ge(st["taken"], i * (2 * SLOTS) + 2 * (j - 1))
                            gemm_chunk(st, n0 + j, i, j, i * SLOTS + j, w)

            def wide(name, st, k0, k_n, w):
                wait_landed(pe, first[name])
                wt = tiles_of(first[name], k_n, 2 * w)
                for t in range(NT):
                    for half in range(2):
                        for k in range(k_n):
                            ins = pe.matmul(G[2 * t + half][:, 0:w], hT[:, k0 + k, t * P:(t + 1) * P],
                                            wt[:, k, half * w:(half + 1) * w], start=(k == 0), stop=(k == k_n - 1))
                        ins.then_inc(st["full"], 1)

            def ffn_pe(name, st):
                n0 = first[name]

                def gate_up(b, s, n, more):
                    wait_landed(pe, n, more)
                    w = slot_of(n, 3072)
                    for part in range(2):
                        for k in range(KT):
                            at = (part * KT + k) * P
                            ins = pe.matmul(S[b][:, part * T:(part + 1) * T], w[:, at:at + P], hT[:, k, :],
                                            start=(k == 0), stop=(k == KT - 1))
                    ins.then_inc(st["gu_full"], 1)

                def down(b, s, n, start, stop):
                    pe.wait_ge(st["act_ready"], s + 1)
                    w = slot_of(n, 3072)
                    for t in range(NT):
                        for half in range(2):
                            at = 2 * KT * P + half * 512
                            ins = pe.matmul(G[2 * t + half][:], actT[:, b, t * P:(t + 1) * P], w[:, at:at + 512],
                                            start=start, stop=stop)
                    ins.then_inc(st["down_full"], 1)

                gate_up(0, 0, n0, 0)
                gate_up(1, 1, n0 + 1, 0)
                down(0, 0, n0, True, False)
                with pe.Fori(0, (FF_STEPS - 2) // SLOTS) as i:
                    for j in range(SLOTS):
                        s = i * SLOTS + (1 + j)
                        pe.wait_ge(st["act_ready"], s)
                        gate_up(j % 2, s + 1, n0 + 2 + j, i)
                        down((1 + j) % 2, s, n0 + 1 + j, False, False)
                down((FF_STEPS - 1) % 2, FF_STEPS - 1, n0 + FF_STEPS - 1, False, True)

            pe.wait_ge(consts_set, 2)
            pe.wait_ge(tab_loaded, 16)
            for j in range(ADA_C):
                if j >= 2:
                    pe.wait_ge(ada[0]["taken"], j - 1)
                ada_chunk(0, j, j)

            pe.wait_ge(norm["ready"], norm_ready(0))
            turn_pe(pe, "h0")
            pe.wait_ge(turn["taken"], turned_all("h0"))
            pe.wait_ge(ada[0]["taken"], ADA_C)
            n0, st = first["nsa_ada1"], proj["nsa_in"]
            for j in range(2):
                gemm_chunk(st, n0 + 2 * j, 0, j, j, NSA_W)
                ada_chunk(1, j, j)
            with pe.Fori(1, NSA_C // 2) as i:
                for j in range(2):
                    pe.wait_ge(st["taken"], i * 4 + 2 * (j - 1))
                    gemm_chunk(st, n0 + 2 * j, i, j, i * 2 + j, NSA_W)
                    pe.wait_ge(ada[1]["taken"], i * 2 + j - 1)
                    ada_chunk(1, j, i * 2 + j)

            pe.wait_ge(st["taken"], 2 * NSA_C)
            turn_pe(pe, "nsa_plain")
            pe.wait_ge(turn["taken"], turned_all("nsa_plain"))
            pe.wait_ge(small_loaded, 16 * SMALL_LOADS)
            for v in range(2):
                ins = pe.transpose(TB[0][:, v * 16:(v + 1) * 16], pe_rows[:, v, :], ident[0:16, 0:16])
            ins.then_inc(nsa_s["pos_turned"], 1)
            pe.wait_ge(nsa_s["kc_ready"], 1)
            pe.wait_ge(nsa_s["pos_taken"], 1)
            turn_pe(pe, "nsa_kc")
            pe.wait_ge(nsa_s["blocks"], 8)
            for v in range(2):
                for kh in range(2):
                    n = first["w1"] + 2 * v + kh
                    wait_landed(pe, n)
                    w1 = tiles_of(n, 8, 256)
                    for mh in range(2):
                        for c in range(8):
                            ins = pe.matmul(G[2 * v + mh][:, 0:2 * NCMP], w1[:, c, mh * P:(mh + 1) * P],
                                            blkT[:, v, kh * 8 + c, :, :], start=(kh == 0 and c == 0), stop=(kh == 1 and c == 7))
                    ins.then_inc(nsa_s["hidden"], 1)
            pe.wait_ge(nsa_s["rot_ready"], 1)
            turn_pe(pe, "nsa_rot")
            pe.wait_ge(nsa_s["hidden_act"], 4)
            pe.wait_ge(ada[1]["taken"], ADA_C)
            for mh in range(2):
                ins = pe.matmul(S[0][:, 0:2 * NCMP], w2[:, mh, 0:P], hid[:, 0, mh, :], start=(mh == 0), stop=(mh == 1))
            ins.then_inc(nsa_s["kv_full"], 1)
            pe.wait_ge(nsa_s["hid8"], 4)
            for g in range(2):
                for mh in range(2):
                    ins = pe.matmul(S[1][0:8 * NCMP, g * DH:(g + 1) * DH], hid8[:, g, mh, :], w2[:, mh, P:3 * DH],
                                    start=(mh == 0), stop=(mh == 1))
            ins.then_inc(nsa_s["kv_full"], 1)
            pe.wait_ge(nsa_s["kcT_ready"], 1)
            for t in range(NT):
                for h in range(H):
                    lo = (h % 2) * DH
                    at = (t * 8 + h // 2) * NCMP
                    ins = pe.matmul(G[h % 2][:, at:at + NCMP], q2T[lo:lo + DH, h // 2, t * P:(t + 1) * P],
                                    kcT[lo:lo + DH, (h // 8) * NCMP:(h // 8 + 1) * NCMP], start=True, stop=True)
            ins.then_inc(nsa_s["scored"], 1)
            pe.wait_ge(turn["taken"], turned_all("nsa_rot"))
            pe.wait_ge(nsa_s["cmp_prob"], 1)
            for b in range(4):
                ins = pe.transpose(TB[0][0:8 * NCMP, b * P:(b + 1) * P], sc[:, b * 8:(b + 1) * 8, :], ident)
            ins.then_inc(nsa_s["cmp_turned"], 1)
            pe.wait_ge(nsa_s["cmp_taken"], 1)
            pe.wait_ge(nsa_s["vbd"], 2)
            for b in range(4):
                pe.matmul(G[b][:], pcT[:, b, :], vbd[:, b % 2, :], start=True, stop=True).then_inc(nsa_s["cmp_out"], 1)
            pe.wait_ge(nsa_s["cmp_summed"], 4)
            att_pe(pe, "nsa")

            def project_out(i, name):
                pe.wait_ge(out_ready, i + 1)
                turn_pe(pe, f"o{i}")
                pe.wait_ge(turn["taken"], turned_all(f"o{i}"))
                gemm(name, outp, OUT_C, OUT_W, i * 2 * OUT_C)

            project_out(0, "nsa_out")

            pe.wait_ge(norm["ready"], norm_ready(1))
            turn_pe(pe, "h1")
            pe.wait_ge(turn["taken"], turned_all("h1"))
            gemm("dil_in", proj["dil_in"], DIL_C, DIL_W)
            pe.wait_ge(dil_s["rot_ready"], 1)
            pe.wait_ge(proj["dil_in"]["taken"], 2 * DIL_C)
            turn_pe(pe, "dil_rot")
            pe.wait_ge(turn["taken"], turned_all("dil_rot"))
            att_pe(pe, "dil")
            project_out(1, "dil_out")

            pe.wait_ge(norm["ready"], norm_ready(2))
            turn_pe(pe, "x0")
            pe.wait_ge(turn["taken"], turned_all("x0"))
            gemm("ab_in", proj["ab_in"], AB_C, AB_W)
            pe.wait_ge(ab_s["c_ready"], 1)
            turn_pe(pe, "ab_c")
            pe.wait_ge(turn["taken"], turned_all("ab_c"))
            pe.wait_ge(proj["ab_in"]["taken"], 2 * AB_C)
            wide("uq", proj["uq"], 0, 3, 384)
            pe.wait_ge(proj["uq"]["taken"], 4)
            wide("ukv", proj["ukv"], 3, 2, 512)
            pe.wait_ge(ab_s["rot_ready"], 1)
            pe.wait_ge(ab_s["nope"], 4)
            pe.wait_ge(proj["ukv"]["taken"], 4)
            turn_pe(pe, "ab_rot")
            pe.wait_ge(turn["taken"], turned_all("ab_rot"))
            att_pe(pe, "mla")
            pe.wait_ge(att["outs"], att_base["mla"] + 8)
            att_pe(pe, "swa")
            project_out(2, "ab_out")

            pe.wait_ge(norm["ready"], norm_ready(5))
            turn_pe(pe, "f0")
            pe.wait_ge(turn["taken"], turned_all("f0"))
            ffn_pe("ffn0", ffn[0])

            pe.wait_ge(norm["ready"], norm_ready(6))
            turn_pe(pe, "x1")
            pe.wait_ge(turn["taken"], turned_all("x1"))
            gemm("cd_in", proj["cd_in"], CD_C, CD_W)
            pe.wait_ge(proj["cd_in"]["taken"], 2 * CD_C)
            pe.wait_ge(ck_loaded, 48)
            for h in range(8):
                if h >= 4:
                    pe.wait_ge(cd_s["bias_ready"], h - 3)
                pe.matmul(G[h % 4][:, 0:SW], table("flip"), bias8[:, h * SW:(h + 1) * SW], start=True, stop=True).then_inc(cd_s["flipped"], 1)
            pe.wait_ge(cd_s["f_ready"], 1)
            f = fox[:, 3, :]
            pe.matmul(S[0][:, 0:8], table("tri"), f[:, 0:8], start=True, stop=True)
            pe.matmul(S[0][:, 8:16], table("tri"), f[:, 8:16], start=True, stop=False)
            pe.matmul(S[0][:, 8:16], ones[:], f[:, 0:8], start=False, stop=True).then_inc(cd_s["cum"], 1)
            pe.wait_ge(cd_s["aug_ready"], 1)
            pe.wait_ge(proj["cd_in"]["taken"], 2 * CD_C)
            turn_pe(pe, "cd_rot")
            pe.wait_ge(turn["taken"], turned_all("cd_rot"))
            att_pe(pe, "fox")
            pe.wait_ge(att["outs"], att_base["fox"] + 8)
            att_pe(pe, "ck")
            project_out(3, "cd_out")

            pe.wait_ge(norm["ready"], norm_ready(7))
            turn_pe(pe, "f1")
            pe.wait_ge(turn["taken"], turned_all("f1"))
            ffn_pe("ffn1", ffn[1])

        @block.scalar
        def _(act):
            tl = Tally(act, act_step)
            act.dma_start(csil, a["c"]).then_inc(c_loaded, 16)
            act.dma_start(mod0[:], a["ada_b"][0:1, :].rearrange("a d -> (a d)").partition_broadcast(P)).then_inc(mod0_loaded, 16)
            act.dma_start(x[:], a["x"].rearrange("b (t p) d -> p (b t) d", p=P)).then_inc(x_loaded, 16)
            act.dma_start(tab[:], a["tables"]).then_inc(tab_loaded, 16)
            act.dma_start(mod1[:], a["ada_b"][1:2, :].rearrange("a d -> (a d)").partition_broadcast(P)).then_inc(mod1_loaded, 16)
            for dst, src in ((q_gain, a["q_norm"]), (kv_gain, a["kv_norm"]), (sinks, a["sinks"]), (forget, a["b_forget"])):
                act.dma_start(dst, src.partition_broadcast(P)).then_inc(small_loaded, 16)
            act.dma_start(bdmask[:], a["bdmask"]).then_inc(small_loaded, 16)
            act.dma_start(pe_rows[:], a["pos"]).then_inc(small_loaded, 16)
            act.dma_start(w2[:, :, 0:DH], a["cmp_w2"][:, 0]).then_inc(small_loaded, 16)
            act.dma_start(w2[:, :, DH:P], a["cmp_w2"][:, 0]).then_inc(small_loaded, 16)
            act.dma_start(w2[:, :, P:3 * DH], a["cmp_w2"][:, 1]).then_inc(small_loaded, 16)
            act.wait_ge(c_loaded, 16)
            tl.done(act.activation(csil, csil, ACT.Silu), c_ready)

            def take_chunk(st, j, m, w, t):
                act.wait_ge(st["full"], 2 * m + (t + 1))
                at = m * w
                dst = u[:, t, at:at + w] if isinstance(at, int) else u[:, t, bass.ds(at, w)]
                act.copy(dst, G[(j % 2) * 2 + t][:, 0:w]).then_inc(st["taken"], 1)

            def take_all(st, count, w):
                for j in range(SLOTS):
                    for t in range(NT):
                        take_chunk(st, j, j, w, t)
                if count > SLOTS:
                    with act.Fori(1, count // SLOTS) as i:
                        for j in range(SLOTS):
                            for t in range(NT):
                                take_chunk(st, j, i * SLOTS + j, w, t)

            def take_wide(st, at, w):
                for t in range(NT):
                    for half in range(2):
                        act.wait_ge(st["full"], 2 * t + half + 1)
                        act.copy(u[:, t, at + half * w:at + (half + 1) * w], G[2 * t + half][:, 0:w]).then_inc(st["taken"], 1)

            def ffn_act(st):
                def step(b, s):
                    act.wait_ge(st["gu_full"], s + 1)
                    act.activation(sil[:, b, :], S[b][:, 0:T], ACT.Silu).then_inc(st["silu_done"], 1)

                step(0, 0)
                step(1, 1)
                with act.Fori(1, FF_STEPS // 2) as i:
                    for b in range(2):
                        act.wait_ge(st["act_ready"], i * 2 + (b - 1))
                        step(b, i * 2 + b)

            turn_act(act, "h0")
            take_all(proj["nsa_in"], NSA_C, NSA_W)
            act.wait_ge(proj["nsa_in"]["taken"], 2 * NSA_C)
            act.activation(gate[:], u[:, :, 2816:2864], ACT.Exp, scale=-1.0).then_inc(nsa_s["gates_exp"], 1)
            act.activation(u[:, :, 1792:2816], u[:, :, 1792:2816], ACT.Silu).then_inc(nsa_s["silu"], 1)
            turn_act(act, "nsa_plain")
            act.wait_ge(nsa_s["pos_turned"], 1)
            act.copy(peT[:], TB[0][:, 0:32].rearrange("p (v c) -> p v c", v=2)).then_inc(nsa_s["pos_taken"], 1)
            turn_act(act, "nsa_kc")
            act.wait_ge(nsa_s["hidden"], 4)
            for v in range(2):
                for mh in range(2):
                    act.activation(hid[:, v, mh, :], G[2 * v + mh][:, 0:2 * NCMP], ACT.Silu).then_inc(nsa_s["hidden_act"], 1)
            turn_act(act, "nsa_rot")
            act.wait_ge(nsa_s["cmp_sub"], 1)
            act.activation(sc[:], sc[:], ACT.Exp).then_inc(nsa_s["cmp_exp"], 1)
            act.wait_ge(nsa_s["cmp_turned"], 1)
            act.copy(pcT[:], TB[0][0:8 * NCMP, :].rearrange("p (b c) -> p b c", b=4)).then_inc(nsa_s["cmp_taken"], 1)
            att_act(act, "nsa")
            turn_act(act, "o0")

            turn_act(act, "h1")
            take_all(proj["dil_in"], DIL_C, DIL_W)
            act.wait_ge(proj["dil_in"]["taken"], 2 * DIL_C)
            act.activation(u[:, :, 3 * D:4 * D], u[:, :, 3 * D:4 * D], ACT.Silu).then_inc(dil_s["silu"], 1)
            turn_act(act, "dil_rot")
            att_act(act, "dil")
            for k, (src, func) in enumerate(((0, ACT.Ln), (3, ACT.Exp), (4, ACT.Ln), (5, ACT.Exp))):
                act.wait_ge(dil_s["lse_in"], k + 1)
                v = {0: lse[:, 0, :], 3: lse[:, 3, :], 4: glse[:, 4, 0:6], 5: glse[:, 5, 0:6]}[src]
                act.activation(v, v, func).then_inc(dil_s["lse_out"], 1)
            turn_act(act, "o1")

            turn_act(act, "x0")
            take_all(proj["ab_in"], AB_C, AB_W)
            turn_act(act, "ab_c")
            take_wide(proj["uq"], 1536, 384)
            take_wide(proj["ukv"], 2560, 512)
            act.wait_ge(proj["ukv"]["taken"], 4)
            for t in range(NT):
                act.copy(qcat[:, t, :].rearrange("p (h d) -> p h d", h=8)[:, :, 0:DH],
                         u[:, t, 1536:2304].rearrange("p (h d) -> p h d", h=8)[:, :, 0:DH]).then_inc(ab_s["nope"], 1)
                act.copy(kcat[:, t, :].rearrange("p (h d) -> p h d", h=8)[:, :, 0:DH],
                         u[:, t, 2560:3584].rearrange("p (h d) -> p h d", h=8)[:, :, 0:DH]).then_inc(ab_s["nope"], 1)
            turn_act(act, "ab_rot")
            att_act(act, "mla")
            act.wait_ge(att["outs"], att_base["mla"] + 8)
            att_act(act, "swa", sink=True)
            turn_act(act, "o2")
            turn_act(act, "f0")
            ffn_act(ffn[0])

            turn_act(act, "x1")
            take_all(proj["cd_in"], CD_C, CD_W)
            act.wait_ge(cd_s["f_in"], 1)
            act.activation(fox[:, 1, :], fox[:, 1, :], ACT.Exp, scale=-1.0).then_inc(cd_s["f_exp"], 1)
            act.wait_ge(cd_s["f_exp"], 1)
            act.activation(fox[:, 1, :], fox[:, 1, :], ACT.Ln, bias=1.0).then_inc(cd_s["f_ln"], 1)
            turn_act(act, "cd_rot")
            att_act(act, "fox")
            act.wait_ge(att["outs"], att_base["fox"] + 8)
            att_act(act, "ck")
            turn_act(act, "o3")
            turn_act(act, "f1")
            ffn_act(ffn[1])

        @block.vector
        def _(dve):
            tl = Tally(dve, dve_step)
            done = tl.done
            TT, STT, TS = dve.tensor_tensor, dve.scalar_tensor_tensor, dve.tensor_scalar

            def ada_sum(layer, n, more, j, m, mod):
                wait_landed(dve, n, more)
                w = tiles_of(n, KT, ADA_W)
                done(TS(acc[:, j % 2, :], w[:, 0, :], csil[:, 0:1], None, ALU.mult))
                for k in range(1, KT):
                    done(STT(acc[:, j % 2, :], w[:, k, :], csil[:, k:k + 1], acc[:, j % 2, :], ALU.mult, ALU.add),
                         ada[layer]["summed"] if k == KT - 1 else None)
                dve.wait_ge(ada[layer]["full"], m + 1)
                at = m * ADA_W
                dst = mod[:, at:at + ADA_W] if isinstance(at, int) else mod[:, bass.ds(at, ADA_W)]
                done(TT(dst, dst, S[j % 2][:, 0:ADA_W], ALU.add), ada[layer]["taken"])

            def stats(src, layer_norm, eps):
                w = src[0].shape[1]
                pieces = -(-w // 512)
                for t in range(NT):
                    for c in range(pieces):
                        done(dve.bn_stats(bstat[:, c, :], src[t][:, c * w // pieces:(c + 1) * w // pieces]))
                    done(dve.bn_aggr(mv[:, t, :], bstat[:, 0:pieces, :]))
                if layer_norm:
                    done(TS(var[:], mv[:, :, 1], eps, None, ALU.add), norm["var"])
                else:
                    done(TT(var[:], mv[:, :, 0], mv[:, :, 0], ALU.mult))
                    done(TT(var[:], var[:], mv[:, :, 1], ALU.add))
                    done(TS(var[:], var[:], eps, None, ALU.add), norm["var"])

            vec_n = [0]

            def next_vec():
                v = vec_n[0]
                vec_n[0] += 1
                dve.wait_ge(vec_loaded[v % 2], 16 * (v // 2 + 1))
                return vec[:, v % 2, :]

            def ada_norm(i, mod):
                shift, scale = mod[:, 0:D], mod[:, D:2 * D]
                g = next_vec()
                done(STT(scale, scale, 1.0, g, ALU.add, ALU.mult), vec_used)
                stats([x[:, t, :] for t in range(NT)], False, EPS_RMS)
                dve.wait_ge(norm["rstd"], i + 1)
                for t in range(NT):
                    done(STT(tok[:, t, :], x[:, t, :], rstd[:, t:t + 1], scale, ALU.mult, ALU.mult))
                    done(TT(tok[:, t, :], tok[:, t, :], shift, ALU.add), norm["ready"])

            def layer_norm(i):
                g = next_vec()
                b = next_vec()
                stats([x[:, t, :] for t in range(NT)], True, EPS_LN)
                dve.wait_ge(norm["rstd"], i + 1)
                for t in range(NT):
                    done(TS(x[:, t, :], x[:, t, :], mv[:, t, 0:1], rstd[:, t:t + 1], ALU.subtract, ALU.mult))
                for t in range(NT):
                    done(TT(x[:, t, :], x[:, t, :], g, ALU.mult), vec_used if t == 1 else None)
                for t in range(NT):
                    ins = TT(x[:, t, :], x[:, t, :], b, ALU.add)
                    done(ins, norm["ready"])
                done(TS(var[:, 0:1], var[:, 0:1], 1.0, None, ALU.mult), vec_used)

            def rotate(dst, src, c, s, n, half, t):
                x1, x2 = src[:, :, 0:half], src[:, :, half:2 * half]
                cb, sb_ = over(c[:, t, :], 1, n), over(s[:, t, :], 1, n)
                ta = tmp[:, 0, 0:n * half].rearrange("p (n d) -> p n d", n=n)
                tb = tmp[:, 1, 0:n * half].rearrange("p (n d) -> p n d", n=n)
                done(TT(ta, x1, cb, ALU.mult))
                done(TT(tb, x2, sb_, ALU.mult))
                done(TT(dst[:, :, 0:half], ta, tb, ALU.subtract))
                done(TT(ta, x2, cb, ALU.mult))
                done(TT(tb, x1, sb_, ALU.mult))
                done(TT(dst[:, :, half:2 * half], ta, tb, ALU.add))

            def set_head(col):
                def take(st, j, o, r):
                    done(TT(tok[:, :, (col + j) * DH:(col + j + 1) * DH], o, over(r, 2, DH), ALU.mult), st["outs"])
                return take

            def residual_gated(i, gatev):
                st = outp
                for m in range(OUT_C):
                    for t in range(NT):
                        dve.wait_ge(st["full"], 2 * OUT_C * i + 2 * m + t + 1)
                        cols = slice(m * OUT_W, (m + 1) * OUT_W)
                        done(TT(tmp[:, t, 0:OUT_W], G[(m % 2) * 2 + t][:, 0:OUT_W], gatev[:, cols], ALU.mult), st["taken"])
                        done(TT(x[:, t, cols], x[:, t, cols], tmp[:, t, 0:OUT_W], ALU.add))

            def residual_deep(i):
                st = outp
                for m in range(OUT_C):
                    for t in range(NT):
                        dve.wait_ge(st["full"], 2 * OUT_C * i + 2 * m + t + 1)
                        cols = slice(m * OUT_W, (m + 1) * OUT_W)
                        done(STT(x[:, t, cols], x[:, t, cols], ALPHA, G[(m % 2) * 2 + t][:, 0:OUT_W], ALU.mult, ALU.add), st["taken"])

            def ffn_dve(st):
                def step(b, s):
                    dve.wait_ge(st["silu_done"], s + 1)
                    TT(actT[:, b, :], S[b][:, T:2 * T], sil[:, b, :], ALU.mult).then_inc(st["act_ready"], 1)

                step(0, 0)
                step(1, 1)
                with dve.Fori(1, FF_STEPS // 2) as i:
                    for b in range(2):
                        dve.wait_ge(st["down_full"], i * 2 + (b - 1))
                        step(b, i * 2 + b)
                dve.wait_ge(st["down_full"], FF_STEPS)
                for t in range(NT):
                    for half in range(2):
                        cols = slice(half * 512, (half + 1) * 512)
                        done(STT(x[:, t, cols], x[:, t, cols], ALPHA, G[2 * t + half][:], ALU.mult, ALU.add))

            def attention(name, bias_of, scale, take, sink=None):
                att_dve(dve, tl, name, bias_of, scale, lambda j, o, r: take(att, j, o, r), sink)

            dve.wait_ge(c_ready, 1)
            dve.wait_ge(mod0_loaded, 16)
            for j in range(ADA_C):
                ada_sum(0, first["ada0"] + j, 0, j, j, mod0)
            dve.wait_ge(x_loaded, 16)
            ada_norm(0, mod0)

            dve.wait_ge(mod1_loaded, 16)
            n0 = first["nsa_ada1"] + 1
            for j in range(2):
                ada_sum(1, n0 + 2 * j, 0, j, j, mod1)
            with dve.Fori(1, ADA_C // 2) as i:
                tl.enter(i - 1, {dve_step: 2 * (KT - 1), ada[1]["summed"]: 2, ada[1]["taken"]: 2})
                for j in range(2):
                    ada_sum(1, n0 + 2 * j, i, j, i * 2 + j, mod1)
            tl.leave(ADA_C // 2 - 1)

            dve.wait_ge(proj["nsa_in"]["taken"], 2 * NSA_C)
            dve.wait_ge(tab_loaded, 16)
            dve.wait_ge(small_loaded, 16 * SMALL_LOADS)
            for t in range(NT):
                ins = dve.tensor_copy(kcdup[:, t, :].rearrange("p (n two d) -> p n two d", n=4, two=2),
                                      over(u[:, t, 1024:1280].rearrange("p (n d) -> p n d", n=4), 2, 2))
                done(ins, nsa_s["kc_ready"] if t == 1 else None)
            for t in range(NT):
                for lo, col in ((1280, 0), (1536, 256)):
                    kd = kdup[:, t, col:col + 256].rearrange("p (g two d) -> p g two d", g=2, two=2)
                    rotate(kd[:, :, 0, :], u[:, t, lo:lo + P].rearrange("p (g d) -> p g d", g=2), cos, sin, 2, HALF, t)
                    done(dve.tensor_copy(kd[:, :, 1, :], kd[:, :, 0, :]))
            dve.wait_ge(turn["taken"], turned_all("nsa_kc"))
            for v in range(2):
                for g in range(2):
                    for far in range(2):
                        src = a2[:, v, g, 16 * far:16 * far + 240].rearrange("p (n b two) -> p b n two", two=2, b=8)[:, :, :, 0]
                        done(TT(blkT[:, v, far * 8:far * 8 + 8, g, :], src, over(peT[:, v, far * 8:far * 8 + 8], 2, NCMP), ALU.add), nsa_s["blocks"])
            for t in range(NT):
                rotate(tok[:, t, :].rearrange("p (h d) -> p h d", h=H), u[:, t, 0:D].rearrange("p (h d) -> p h d", h=H), cos, sin, H, HALF, t)
            done(TS(var[:, 0:1], var[:, 0:1], 1.0, None, ALU.mult), nsa_s["rot_ready"])
            dve.wait_ge(nsa_s["gates_exp"], 1)
            done(TS(gate[:], gate[:], 1.0, None, ALU.add))
            done(dve.reciprocal(gate[:], gate[:]))
            dve.wait_ge(nsa_s["hidden_act"], 4)
            for g in range(2):
                for mh in range(2):
                    done(dve.tensor_copy(hid8[:, g, mh, :].rearrange("p (r n) -> p r n", r=8),
                                         over(hid[:, 1, mh, g * NCMP:(g + 1) * NCMP], 1, 8)), nsa_s["hid8"])
            dve.wait_ge(nsa_s["kv_full"], 1)
            done(dve.tensor_copy(kcT[:], S[0][:, 0:2 * NCMP]), nsa_s["kcT_ready"])
            dve.wait_ge(nsa_s["kv_full"], 2)
            for g in range(2):
                done(TT(vbd[:, g, :].rearrange("p (r d) -> p r d", r=8), over(S[1][0:8 * NCMP, g * DH:(g + 1) * DH], 1, 8),
                        bdmask[:].rearrange("p (r d) -> p r d", r=8), ALU.mult), nsa_s["vbd"])
            dve.wait_ge(nsa_s["scored"], 1)
            for t in range(NT):
                for odd in range(2):
                    done(STT(sc[:, t * H + odd:(t + 1) * H:2, :], G[odd][:, t * 8 * NCMP:(t + 1) * 8 * NCMP].rearrange("p (h n) -> p h n", h=8), SCALE,
                             over(cneg[:, t, :], 1, 8), ALU.mult, ALU.add))
            done(dve.tensor_reduce(scm[:], sc[:], AX.X, ALU.max))
            done(TT(sc[:], sc[:], over(scm[:], 2, NCMP), ALU.subtract), nsa_s["cmp_sub"])
            dve.wait_ge(nsa_s["cmp_exp"], 1)
            for t in range(NT):
                part = sc[:, t * H:(t + 1) * H, :]
                done(TT(part, part, over(cone[:, t, :], 1, H), ALU.mult))
            done(dve.tensor_reduce(scm[:], sc[:], AX.X, ALU.add))
            done(TS(scm[:], scm[:], 1.0, None, ALU.max))
            done(dve.reciprocal(scm[:], scm[:]))
            done(TT(sc[:], sc[:], over(scm[:], 2, NCMP), ALU.mult), nsa_s["cmp_prob"])
            gates = gate[:].rearrange("p t (h b) -> p t h b", b=3)
            dve.wait_ge(turn["taken"], turned_all("nsa_rot"))
            for b in range(4):
                t, g = b // 2, b % 2
                dve.wait_ge(nsa_s["cmp_out"], b + 1)
                done(TT(tok[:, t, g * 512:(g + 1) * 512].rearrange("p (h d) -> p h d", h=8), G[b][:].rearrange("p (h d) -> p h d", h=8),
                        over(gates[:, t, g * 8:(g + 1) * 8, 0], 2, DH), ALU.mult), nsa_s["cmp_summed"])

            def add_gated(st, j, o, r):
                h, branch = j % H, 1 + j // H
                done(TT(r, r, gates[:, :, h, branch], ALU.mult))
                part = tmp[:, 0, 0:2 * DH].rearrange("p (t d) -> p t d", t=NT)
                done(TT(part, o, over(r, 2, DH), ALU.mult), st["outs"])
                dst = tok[:, :, h * DH:(h + 1) * DH]
                done(TT(dst, dst, part, ALU.add))

            attention("nsa", lambda i: table("causal"), SCALE, add_gated)
            dve.wait_ge(nsa_s["silu"], 1)
            done(TT(tok[:], tok[:], u[:, :, 1792:2816], ALU.mult), out_ready)
            residual_gated(0, mod0[:, 2 * D:3 * D])
            ada_norm(1, mod1)

            dve.wait_ge(proj["dil_in"]["taken"], 2 * (2 * D // DIL_W))
            for t in range(NT):
                rotate(tok[:, t, :].rearrange("p (h d) -> p h d", h=H), u[:, t, 0:D].rearrange("p (h d) -> p h d", h=H), cos, sin, H, HALF, t)
                rotate(rotk[:, t, :].rearrange("p (h d) -> p h d", h=H), u[:, t, D:2 * D].rearrange("p (h d) -> p h d", h=H), cos, sin, H, HALF, t)
            done(TS(var[:, 0:1], var[:, 0:1], 1.0, None, ALU.mult), dil_s["rot_ready"])
            groups = (6, 5, 5)
            offs = (0, 6, 11, 16)
            group = [g for g, n in enumerate(groups) for _ in range(n)]
            attention("dil", lambda i: table(f"dil{group[i]}"), SCALE, set_head(0))
            done(dve.tensor_copy(lse[:, 0, :].rearrange("p (h t) -> p h t", t=NT), den[:, 0:H, :]), dil_s["lse_in"])
            dve.wait_ge(dil_s["lse_out"], 1)
            done(TT(lse[:, 1, :], lse[:, 0, :], negmax[:].rearrange("p h t -> p (h t)"), ALU.subtract))
            l1 = lse[:, 1, :].rearrange("p (h t) -> p t h", t=NT)
            l3 = lse[:, 3, :].rearrange("p (h t) -> p t h", t=NT)
            gl = [glse[:, k, 0:6].rearrange("p (t g) -> p t g", t=NT) for k in range(8)]
            for g in range(3):
                hs = slice(offs[g], offs[g + 1])
                done(dve.tensor_reduce(gl[0][:, :, g], l1[:, :, hs], AX.X, ALU.max))
                done(TT(l3[:, :, hs], l1[:, :, hs], over(gl[0][:, :, g], 2, groups[g]), ALU.subtract), dil_s["lse_in"] if g == 2 else None)
            dve.wait_ge(dil_s["lse_out"], 2)
            for g in range(3):
                hs = slice(offs[g], offs[g + 1])
                done(dve.tensor_reduce(gl[4][:, :, g], l3[:, :, hs], AX.X, ALU.add), dil_s["lse_in"] if g == 2 else None)
            dve.wait_ge(dil_s["lse_out"], 3)
            for g in range(3):
                done(STT(gl[1][:, :, g], gl[4][:, :, g], -float(np.log(groups[g])), gl[0][:, :, g], ALU.add, ALU.add))
            done(dve.tensor_reduce(glse[:, 6, 0:NT], gl[1], AX.X, ALU.max))
            done(TT(gl[5], gl[1], over(glse[:, 6, 0:NT], 2, 3), ALU.subtract), dil_s["lse_in"])
            dve.wait_ge(dil_s["lse_out"], 4)
            done(dve.tensor_reduce(glse[:, 6, 0:NT], gl[5], AX.X, ALU.add))
            done(dve.reciprocal(glse[:, 6, 0:NT], glse[:, 6, 0:NT]))
            done(TS(glse[:, 6, 0:NT], glse[:, 6, 0:NT], 3.0, None, ALU.mult))
            done(TT(gl[5], gl[5], over(glse[:, 6, 0:NT], 2, 3), ALU.mult))
            dve.wait_ge(dil_s["silu"], 1)
            for g in range(3):
                lo, hi = offs[g] * DH, offs[g + 1] * DH
                for t in range(NT):
                    done(STT(tok[:, t, lo:hi], tok[:, t, lo:hi], gl[5][:, t, g:g + 1], u[:, t, 3 * D + lo:3 * D + hi], ALU.mult, ALU.mult),
                         out_ready if (g, t) == (2, 1) else None)
            residual_gated(1, mod1[:, 2 * D:3 * D])
            g_final = next_vec()
            stats([x[:, t, :] for t in range(NT)], False, EPS_RMS)
            done(dve.tensor_copy(scm[:, 0:2], mv[:, :, 0]), mod1_used)
            dve.wait_ge(norm["rstd"], 2 + 1)
            for t in range(NT):
                done(STT(x[:, t, :], x[:, t, :], rstd[:, t:t + 1], g_final, ALU.mult, ALU.mult), norm["ready"])
            done(dve.tensor_copy(scm[:, 0:2], mv[:, :, 0]), vec_used)

            dve.wait_ge(proj["ab_in"]["taken"], 2 * AB_C)
            for i, (lo, w, gain) in enumerate(((0, 384, q_gain), (384, 256, kv_gain))):
                stats([u[:, t, lo:lo + w] for t in range(NT)], False, EPS_RMS)
                dve.wait_ge(norm["rstd"], 3 + i + 1)
                for t in range(NT):
                    ins = STT(tok[:, t, lo:lo + w], u[:, t, lo:lo + w], rstd[:, t:t + 1], gain, ALU.mult, ALU.mult)
                    done(ins, ab_s["c_ready"] if (i, t) == (1, 1) else None)
            for t in range(NT):
                done(dve.tensor_copy(kswa[:, t, :].rearrange("p (g two d) -> p g two d", g=2, two=2),
                                     over(u[:, t, 1184:1312].rearrange("p (g d) -> p g d", g=2), 2, 2)))
            dve.wait_ge(proj["ukv"]["taken"], 4)
            for t in range(NT):
                kr = lse[:, t, :].rearrange("p (n d) -> p n d", n=1)
                rotate(kr, u[:, t, 640:672].rearrange("p (n d) -> p n d", n=1), cos_m, sin_m, 1, 16, t)
                done(dve.tensor_copy(kcat[:, t, :].rearrange("p (h d) -> p h d", h=8)[:, :, DH:96], over(lse[:, t, :], 1, 8)))
                rotate(qcat[:, t, :].rearrange("p (h d) -> p h d", h=8)[:, :, DH:96],
                       u[:, t, 1536:2304].rearrange("p (h d) -> p h d", h=8)[:, :, DH:96], cos_m, sin_m, 8, 16, t)
            done(dve.tensor_copy(scm[:, 0:2], mv[:, :, 0]), ab_s["rot_ready"])
            dve.wait_ge(turn["taken"], turned_all("ab_rot"))
            attention("mla", lambda i: table("chunk"), MLA_SCALE, set_head(0))
            dve.wait_ge(swa_loaded, 16)
            attention("swa", lambda i: bias8[:, i * SW:(i + 1) * SW], SCALE, set_head(8), sink=lambda i: sinks[:, i:i + 1].broadcast_to([P, 2]))
            done(dve.tensor_copy(scm[:, 0:2], mv[:, :, 0]), out_ready)
            done(dve.tensor_copy(scm[:, 0:2], mv[:, :, 0]), swa_used)
            residual_deep(2)
            layer_norm(5)
            ffn_dve(ffn[0])
            layer_norm(6)

            dve.wait_ge(proj["cd_in"]["taken"], 2 * CD_C)
            f = [fox[:, k, :].rearrange("p (t h) -> p t h", t=NT) for k in range(6)]
            done(TT(f[0], u[:, :, 1536:1544], over(forget, 1, NT), ALU.add))
            done(STT(f[1], f[0], -1.0, f[0], ALU.mult, ALU.max), cd_s["f_in"])
            done(TS(f[2], f[0], 0.0, None, ALU.min))
            dve.wait_ge(cd_s["f_ln"], 1)
            done(TT(f[3], f[2], f[1], ALU.subtract), cd_s["f_ready"])
            for h in range(8):
                dve.wait_ge(cd_s["flipped"], h + 1)
                done(TT(bias8[:, h * SW:(h + 1) * SW], G[h % 4][:, 0:SW], table("chunk"), ALU.add), cd_s["bias_ready"])
            qa = [qaug[:, t, :].rearrange("p (h d) -> p h d", h=8) for t in range(NT)]
            ka = [kaug[:, t, :].rearrange("p (h d) -> p h d", h=8) for t in range(NT)]
            for t in range(NT):
                done(dve.tensor_copy(qa[t][:, :, 0:DH], u[:, t, 0:512].rearrange("p (h d) -> p h d", h=8)))
                done(dve.tensor_copy(ka[t][:, :, 0:DH], u[:, t, 512:1024].rearrange("p (h d) -> p h d", h=8)))
                done(dve.memset(qa[t][:, :, DH + 1:DH + 2], 1.0))
                done(dve.memset(ka[t][:, :, DH:DH + 1], 1.0))
            dve.wait_ge(cd_s["cum"], 1)
            for t in range(NT):
                c = S[0][:, t * 8:(t + 1) * 8].unsqueeze(2)
                done(TS(qa[t][:, :, DH:DH + 1], c, 1.0 / SCALE, None, ALU.mult))
                done(TS(ka[t][:, :, DH + 1:DH + 2], c, -1.0 / SCALE, None, ALU.mult), cd_s["aug_ready"] if t == 1 else None)
            dve.wait_ge(turn["taken"], turned_all("cd_rot"))
            attention("fox", lambda i: table("causal"), SCALE, set_head(0))
            attention("ck", lambda i: bias8[:, i * SW:(i + 1) * SW], SCALE, set_head(8))
            done(dve.tensor_copy(scm[:, 0:2], mv[:, :, 0]), out_ready)
            residual_deep(3)
            layer_norm(7)
            ffn_dve(ffn[1])
            layer_norm(8)


def shape_tables():
    f = np.float32
    tab = np.zeros((P, TAB_W), f)

    def put(name, v):
        lo, hi = TAB[name]
        tab[:, lo:hi] = np.asarray(v, f).reshape(P, hi - lo)

    def by_token(v):
        return v.reshape(NT, P, -1).transpose(1, 0, 2)

    put("ident", np.eye(P))
    put("flip", np.eye(P)[::-1])
    put("tri", np.triu(np.ones((P, P))))
    for half, c, s, inv in ((HALF, "cos", "sin", f(10000.0) ** (-np.arange(HALF, dtype=f) / f(HALF))),
                            (16, "cos_m", "sin_m", f(10000.0) ** (-np.arange(0, 32, 2, dtype=f) / f(32)))):
        ang = np.arange(T, dtype=f)[:, None] * inv.astype(f)[None, :]
        put(c, by_token(np.cos(ang)))
        put(s, by_token(np.sin(ang)))
    q, k = np.arange(T)[:, None], np.arange(T)[None, :]

    def packed(m):
        return np.concatenate([m[0:P, 0:P], m[P:, 0:P], m[P:, P:]], axis=-1)

    def hidden(seen):
        return packed(np.where(seen, 0.0, -1e30))

    put("causal", hidden(k <= q))
    put("dil0", hidden((k <= q) & (q - k <= 128)))
    put("dil1", hidden((k <= q) & ((q - k) % 4 == 0)))
    put("dil2", hidden((k <= q) & ((q - k) % 16 == 0)))
    put("chunk", hidden(k // 64 <= q // 64))
    seen = (16 * np.arange(NCMP) + 31)[None, :] <= np.arange(T)[:, None]
    put("cneg", by_token(np.where(seen, 0.0, -1e30)))
    put("cone", by_token(np.where(seen, 1.0, 0.0)))
    near = (k // 64 <= q // 64) & (k // 64 >= q // 64 - 2)
    slopes = np.exp2(-8.0 * np.arange(1, 9) / 8)
    swa = np.stack([packed(np.where(near, -s * np.abs(q - k), -1e30)) for s in slopes], axis=1).reshape(P, 8 * SW).astype(f)
    bd = np.kron(np.eye(8), np.ones((NCMP, DH))).astype(f)
    return {"tables": tab, "swa_bias": swa, "bdmask": bd}


def tiles(w, width):
    k, n = w.shape
    return np.ascontiguousarray(w.reshape(k // P, P, n // width, width).transpose(2, 1, 0, 3)).reshape(n // width, P, -1)


def ffn_steps(gate, up, down):
    return np.concatenate([tiles(gate, P), tiles(up, P), down.reshape(FF_STEPS, P, D)], axis=2)


def kernel(**inputs):
    import concourse.bacc as bacc
    from concourse.bass_utils import run_bass_kernel_spmd

    v = {k: np.asarray(w) for k, w in inputs.items()}
    rel = v["cd_rel_bias_2"][0]
    arrays = {
        "x": v["x"],
        "c": np.ascontiguousarray(v["c"].reshape(KT, P).T),
        "ada_w0": tiles(v["ada_w"][0], ADA_W), "ada_w1": tiles(v["ada_w"][1], ADA_W), "ada_b": v["ada_b"],
        "nsa_w_in": tiles(v["nsa_w_in"][0], NSA_W),
        "cmp_w1": np.stack([w[0].reshape(2, 8, P, 256).transpose(0, 2, 1, 3).reshape(2, P, 2048)
                            for w in (v["nsa_ck_w1"], v["nsa_cv_w1"])]).reshape(4, P, 2048),
        "cmp_w2": np.ascontiguousarray(np.stack([w[0].reshape(2, P, DH).transpose(1, 0, 2) for w in (v["nsa_ck_w2"], v["nsa_cv_w2"])], axis=1)),
        "pos": np.ascontiguousarray(np.stack([w[0].reshape(16, P) for w in (v["nsa_pe_k"], v["nsa_pe_v"])], axis=1)),
        "nsa_w_out": tiles(v["nsa_w_out"][0], OUT_W),
        "dil_w_in": tiles(v["dil_w_in"][0], DIL_W), "dil_w_out": tiles(v["dil_w_out"][0], OUT_W),
        "ab_w_in": tiles(v["ab_w_in_2"][0], AB_W), "ab_w_uq": tiles(v["ab_w_uq_2"][0], 768),
        "ab_w_ukv": tiles(v["ab_w_ukv_2"][0], 1024), "ab_w_out": tiles(v["ab_w_out_2"][0], OUT_W),
        "cd_w_in": tiles(v["cd_w_in_2"][0], CD_W), "cd_w_out": tiles(v["cd_w_out_2"][0], OUT_W),
        "ffn0": ffn_steps(v["ffn_w_gate_2"][0], v["ffn_w_up_2"][0], v["ffn_w_down_2"][0]),
        "ffn1": ffn_steps(v["ffn_w_gate_2"][1], v["ffn_w_up_2"][1], v["ffn_w_down_2"][1]),
        "vecs": np.stack([v["norm_g"][0], v["norm_g"][1], v["final_g"], v["ln1_g_2"][0], v["ln1_b_2"][0], v["ln2_g_2"][0],
                          v["ln2_b_2"][0], v["ln1_g_2"][1], v["ln1_b_2"][1], v["ln2_g_2"][1], v["ln2_b_2"][1]]),
        "q_norm": v["ab_q_norm_2"][0], "kv_norm": v["ab_kv_norm_2"][0], "sinks": v["ab_sinks_2"][0], "b_forget": v["cd_b_forget_2"][0],
        "rel_rev": np.pad(rel[318::-1].T, ((0, 0), (0, 512 - 319))),
        **shape_tables(),
    }
    arrays = {k: np.ascontiguousarray(w) for k, w in arrays.items()}
    nc = bacc.Bacc("TRN2", target_bir_lowering=False, num_devices=1)
    aps = {k: nc.dram_tensor(f"in_{k}", w.shape, mybir.dt.from_np(w.dtype), kind="ExternalInput").ap() for k, w in arrays.items()}
    out = nc.dram_tensor("out", v["x"].shape, F32, kind="ExternalOutput").ap()
    two_stacks(nc, aps, out)
    got = run_bass_kernel_spmd(nc, [{f"in_{k}": w for k, w in arrays.items()}], core_ids=[0])
    return got.results[0]["out"]
```

```python
from contextlib import ExitStack

import numpy as np

import concourse.bass as bass
from concourse import mybir

P = 128
D = 1024
T = 256
NT = T // P
KT = D // P
H = 16
DH = 64
HALF = DH // 2
SLOTS = 2
SLOT = 3072
ADA_C, ADA_W = 8, 384
ADA_EARLY = 6
ADA_PE = 4
NSA_C, NSA_W = 8, 358
DIL_C, DIL_W = 16, 256
AB_C, AB_W = 4, 360
CD_C, CD_W = 10, 308
OUT_C, OUT_W = 4, 256
FF_STEPS = 22
NCMP = 15
EPS_RMS = 1e-6
EPS_LN = 1e-5
ALPHA = 4.0 ** 0.25
SCALE = DH ** -0.5
MLA_SCALE = 96 ** -0.5
SW = 3 * P
FOXW = DH + 2

ALU = mybir.AluOpType
ACT = mybir.ActivationFunctionType
F32 = mybir.dt.float32
F32R = mybir.dt.float32r
AX = mybir.AxisListType

TAB = {}
_at = 0
for _name, _n in (("ident", P), ("flip", P), ("tri", P), ("cos", NT * HALF), ("sin", NT * HALF), ("cos_m", NT * 16),
                  ("sin_m", NT * 16), ("causal", SW), ("dil0", SW), ("dil1", SW), ("dil2", SW),
                  ("chunk", SW), ("cneg", NT * 2 * NCMP), ("cone", NT * NCMP)):
    TAB[_name] = (_at, _at + _n)
    _at += _n
TAB_W = _at

VECS = ("norm_g0", "norm_g1", "final_g", "ln1_g0", "ln1_b0", "ln2_g0", "ln2_b0", "ln1_g1", "ln1_b1", "ln2_g1", "ln2_b1")


class Tally:

    def __init__(self, eng, own):
        self.eng, self.own, self.n, self.turns = eng, own, {}, None

    def mark(self, ins, sem):
        ins.then_inc(sem, 1)
        self.n[sem.name] = self.n.get(sem.name, 0) + 1

    def done(self, ins, sem=None):
        sem = self.own if sem is None else sem
        self.mark(ins, sem)
        self.eng.wait_ge(sem, self.n[sem.name] + (0 if self.turns is None else self.turns * self.per[sem.name]))

    def enter(self, turns, per):
        self.turns, self.per = turns, {k.name: v for k, v in per.items()}

    def leave(self, times):
        for name, per in self.per.items():
            self.n[name] += per * (times - 1)
        self.turns = None


SMALL_LOADS = 9


class Signals:

    def __init__(self, ctx, nc, stage, names):
        self.s = {n: ctx.enter_context(nc.semaphore(f"{stage}_{n}")) for n in names.split()}

    def __getitem__(self, n):
        return self.s[n]


def over(ap, axis, n):
    a = ap.unsqueeze(axis)
    shape = list(a.shape)
    shape[axis] = n
    return a.broadcast_to(shape)


def two_stacks(nc, a, out):
    with ExitStack() as ctx:
        def sem(name):
            return ctx.enter_context(nc.semaphore(name))

        def stage(name, names):
            return Signals(ctx, nc, name, names)

        at_byte = [-(-nc.sbuf_base // 32) * 32]
        place = {}

        def sb(name, shape, dt=F32, over=None, skip=0):
            size = -(-4 * int(np.prod(shape[1:])) // 32) * 32
            if over is None:
                place[name] = at_byte[0]
                at_byte[0] += size
                assert at_byte[0] <= nc.sbuf_top, (name, at_byte[0], nc.sbuf_top)
            else:
                place[name] = place[over] + skip
            return nc.alloc_sbuf_tensor_at(name, list(shape), dt, offset=place[name])

        x = sb("x", [P, NT, D])
        tok = sb("tok", [P, NT, D])
        rotk = sb("rotk", [P, NT, D])
        hTh = sb("hTh", [P, KT, T], F32R)
        u = sb("u", [P, NT, 4 * D])
        qT = sb("qT", [P, 8, T])
        kT = sb("kT", [P, 8, T])
        q2T = sb("q2T", [P, 8, T])
        ring = sb("ring", [P, SLOTS, SLOT])
        whi = [sb("whi0", [P, SLOT], F32R), sb("whi1", [P, SLOT], F32R, over="qT")]
        wlo = [sb("wlo0", [P, SLOT], F32R), sb("wlo1", [P, SLOT], F32R, over="qT", skip=4 * SLOT)]
        scr = sb("scr", [P, 3, SW + 2])
        prob = sb("prob", [P, 3, SW + 2])
        probT = sb("probT", [P, 3, SW])
        hTl = sb("hTl", [P, KT, T], F32R, over="scr")
        acc = sb("acc", [P, 2, ADA_W], over="probT")
        sil = sb("sil", [P, 2, T], over="u")
        act = sb("act", [P, 2, T], over="u", skip=4 * 2 * T)
        acth = sb("acth", [P, 2, T], F32R, over="u", skip=8 * 2 * T)
        actl = sb("actl", [P, 2, T], F32R, over="u", skip=12 * 2 * T)
        tab = sb("tab", [P, TAB_W])
        mod0 = sb("mod0", [P, 3 * D])
        bias8 = sb("bias8", [P, 8 * SW])
        vec = sb("vec", [P, 2, D])
        small = sb("small", [P, 384 + 256 + 8 + 8 + KT])
        cb = sb("cb", [P, ADA_PE, P], over="rotk")
        tmp = sb("tmp", [P, 2, 512])
        negmax = sb("negmax", [P, H, 2])
        den = sb("den", [P, 2 * H, 2])
        rden = sb("rden", [P, 2 * H, 2])
        gate = sb("gate", [P, NT, 48])
        bstat = sb("bstat", [P, NT, 4, 6])
        mv = sb("mv", [P, NT, 2])
        kr = sb("kr", [P, NT, 32])
        var = sb("var", [P, NT])
        rstd = sb("rstd", [P, NT])
        mhalf = sb("mhalf", [P, NT])
        ones = sb("ones", [P, P])
        peT = sb("peT", [P, 2, 16])
        pe_rows = sb("pe_rows", [16, 2, P])
        hid = sb("hid", [P, 2, 2, 2 * NCMP])
        hid8 = sb("hid8", [P, 2, 2, 8 * NCMP], over="tmp")
        w2 = sb("w2", [P, 2, 3 * DH])
        kc2 = sb("kc2", [P, 2, P])
        bdmask = sb("bdmask", [8 * NCMP, 8 * DH])
        scm = sb("scm", [P, NT * H])
        lse = sb("lse", [P, 8, NT * H], over="tmp")
        glse = sb("glse", [P, 8, NT * 3])
        fox = sb("fox", [P, 6, NT * 8])
        negsink = sb("negsink", [P, 8])

        G = [ctx.enter_context(nc.psum_tensor(f"G{i}", [P, 512], F32)) for i in range(4)]
        S = [ctx.enter_context(nc.psum_tensor(f"S{i}", [P, 512], F32)) for i in range(2)]
        TB = [ctx.enter_context(nc.psum_tensor(f"T{i}", [P, 512], F32)) for i in range(2)]

        def table(name):
            lo, hi = TAB[name]
            return tab[:, lo:hi]

        ident = table("ident")
        cos = table("cos").rearrange("p (t d) -> p t d", t=NT)
        sin = table("sin").rearrange("p (t d) -> p t d", t=NT)
        cos_m = table("cos_m").rearrange("p (t d) -> p t d", t=NT)
        sin_m = table("sin_m").rearrange("p (t d) -> p t d", t=NT)
        cneg = table("cneg").rearrange("p (t n) -> p t n", t=NT)
        cone = table("cone").rearrange("p (t n) -> p t n", t=NT)
        q_gain, kv_gain = small[:, 0:384], small[:, 384:640]
        sinks, forget = small[:, 640:648], small[:, 648:656]
        csil = small[:, 656:656 + KT]
        mod1 = bias8
        a2 = u[:, 0, 2864:2864 + 4 * T].rearrange("p (v g t) -> p v g t", v=2, g=2)
        blkT = u[:, 1, 2864:2864 + 960].rearrange("p (v c g n) -> p v c g n", v=2, c=16, g=2)

        vbd = rotk[0:8 * NCMP, :, 512:1024]
        sc = kT[:, 4:6, :].rearrange("p a t -> p (a t)")[:, 0:NT * H * NCMP].rearrange("p (h n) -> p h n", n=NCMP)
        hidr = kT[0:2 * NCMP, 6:8, :]
        pcT = kT[0:8 * NCMP, 6:8, :].rearrange("p a t -> p (a t)").rearrange("p (b c) -> p b c", b=4)

        landed = [sem(f"slot{i}_landed") for i in range(SLOTS)]
        hi_done, lo_done = sem("hi_done"), sem("lo_done")
        used = sem("used")
        x_loaded, tab_loaded, small_loaded = sem("x_loaded"), sem("tab_loaded"), sem("small_loaded")
        c_loaded, c_ready, cb_ready = sem("c_loaded"), sem("c_ready"), sem("cb_ready")
        mod0_loaded, mod1_loaded, swa_loaded, ck_loaded = (sem(n) for n in ("mod0_loaded", "mod1_loaded", "swa_loaded", "ck_loaded"))
        vec_loaded, vec_used = [sem("vec0_loaded"), sem("vec1_loaded")], sem("vec_used")
        consts_set, stored = sem("consts_set"), sem("stored")
        mod1_used, swa_used = sem("mod1_used"), sem("swa_used")
        dve_step, act_step, pool_step = sem("dve_step"), sem("act_step"), sem("pool_step")
        ada = [stage(f"ada{i}", "summed full taken") for i in range(2)]
        norm = stage("norm", "var rstd ready")
        turn = stage("turn", "turned taken low")
        out_ready = sem("out_ready")
        proj = {n: stage(n, "full taken") for n in ("nsa_in", "dil_in", "ab_in", "uq", "ukv", "cd_in")}
        outp = stage("outp", "full taken")
        ffn = [stage(f"ffn{i}", "gu_hi gu_lo dn_hi dn_lo gu_full silu_done hidden high act_ready") for i in range(2)]
        att = stage("att", "scores maxes probs turns turned pv outs")
        nsa_s = stage("nsa", "pos_turned pos_taken cmp_sub cmp_summed kc_ready blocks hidden hidden_act hid_turned hid_taken hid8 kv_full kcT_ready vbd scored cmp_exp cmp_prob cmp_turned cmp_taken cmp_out rot_ready keys_ready gates_exp silu")
        dil_s = stage("dil", "rot_ready lse_in lse_out silu")
        ab_s = stage("ab", "c_ready nope rot_ready")
        cd_s = stage("cd", "f_in f_exp f_ln f_ready cum aug_ready flipped bias_ready")

        first, n_items = {}, 0
        split0, part0 = {}, {}
        n_split = n_part = 0
        for name, count in (("ada0", ADA_EARLY), ("nsa_in", 2 * NSA_C), ("ada0_gate", ADA_C - ADA_EARLY), ("w1", 4), ("nsa_out", OUT_C),
                            ("dil_in", DIL_C), ("dil_out", OUT_C), ("ab_in", AB_C), ("uq", 1), ("ukv", 1),
                            ("ab_out", OUT_C), ("ffn0", FF_STEPS), ("cd_in", CD_C), ("cd_out", OUT_C), ("ffn1", FF_STEPS)):
            first[name] = n_items
            n_items += count
            if name not in ("ada0", "ada0_gate", "w1"):
                split0[name] = n_split
                n_split += NSA_C if name == "nsa_in" else count
                if not name.startswith("ffn"):
                    part0[name] = n_part
                    n_part += NSA_C if name == "nsa_in" else count

        def slot_of(n, cols):
            return ring[:, n % SLOTS, 0:cols]

        def tiles_of(n, k, w):
            return slot_of(n, k * w).rearrange("p (k w) -> p k w", k=k)

        def wait_landed(eng, n, more=0):
            eng.wait_ge(landed[n % SLOTS], more * 16 + 16 * (n // SLOTS + 1))

        def norm_ready(i):
            return 2 * (i + 1 if i < 3 else i - 1)

        block = ctx.enter_context(nc.Block())

        group_of = {}
        for name, n0 in first.items():
            for n in range(n0, n_items):
                group_of[n] = name

        def released(n):
            name = group_of[n]
            m = n - first[name]
            if name in ("ada0", "ada0_gate"):
                return ada[0]["full"], m + 1 + (ADA_EARLY if name == "ada0_gate" else 0)
            if name == "nsa_in":
                return (ada[1]["summed"], m // 2 + 1) if m % 2 else (lo_done, part0[name] + m // 2 + 1)
            if name == "w1":
                return nsa_s["hidden"], m + 1
            if name.startswith("ffn"):
                return ffn[int(name[3:])]["dn_lo"], m + 1
            return lo_done, part0[name] + m + 1

        @block.sync
        def _(sp):
            def fetch(n, src, cols):
                if n >= SLOTS:
                    sp.wait_ge(*released(n - SLOTS))
                sp.dma_start(slot_of(n, cols), src).then_inc(landed[n % SLOTS], 16)

            def group(name, srcs, cols):
                n0, count = first[name], srcs.shape[0]
                for j in range(min(SLOTS, count)):
                    fetch(n0 + j, srcs[j], cols)
                if count > 2 * SLOTS:
                    with sp.Fori(1, count // SLOTS) as i:
                        for j in range(SLOTS):
                            done, value = released(n0 + j)
                            sp.wait_ge(done, i * SLOTS + (value - SLOTS))
                            sp.dma_start(slot_of(n0 + j, cols), srcs[i * SLOTS + j]).then_inc(landed[(n0 + j) % SLOTS], 16)
                else:
                    for j in range(SLOTS, count):
                        fetch(n0 + j, srcs[j], cols)

            group("ada0", a["ada_w0"][0:ADA_EARLY], KT * ADA_W)
            n0 = first["nsa_in"]
            fetch(n0, a["nsa_w_in"][0], KT * NSA_W)
            fetch(n0 + 1, a["ada_w1"][0], KT * ADA_W)
            with sp.Fori(1, NSA_C) as i:
                sp.wait_ge(lo_done, i)
                sp.dma_start(slot_of(n0, KT * NSA_W), a["nsa_w_in"][i]).then_inc(landed[0], 16)
                sp.wait_ge(ada[1]["summed"], i)
                sp.dma_start(slot_of(n0 + 1, KT * ADA_W), a["ada_w1"][i]).then_inc(landed[1], 16)
            group("ada0_gate", a["ada_w0"][ADA_EARLY:], KT * ADA_W)
            group("w1", a["cmp_w1"], 2048)
            group("nsa_out", a["nsa_w_out"], KT * OUT_W)
            group("dil_in", a["dil_w_in"], KT * DIL_W)
            group("dil_out", a["dil_w_out"], KT * OUT_W)
            group("ab_in", a["ab_w_in"], KT * AB_W)
            group("uq", a["ab_w_uq"], 3 * 768)
            group("ukv", a["ab_w_ukv"], 2 * 1024)
            group("ab_out", a["ab_w_out"], KT * OUT_W)
            group("ffn0", a["ffn0"], 3072)
            group("cd_in", a["cd_w_in"], KT * CD_W)
            group("cd_out", a["cd_w_out"], KT * OUT_W)
            group("ffn1", a["ffn1"], 3072)
            for t in range(NT):
                sp.wait_ge(norm["ready"], norm_ready(8) - 1 + t)
                sp.dma_start(out[:, t * P:(t + 1) * P, :].rearrange("b p d -> p (b d)"), x[:, t, :]).then_inc(stored, 16)
            sp.wait_ge(stored, 16 * NT)

        turns = {}
        turn_n = [0, 0, 0]

        def plan_turn(name, groups, split=False):
            turns[name] = (groups, *turn_n, split)
            turn_n[0] += len(groups)
            turn_n[1] += sum(len(takes) for _, takes in groups)
            turn_n[2] += len(groups) if split else 0

        def turned_all(name):
            groups, _, t0, l0, split = turns[name]
            return (turn["low"], l0 + len(groups)) if split else (turn["taken"], t0 + sum(len(takes) for _, takes in groups))

        def turn_src(g, take):
            rows, cols, dst, n = take
            return TB[g % 2][rows[0]:rows[1], cols[0]:cols[1]].rearrange("p (n c) -> p n c", n=n)[:, :, P - dst.shape[2]:]

        def turn_pe(pe, name, ready=None):
            groups, _, t0, l0, split = turns[name]
            for g, (srcs, takes) in enumerate(groups):
                if ready is not None:
                    ready(g)
                if g >= 2:
                    pe.wait_ge(*((turn["low"], l0 + g - 1) if split else (turn["taken"], t0 + (g - 1) * len(takes))))
                for n, (src, width) in enumerate(srcs):
                    ins = pe.transpose(TB[g % 2][0:width, n * P:(n + 1) * P], src, ident)
                ins.then_inc(turn["turned"], 1)

        def turn_act(act_, name):
            groups, g0 = turns[name][0:2]
            for g, (srcs, takes) in enumerate(groups):
                act_.wait_ge(turn["turned"], g0 + g + 1)
                for take in takes:
                    act_.copy(take[2], turn_src(g, take)).then_inc(turn["taken"], 1)

        def turn_low(dve, name):
            groups, _, t0, _, _ = turns[name]
            for g, (srcs, takes) in enumerate(groups):
                dve.wait_ge(turn["taken"], t0 + g + 1)
                rows, cols, dst, n = takes[0]
                low = dst_low[name][g]
                dve.tensor_tensor(low, turn_src(g, takes[0]), dst.bitcast(F32), ALU.subtract).then_inc(turn["low"], 1)

        def rotate(tl, dst, src, c, s, n, half, t, scratch, ready=None):
            TT, done = tl.eng.tensor_tensor, tl.done
            x1, x2 = src[:, :, 0:half], src[:, :, half:2 * half]
            cb_, sb_ = over(c[:, t, :], 1, n), over(s[:, t, :], 1, n)
            ta = scratch[:, 0:n * half].rearrange("p (n d) -> p n d", n=n)
            tb = scratch[:, 512:512 + n * half].rearrange("p (n d) -> p n d", n=n)
            tl.mark(TT(ta, x1, cb_, ALU.mult), tl.own)
            done(TT(tb, x2, sb_, ALU.mult))
            done(TT(dst[:, :, 0:half], ta, tb, ALU.subtract))
            tl.mark(TT(ta, x2, cb_, ALU.mult), tl.own)
            done(TT(tb, x1, sb_, ALU.mult))
            done(TT(dst[:, :, half:2 * half], ta, tb, ALU.add), ready)

        def rows_to(dst, src, per=4, width=P, t_n=NT):
            groups = []
            for t in range(t_n):
                n_all = src[t].shape[1]
                for n in range(0, n_all, per):
                    m = min(per, n_all - n)
                    groups.append(([(src[t][:, n + j, :], width) for j in range(m)],
                                   [((0, width), (0, m * P), dst[0:width, n:n + m, t * P:(t + 1) * P], m)]))
            return groups

        def blocks_of(ap2, w=P):
            return [ap2[:, t, :].rearrange("p (n w) -> p n w", w=w) for t in range(NT)]

        turn_full = rows_to(hTh, blocks_of(tok))
        turn_resid = rows_to(hTh, blocks_of(x))
        low_full = [takes[0][2] for _, takes in rows_to(hTl, blocks_of(tok))]
        dst_low = {name: low_full for name in ("h0", "h1", "o0", "o1", "o2", "o3", "x0", "x1", "f0", "f1")}

        def att_pe(pe, name):
            jobs, b0 = att_jobs[name], att_base[name]
            n = len(jobs)
            for i in range(n + 3):
                if i < n:
                    q, k, _, _ = jobs[i]
                    if i >= 2:
                        pe.wait_ge(att["maxes"], 2 * (b0 + i - 1))
                    pe.matmul(S[i % 2][:, 0:P], q[:, 0:P], k[:, 0:P], start=True, stop=True)
                    pe.matmul(S[i % 2][:, P:SW], q[:, P:T], k[:, 0:T], start=True, stop=True).then_inc(att["scores"], 1)
                if 2 <= i < n + 2:
                    j = i - 2
                    pe.wait_ge(att["probs"], 2 * (b0 + j) + 2)
                    if j >= 2:
                        pe.wait_ge(att["turned"], b0 + j - 1)
                    for b in range(3):
                        ins = pe.transpose(TB[j % 2][:, b * P:(b + 1) * P], prob[:, j % 3, 1 + b * P:1 + (b + 1) * P], ident)
                    ins.then_inc(att["turns"], 1)
                if i >= 3:
                    j = i - 3
                    v = jobs[j][2]
                    pe.wait_ge(att["turned"], b0 + j + 1)
                    if j >= 4:
                        pe.wait_ge(att["outs"], b0 + j - 3)
                    o = G[j % 4]
                    pt = probT[:, j % 3, :]
                    pe.matmul(o[:, 0:P], pt[:, 0:P], v[0], start=True, stop=True)
                    pe.matmul(o[:, P:2 * P], pt[:, P:2 * P], v[0], start=True, stop=False)
                    pe.matmul(o[:, P:2 * P], pt[:, 2 * P:SW], v[1], start=False, stop=True).then_inc(att["pv"], 1)

        def att_dve(dve, tl, name, bias_of, scale, take, sink=None):
            jobs, b0 = att_jobs[name], att_base[name]
            n = len(jobs)
            for i in range(n + 4):
                if i < n:
                    dve.wait_ge(att["scores"], b0 + i + 1)
                    if i >= 3:
                        dve.wait_ge(att["probs"], 2 * (b0 + i) - 4)
                    s, bank, bias, h = scr[:, i % 3, :], S[i % 2], bias_of(i), i % H
                    if i >= H:
                        dve.wait_ge(att["probs"], 2 * (b0 + i - H) + 2)
                    least = 3e38
                    if sink is not None:
                        tl.mark(dve.tensor_copy(s[:, 0:SW + 2:SW + 1], sink(i).broadcast_to([P, 2])), tl.own)
                        least = sink(i)
                    tl.mark(dve.tensor_tensor_reduce(s[:, 1:1 + P], bank[:, 0:P], bias[:, 0:P], -scale, least, ALU.add, ALU.min,
                                                     negmax[:, h, 0:1]), att["maxes"])
                    tl.mark(dve.tensor_tensor_reduce(s[:, 1 + P:1 + SW], bank[:, P:SW], bias[:, P:SW], -scale, least, ALU.add, ALU.min,
                                                     negmax[:, h, 1:2]), att["maxes"])
                if i >= 4:
                    j = i - 4
                    dve.wait_ge(att["pv"], b0 + j + 1)
                    tl.done(dve.reciprocal(rden[:, j, :], den[:, j, :]))
                    off = jobs[j][3]
                    take(j, G[j % 4][:, 0:2 * P].rearrange("p (t d) -> p t d", t=NT)[:, :, off:off + DH], rden[:, j, :])

        def att_act(act_, name, sink=False):
            n, b0 = len(att_jobs[name]), att_base[name]
            lo, hi = (0, SW + 2) if sink else (1, SW + 1)
            for i in range(n + 2):
                if i < n:
                    act_.wait_ge(att["maxes"], 2 * (b0 + i) + 2)
                    if i >= 3:
                        act_.wait_ge(att["turns"], b0 + i - 2)
                    h, b = i % H, i % 3
                    act_.activation(prob[:, b, lo:1 + P], scr[:, b, lo:1 + P], ACT.Exp, bias=negmax[:, h, 0:1], scale=-1.0,
                                    accum_out=den[:, i, 0:1]).then_inc(att["probs"], 1)
                    act_.activation(prob[:, b, 1 + P:hi], scr[:, b, 1 + P:hi], ACT.Exp, bias=negmax[:, h, 1:2], scale=-1.0,
                                    accum_out=den[:, i, 1:2]).then_inc(att["probs"], 1)
                if i >= 2:
                    j = i - 2
                    act_.wait_ge(att["turns"], b0 + j + 1)
                    if j >= 3:
                        act_.wait_ge(att["pv"], b0 + j - 2)
                    act_.copy(probT[:, j % 3, :], TB[j % 2][:, 0:SW]).then_inc(att["turned"], 1)

        def pair(tile, h):
            return tile[(h % 2) * DH:(h % 2) * DH + DH, h // 2, :]

        def v_of(lo, off):
            return [u[:, t, lo:lo + P] for t in range(NT)], off

        def twin(tile, h, g):
            return tile[(h % 2) * DH:(h % 2) * DH + DH, g, :]

        nsa_jobs = [(pair(qT, h), twin(kT, h, br * 2 + h // 8), *v_of(1408 + 256 * br, DH * (h // 8)))
                    for br in range(2) for h in range(H)]
        dil_jobs = [(pair(qT, h), pair(kT, h), *v_of(2 * D + P * (h // 2), DH * (h % 2))) for h in range(H)]
        mla_jobs = [(qT[0:96, h, :], kT[0:96, h, :], *v_of(2560 + P * h, DH)) for h in range(8)]
        swa_jobs = [(pair(q2T, h), twin(q2T, h, 4 + h // 4), *v_of(1312, DH * (h // 4))) for h in range(8)]
        fox_jobs = [(qT[0:FOXW, h, :], kT[0:FOXW, h, :], *v_of(1024 + P * (h // 2), DH * (h % 2))) for h in range(8)]
        ck_jobs = [(pair(q2T, h), twin(q2T, h, 4 + h // 2), *v_of(2568 + P * (h // 2), DH * (h % 2))) for h in range(8)]
        att_jobs = {"nsa": nsa_jobs, "dil": dil_jobs, "mla": mla_jobs, "swa": swa_jobs, "fox": fox_jobs, "ck": ck_jobs}
        att_base, heads_n = {}, 0
        for name, jobs in att_jobs.items():
            att_base[name] = heads_n
            heads_n += len(jobs)

        nsa_plain = rows_to(q2T, blocks_of(u[:, :, 0:D]))
        kdup = rotk[:, :, 0:512]
        kcdup = rotk[:, :, 512:1024]
        nsa_rot = rows_to(qT, blocks_of(tok)) + rows_to(kT, blocks_of(kdup))
        a2f = a2.rearrange("p v g t -> p (v g) t")
        nsa_kc = [([(kcdup[:, t, n * P:(n + 1) * P], P) for n in range(4)],
                   [((0, DH), (0, 4 * P), a2f[0:DH, :, t * P:(t + 1) * P], 4),
                    ((DH, P), (0, 4 * P), a2f[DH:P, :, max(t * P - 1, 0):(t + 1) * P - 1], 4)]) for t in range(NT)]
        dil_rot = rows_to(qT, blocks_of(tok)) + rows_to(kT, blocks_of(rotk))
        ab_c = rows_to(hTh, blocks_of(tok[:, :, 0:640]))
        dst_low["ab_c"] = [takes[0][2] for _, takes in rows_to(hTl, blocks_of(tok[:, :, 0:640]))]
        qcat = tok[:, :, 0:768]
        kcat = rotk[:, :, 0:768]
        kswa = tok[:, :, 768:1024]
        ab_rot = (rows_to(qT, blocks_of(qcat, 96), width=96) + rows_to(kT, blocks_of(kcat, 96), width=96)
                  + rows_to(q2T, blocks_of(u[:, :, 672:1184])) + rows_to(q2T[:, 4:6, :], blocks_of(kswa)))
        qaug = tok[:, :, 0:8 * FOXW]
        kaug = rotk[:, :, 0:8 * FOXW]
        cd_rot = (rows_to(qT, blocks_of(qaug, FOXW), width=FOXW) + rows_to(kT, blocks_of(kaug, FOXW), width=FOXW)
                  + rows_to(q2T, blocks_of(u[:, :, 1544:2056])) + rows_to(q2T[:, 4:8, :], blocks_of(u[:, :, 2056:2568])))

        for name, groups in (("h0", turn_full), ("nsa_plain", nsa_plain), ("nsa_kc", nsa_kc), ("nsa_rot", nsa_rot), ("o0", turn_full),
                             ("h1", turn_full), ("dil_rot", dil_rot), ("o1", turn_full), ("x0", turn_resid), ("ab_c", ab_c),
                             ("ab_rot", ab_rot), ("o2", turn_full), ("f0", turn_resid), ("x1", turn_resid), ("cd_rot", cd_rot),
                             ("o3", turn_full), ("f1", turn_resid)):
            plan_turn(name, groups, name in dst_low)

        @block.gpsimd
        def _(pool):
            pool.memset(mhalf[:], -0.5).then_inc(consts_set, 1)
            pool.memset(ones[:], 1.0).then_inc(consts_set, 1)
            pool.memset(kc2[:], 0.0).then_inc(consts_set, 1)
            pool.wait_ge(consts_set, 3)
            tl = Tally(pool, pool_step)

            def load_vec(v):
                if v >= 2:
                    pool.wait_ge(vec_used, v - 1)
                pool.dma_start(vec[:, v % 2, :], a["vecs"][v:v + 1, :].rearrange("a d -> (a d)").partition_broadcast(P)).then_inc(vec_loaded[v % 2], 16)

            def rstd_of(i):
                for t in range(NT):
                    pool.wait_ge(norm["var"], 2 * i + t + 1)
                    pool.tensor_tensor(rstd[:, t:t + 1], var[:, t:t + 1], mhalf[:, t:t + 1], ALU.pow).then_inc(norm["rstd"], 1)

            def rotate_all(dst, lo, scratch, ready):
                for t in range(NT):
                    rotate(tl, dst[:, t, :].rearrange("p (h d) -> p h d", h=H), u[:, t, lo:lo + D].rearrange("p (h d) -> p h d", h=H),
                           cos, sin, H, HALF, t, scratch, ready)

            load_vec(0)
            load_vec(1)
            rstd_of(0)
            load_vec(2)
            pool.wait_ge(tab_loaded, 16)
            pool.wait_ge(proj["nsa_in"]["taken"], 2 * -(-D // NSA_W))
            rotate_all(tok, 0, u[:, 1, 2864:3888], nsa_s["rot_ready"])
            rstd_of(1)
            for dst, lo in ((tok, 0), (rotk, D)):
                pool.wait_ge(proj["dil_in"]["taken"], 2 * ((lo + D) // DIL_W))
                rotate_all(dst, lo, tmp[:].rearrange("p a b -> p (a b)"), dil_s["rot_ready"])
            rstd_of(2)
            load_vec(3)
            load_vec(4)
            pool.wait_ge(mod1_used, 1)
            pool.dma_start(bias8[:], a["swa_bias"]).then_inc(swa_loaded, 16)
            rstd_of(3)
            rstd_of(4)
            rstd_of(5)
            load_vec(5)
            load_vec(6)
            pool.wait_ge(swa_used, 1)
            b8 = bias8[:].rearrange("p (h w) -> p h w", h=8)
            rev = a["rel_rev"]
            for lo, base in ((0, P), (P, 0), (2 * P, P)):
                pool.dma_start(b8[:, :, lo:lo + P], bass.AP(tensor=rev.tensor, offset=base, ap=[[1, P], [rev.shape[1], 8], [1, P]])).then_inc(ck_loaded, 16)
            rstd_of(6)
            load_vec(7)
            load_vec(8)
            rstd_of(7)
            load_vec(9)
            load_vec(10)
            rstd_of(8)

        @block.tensor
        def _(pe):
            def ada_chunk(layer, m, j, direct=None):
                bank = S[j % 2][:, 0:ADA_W]
                if direct is not None:
                    wait_landed(pe, direct)
                    w = tiles_of(direct, KT, ADA_W)
                    for k in range(ADA_PE):
                        pe.matmul(bank, cb[:, k, :], w[:, k, :], start=(k == 0), stop=False)
                pe.wait_ge(ada[layer]["summed"], m + 1)
                pe.matmul(bank, ones[:], acc[:, j % 2, :], start=(direct is None), stop=True).then_inc(ada[layer]["full"], 1)

            def split_products(out_, act_h, act_l, w_h, w_l, first_, last_):
                pe.matmul(out_, act_h, w_h, start=first_, stop=False)
                pe.matmul(out_, act_h, w_l, start=False, stop=False)
                return pe.matmul(out_, act_l, w_h, start=False, stop=last_)

            def gemm_chunk(name, st, m, j, w, n_k=KT):
                pe.wait_ge(lo_done, m + (part0[name] + 1))
                wh, wl = (part[j % 2][:, 0:n_k * w].rearrange("p (k w) -> p k w", k=n_k) for part in (whi, wlo))
                for t in range(NT):
                    for k in range(n_k):
                        ins = split_products(G[(j % 2) * 2 + t][:, 0:w], hTh[:, k, t * P:(t + 1) * P], hTl[:, k, t * P:(t + 1) * P],
                                             wh[:, k, :], wl[:, k, :], k == 0, k == n_k - 1)
                    ins.then_inc(st["full"] if t == 0 else used, 1)

            def gemm(name, st, count, w, before=0):
                for j in range(2):
                    gemm_chunk(name, st, j, j, w)
                if count > 4:
                    with pe.Fori(1, count // 2) as i:
                        for j in range(2):
                            pe.wait_ge(st["taken"], i * 4 + (before + 2 * (j - 1)))
                            gemm_chunk(name, st, i * 2 + j, j, w)
                else:
                    for m in range(2, count):
                        pe.wait_ge(st["taken"], before + 2 * (m - 1))
                        gemm_chunk(name, st, m, m, w)

            def wide(name, st, k0, k_n, w):
                pe.wait_ge(lo_done, part0[name] + 1)
                slot = split0[name] % 2
                wh, wl = (part[slot][:, 0:k_n * 2 * w].rearrange("p (k w) -> p k w", k=k_n) for part in (whi, wlo))
                for t in range(NT):
                    for half in range(2):
                        cols = slice(half * w, (half + 1) * w)
                        for k in range(k_n):
                            ins = split_products(G[2 * t + half][:, 0:w], hTh[:, k0 + k, t * P:(t + 1) * P], hTl[:, k0 + k, t * P:(t + 1) * P],
                                                 wh[:, k, cols], wl[:, k, cols], k == 0, k == k_n - 1)
                        ins.then_inc(st["full"] if (t, half) != (1, 1) else used, 1)

            def ffn_pe(name, st):
                def gate_up(b, s):
                    pe.wait_ge(st["gu_lo"], s + 1)
                    for part in range(2):
                        bank = S[b][:, part * T:(part + 1) * T]
                        for k in range(KT):
                            at = slice((part * KT + k) * P, (part * KT + k + 1) * P)
                            pe.matmul(bank, whi[b][:, at], hTh[:, k, :], start=(k == 0), stop=False)
                            pe.matmul(bank, whi[b][:, at], hTl[:, k, :], start=False, stop=False)
                            ins = pe.matmul(bank, wlo[b][:, at], hTh[:, k, :], start=False, stop=(k == KT - 1))
                    ins.then_inc(st["gu_full"], 1)

                def down(b, s, start, stop):
                    pe.wait_ge(st["dn_lo"], s + 1)
                    pe.wait_ge(st["act_ready"], s + 1)
                    for t in range(NT):
                        for half in range(2):
                            at = slice(2 * KT * P + half * 512, 2 * KT * P + (half + 1) * 512)
                            ts = slice(t * P, (t + 1) * P)
                            ins = split_products(G[2 * t + half][:], acth[:, b, ts], actl[:, b, ts], whi[b][:, at], wlo[b][:, at], start, stop)
                    ins.then_inc(used, 1)

                gate_up(0, 0)
                gate_up(1, 1)
                down(0, 0, True, False)
                with pe.Fori(0, (FF_STEPS - 2) // 2) as i:
                    for j in range(2):
                        s = i * 2 + (1 + j)
                        pe.wait_ge(st["hidden"], s)
                        gate_up(j, s + 1)
                        down(1 - j, s, False, False)
                down((FF_STEPS - 1) % 2, FF_STEPS - 1, False, True)

            def norm_tiles(i, per_tile=2):
                def ready(g):
                    if g % per_tile == 0:
                        pe.wait_ge(norm["ready"], norm_ready(i) - 1 + g // per_tile)
                return ready

            pe.wait_ge(consts_set, 3)
            pe.wait_ge(cb_ready, ADA_PE)
            for m in range(ADA_EARLY):
                if m >= 2:
                    pe.wait_ge(ada[0]["taken"], m - 1)
                ada_chunk(0, m, m, first["ada0"] + m)

            pe.wait_ge(tab_loaded, 16)
            turn_pe(pe, "h0", norm_tiles(0))
            pe.wait_ge(*turned_all("h0"))
            st = proj["nsa_in"]
            gemm_chunk("nsa_in", st, 0, 0, NSA_W)
            gemm_chunk("nsa_in", st, 1, 1, NSA_W)
            ada_chunk(1, 0, 0)
            with pe.Fori(1, NSA_C // 2) as i:
                for j in range(2):
                    pe.wait_ge(st["taken"], i * 4 + 2 * (j - 1))
                    gemm_chunk("nsa_in", st, i * 2 + j, j, NSA_W)
                    ada_chunk(1, i * 2 + (j - 1), j + 1)
            ada_chunk(1, ADA_C - 1, ADA_C - 1)
            for m in range(ADA_EARLY, ADA_C):
                pe.wait_ge(ada[1]["taken"], m + 1)
                ada_chunk(0, m, m, first["ada0_gate"] + m - ADA_EARLY)

            pe.wait_ge(st["taken"], 2 * NSA_C)
            turn_pe(pe, "nsa_plain")
            pe.wait_ge(*turned_all("nsa_plain"))
            pe.wait_ge(small_loaded, 16 * SMALL_LOADS)
            for v in range(2):
                ins = pe.transpose(TB[0][:, v * 16:(v + 1) * 16], pe_rows[:, v, :], ident[0:16, 0:16])
            ins.then_inc(nsa_s["pos_turned"], 1)
            pe.wait_ge(nsa_s["kc_ready"], 1)
            pe.wait_ge(nsa_s["pos_taken"], 1)
            turn_pe(pe, "nsa_kc")
            pe.wait_ge(nsa_s["blocks"], 8)
            for v in range(2):
                for kh in range(2):
                    n = first["w1"] + 2 * v + kh
                    wait_landed(pe, n)
                    w1 = tiles_of(n, 8, 256)
                    for c in range(8):
                        ins = pe.matmul(G[v][0:2 * NCMP, 0:256], blkT[:, v, kh * 8 + c, :, :], w1[:, c, :],
                                        start=(kh == 0 and c == 0), stop=(kh == 1 and c == 7))
                    ins.then_inc(nsa_s["hidden"], 1)
            pe.wait_ge(nsa_s["rot_ready"], NT)
            pe.wait_ge(nsa_s["keys_ready"], NT)
            turn_pe(pe, "nsa_rot")
            pe.wait_ge(*turned_all("nsa_rot"))
            pe.wait_ge(nsa_s["hidden_act"], 2)
            for v in range(2):
                for mh in range(2):
                    at = (2 * v + mh) * 2 * NCMP
                    ins = pe.transpose(TB[0][:, at:at + 2 * NCMP], hidr[:, v, mh * P:(mh + 1) * P], ident[0:2 * NCMP, 0:2 * NCMP])
            ins.then_inc(nsa_s["hid_turned"], 1)
            pe.wait_ge(nsa_s["hid_taken"], 1)
            pe.wait_ge(ada[0]["taken"], ADA_C)
            for mh in range(2):
                ins = pe.matmul(S[0][:, 0:2 * NCMP], w2[:, mh, 0:P], hid[:, 0, mh, :], start=(mh == 0), stop=(mh == 1))
            ins.then_inc(nsa_s["kv_full"], 1)
            pe.wait_ge(nsa_s["hid8"], 4)
            for g in range(2):
                for mh in range(2):
                    ins = pe.matmul(S[1][0:8 * NCMP, g * DH:(g + 1) * DH], hid8[:, g, mh, :], w2[:, mh, P:3 * DH],
                                    start=(mh == 0), stop=(mh == 1))
            ins.then_inc(nsa_s["kv_full"], 1)
            pe.wait_ge(nsa_s["kcT_ready"], 4)
            for t in range(NT):
                for pr in range(H // 2):
                    ins = pe.matmul(G[2 * t + pr // 4][:, (pr % 4) * P:(pr % 4 + 1) * P], q2T[:, pr, t * P:(t + 1) * P],
                                    kc2[:, pr // 4, :], start=True, stop=True)
            ins.then_inc(nsa_s["scored"], 1)
            pe.wait_ge(nsa_s["cmp_prob"], 1)
            for b in range(4):
                ins = pe.transpose(TB[0][0:8 * NCMP, b * P:(b + 1) * P], sc[:, b * 8:(b + 1) * 8, :], ident)
            ins.then_inc(nsa_s["cmp_turned"], 1)
            pe.wait_ge(nsa_s["cmp_taken"], 1)
            pe.wait_ge(nsa_s["vbd"], 2)
            for b in range(4):
                pe.matmul(G[b][:], pcT[:, b, :], vbd[:, b % 2, :], start=True, stop=True).then_inc(nsa_s["cmp_out"], 1)
            pe.wait_ge(nsa_s["cmp_summed"], 4)
            att_pe(pe, "nsa")

            def project_out(i, name):
                pe.wait_ge(out_ready, i + 1)
                turn_pe(pe, f"o{i}")
                pe.wait_ge(*turned_all(f"o{i}"))
                gemm(name, outp, OUT_C, OUT_W, i * 2 * OUT_C)

            project_out(0, "nsa_out")

            turn_pe(pe, "h1", norm_tiles(1))
            pe.wait_ge(*turned_all("h1"))
            gemm("dil_in", proj["dil_in"], DIL_C, DIL_W)
            pe.wait_ge(proj["dil_in"]["taken"], 2 * DIL_C)
            turn_pe(pe, "dil_rot", lambda g: pe.wait_ge(dil_s["rot_ready"], g // 2 + 1))
            pe.wait_ge(*turned_all("dil_rot"))
            att_pe(pe, "dil")
            project_out(1, "dil_out")

            turn_pe(pe, "x0", norm_tiles(2))
            pe.wait_ge(*turned_all("x0"))
            gemm("ab_in", proj["ab_in"], AB_C, AB_W)
            pe.wait_ge(ab_s["c_ready"], 1)
            turn_pe(pe, "ab_c")
            pe.wait_ge(*turned_all("ab_c"))
            pe.wait_ge(proj["ab_in"]["taken"], 2 * AB_C)
            wide("uq", proj["uq"], 0, 3, 384)
            pe.wait_ge(proj["uq"]["taken"], 4)
            wide("ukv", proj["ukv"], 3, 2, 512)
            pe.wait_ge(ab_s["rot_ready"], 1)
            pe.wait_ge(ab_s["nope"], 4)
            pe.wait_ge(proj["ukv"]["taken"], 4)
            turn_pe(pe, "ab_rot")
            pe.wait_ge(*turned_all("ab_rot"))
            att_pe(pe, "mla")
            pe.wait_ge(att["outs"], att_base["mla"] + 8)
            att_pe(pe, "swa")
            project_out(2, "ab_out")

            turn_pe(pe, "f0", norm_tiles(5))
            pe.wait_ge(*turned_all("f0"))
            ffn_pe("ffn0", ffn[0])

            turn_pe(pe, "x1", norm_tiles(6))
            pe.wait_ge(*turned_all("x1"))
            gemm("cd_in", proj["cd_in"], CD_C, CD_W)
            pe.wait_ge(proj["cd_in"]["taken"], 2 * CD_C)
            pe.wait_ge(ck_loaded, 48)
            for h in range(8):
                if h >= 4:
                    pe.wait_ge(cd_s["bias_ready"], h - 3)
                pe.matmul(G[h % 4][:, 0:SW], table("flip"), bias8[:, h * SW:(h + 1) * SW], start=True, stop=True).then_inc(cd_s["flipped"], 1)
            pe.wait_ge(cd_s["f_ready"], 1)
            f = fox[:, 3, :]
            pe.matmul(S[0][:, 0:8], table("tri"), f[:, 0:8], start=True, stop=True)
            pe.matmul(S[0][:, 8:16], table("tri"), f[:, 8:16], start=True, stop=False)
            pe.matmul(S[0][:, 8:16], ones[:], f[:, 0:8], start=False, stop=True).then_inc(cd_s["cum"], 1)
            pe.wait_ge(cd_s["aug_ready"], 1)
            pe.wait_ge(proj["cd_in"]["taken"], 2 * CD_C)
            turn_pe(pe, "cd_rot")
            pe.wait_ge(*turned_all("cd_rot"))
            att_pe(pe, "fox")
            pe.wait_ge(att["outs"], att_base["fox"] + 8)
            att_pe(pe, "ck")
            project_out(3, "cd_out")

            turn_pe(pe, "f1", norm_tiles(7))
            pe.wait_ge(*turned_all("f1"))
            ffn_pe("ffn1", ffn[1])

        @block.scalar
        def _(sc_e):
            tl = Tally(sc_e, act_step)
            sc_e.dma_start(csil, a["c"]).then_inc(c_loaded, 16)
            sc_e.dma_start(mod0[:], a["ada_b"][0:1, :].rearrange("a d -> (a d)").partition_broadcast(P)).then_inc(mod0_loaded, 16)
            sc_e.dma_start(x[:], a["x"].rearrange("b (t p) d -> p (b t) d", p=P)).then_inc(x_loaded, 16)
            sc_e.dma_start(tab[:], a["tables"]).then_inc(tab_loaded, 16)
            sc_e.dma_start(mod1[:], a["ada_b"][1:2, :].rearrange("a d -> (a d)").partition_broadcast(P)).then_inc(mod1_loaded, 16)
            for dst, src in ((q_gain, a["q_norm"]), (kv_gain, a["kv_norm"]), (sinks, a["sinks"]), (forget, a["b_forget"])):
                sc_e.dma_start(dst, src.partition_broadcast(P)).then_inc(small_loaded, 16)
            sc_e.dma_start(bdmask[:], a["bdmask"]).then_inc(small_loaded, 16)
            sc_e.dma_start(pe_rows[:], a["pos"]).then_inc(small_loaded, 16)
            sc_e.dma_start(w2[:, :, 0:DH], a["cmp_w2"][:, 0]).then_inc(small_loaded, 16)
            sc_e.dma_start(w2[:, :, DH:P], a["cmp_w2"][:, 0]).then_inc(small_loaded, 16)
            sc_e.dma_start(w2[:, :, P:3 * DH], a["cmp_w2"][:, 1]).then_inc(small_loaded, 16)
            sc_e.wait_ge(c_loaded, 16)
            tl.done(sc_e.activation(csil, csil, ACT.Silu), c_ready)

            def high(name, q, j, cols, stride=1):
                n0, k0 = first[name], split0[name]
                n = n0 + j
                if stride == 1:
                    sc_e.wait_ge(landed[n % 2], q * 16 + 16 * (n // 2 + 1))
                else:
                    sc_e.wait_ge(landed[0], q * 32 + 16 * (n0 // 2 + j + 1))
                if not isinstance(q, int) or k0 + 2 * q + j >= 2:
                    sc_e.wait_ge(used, q * 2 + (k0 + j - 1))
                raw = ring[:, n % 2 if stride == 1 else 0, 0:cols]
                sc_e.copy(whi[(k0 + j) % 2][:, 0:cols], raw).then_inc(hi_done, 1)

            def take_chunk(name, st, q, j, w):
                at = q * (2 * w) + j * w
                for t in range(NT):
                    if t == 0:
                        sc_e.wait_ge(st["full"], q * 2 + j + 1)
                    else:
                        sc_e.wait_ge(used, q * 2 + (split0[name] + j + 1))
                    dst = u[:, t, at:at + w] if isinstance(at, int) else u[:, t, bass.ds(at, w)]
                    sc_e.copy(dst, G[j * 2 + t][:, 0:w]).then_inc(st["taken"], 1)

            def project_in(name, turn_name, count, w, stride=1):
                st = proj[name]
                high(name, 0, 0, KT * w, stride)
                if stride == 1:
                    high(name, 0, 1, KT * w, stride)
                turn_act(sc_e, turn_name)
                if stride == 2:
                    high(name, 0, 1, KT * w, stride)
                take_chunk(name, st, 0, 0, w)
                if count > 4:
                    with sc_e.Fori(1, count // 2) as q:
                        high(name, q, 0, KT * w, stride)
                        take_chunk(name, st, q - 1, 1, w)
                        high(name, q, 1, KT * w, stride)
                        take_chunk(name, st, q, 0, w)
                else:
                    for q in range(1, count // 2):
                        high(name, q, 0, KT * w, stride)
                        take_chunk(name, st, q - 1, 1, w)
                        high(name, q, 1, KT * w, stride)
                        take_chunk(name, st, q, 0, w)
                take_chunk(name, st, count // 2 - 1, 1, w)

            def project_out(i, name, att_last):
                turn_act(sc_e, f"o{i}")
                sc_e.wait_ge(att["scores"], att_base[att_last] + len(att_jobs[att_last]))
                high(name, 0, 1, KT * OUT_W)
                high(name, 1, 0, KT * OUT_W)
                high(name, 1, 1, KT * OUT_W)

            def take_wide(name, st, at, w):
                for t in range(NT):
                    for half in range(2):
                        n = 2 * t + half
                        if n < 3:
                            sc_e.wait_ge(st["full"], n + 1)
                        else:
                            sc_e.wait_ge(used, split0[name] + 1)
                        sc_e.copy(u[:, t, at + half * w:at + (half + 1) * w], G[n][:, 0:w]).then_inc(st["taken"], 1)

            def ffn_act(name, turn_name, st):
                n0, k0 = first[name], split0[name]
                gu, dn = slice(0, 2 * KT * P), slice(2 * KT * P, 3 * KT * P)

                def high_gu(q, b, peeled=False):
                    sc_e.wait_ge(landed[b], q * 16 + 16 * (n0 // 2 + 1))
                    if peeled:
                        sc_e.wait_ge(used, k0 + b - 1)
                    else:
                        sc_e.wait_ge(st["gu_full"], q * 2 + (b - 1))
                    sc_e.copy(whi[b][:, gu], ring[:, b, gu]).then_inc(st["gu_hi"], 1)

                def high_dn(q, b):
                    sc_e.wait_ge(used, q * 2 + (k0 + b - 1))
                    sc_e.copy(whi[b][:, dn], ring[:, b, dn]).then_inc(st["dn_hi"], 1)

                def silu(q, b):
                    sc_e.wait_ge(st["gu_full"], q * 2 + b + 1)
                    sc_e.activation(sil[:, b, :], S[b][:, 0:T], ACT.Silu).then_inc(st["silu_done"], 1)

                def high_act(q, b):
                    sc_e.wait_ge(st["hidden"], q * 2 + b + 1)
                    sc_e.copy(acth[:, b, :], act[:, b, :]).then_inc(st["high"], 1)

                high_gu(0, 0, True)
                high_dn(0, 0)
                high_gu(0, 1, True)
                high_dn(0, 1)
                turn_act(sc_e, turn_name)
                silu(0, 0)
                high_act(0, 0)
                with sc_e.Fori(1, FF_STEPS // 2) as q:
                    high_gu(q, 0)
                    silu(q - 1, 1)
                    high_act(q - 1, 1)
                    high_dn(q, 0)
                    high_gu(q, 1)
                    silu(q, 0)
                    high_act(q, 0)
                    high_dn(q, 1)
                silu(FF_STEPS // 2 - 1, 1)
                high_act(FF_STEPS // 2 - 1, 1)

            project_in("nsa_in", "h0", NSA_C, NSA_W, stride=2)
            sc_e.wait_ge(proj["nsa_in"]["taken"], 2 * NSA_C)
            sc_e.activation(gate[:], u[:, :, 2816:2864], ACT.Exp, scale=-1.0).then_inc(nsa_s["gates_exp"], 1)
            sc_e.activation(u[:, :, 1792:2816], u[:, :, 1792:2816], ACT.Silu).then_inc(nsa_s["silu"], 1)
            turn_act(sc_e, "nsa_plain")
            sc_e.wait_ge(nsa_s["pos_turned"], 1)
            sc_e.copy(peT[:], TB[0][:, 0:32].rearrange("p (v c) -> p v c", v=2)).then_inc(nsa_s["pos_taken"], 1)
            turn_act(sc_e, "nsa_kc")
            for v in range(2):
                sc_e.wait_ge(nsa_s["hidden"], 2 * v + 2)
                sc_e.activation(hidr[:, v, :], G[v][0:2 * NCMP, 0:256], ACT.Silu).then_inc(nsa_s["hidden_act"], 1)
            turn_act(sc_e, "nsa_rot")
            sc_e.wait_ge(nsa_s["hid_turned"], 1)
            sc_e.copy(hid[:], TB[0][:, 0:8 * NCMP].rearrange("p (v m n) -> p v m n", v=2, m=2)).then_inc(nsa_s["hid_taken"], 1)
            sc_e.wait_ge(nsa_s["cmp_sub"], 1)
            sc_e.activation(sc[:], sc[:], ACT.Exp).then_inc(nsa_s["cmp_exp"], 1)
            sc_e.wait_ge(nsa_s["cmp_turned"], 1)
            sc_e.copy(pcT[:], TB[0][0:8 * NCMP, :].rearrange("p (b c) -> p b c", b=4)).then_inc(nsa_s["cmp_taken"], 1)
            high("nsa_out", 0, 0, KT * OUT_W)
            att_act(sc_e, "nsa")
            project_out(0, "nsa_out", "nsa")

            project_in("dil_in", "h1", DIL_C, DIL_W)
            sc_e.wait_ge(proj["dil_in"]["taken"], 2 * DIL_C)
            sc_e.activation(u[:, :, 3 * D:4 * D], u[:, :, 3 * D:4 * D], ACT.Silu).then_inc(dil_s["silu"], 1)
            turn_act(sc_e, "dil_rot")
            high("dil_out", 0, 0, KT * OUT_W)
            att_act(sc_e, "dil")
            for k, (src, func) in enumerate(((0, ACT.Ln), (3, ACT.Exp), (4, ACT.Ln), (5, ACT.Exp))):
                sc_e.wait_ge(dil_s["lse_in"], k + 1)
                v = {0: lse[:, 0, :], 3: lse[:, 3, :], 4: glse[:, 4, 0:6], 5: glse[:, 5, 0:6]}[src]
                sc_e.activation(v, v, func).then_inc(dil_s["lse_out"], 1)
            project_out(1, "dil_out", "dil")

            project_in("ab_in", "x0", AB_C, AB_W)
            high("uq", 0, 0, 3 * 768)
            turn_act(sc_e, "ab_c")
            high("ukv", 0, 0, 2 * 1024)
            take_wide("uq", proj["uq"], 1536, 384)
            take_wide("ukv", proj["ukv"], 2560, 512)
            sc_e.wait_ge(proj["ukv"]["taken"], 4)
            for t in range(NT):
                sc_e.copy(qcat[:, t, :].rearrange("p (h d) -> p h d", h=8)[:, :, 0:DH],
                         u[:, t, 1536:2304].rearrange("p (h d) -> p h d", h=8)[:, :, 0:DH]).then_inc(ab_s["nope"], 1)
                sc_e.copy(kcat[:, t, :].rearrange("p (h d) -> p h d", h=8)[:, :, 0:DH],
                         u[:, t, 2560:3584].rearrange("p (h d) -> p h d", h=8)[:, :, 0:DH]).then_inc(ab_s["nope"], 1)
            turn_act(sc_e, "ab_rot")
            high("ab_out", 0, 0, KT * OUT_W)
            att_act(sc_e, "mla")
            sc_e.wait_ge(att["outs"], att_base["mla"] + 8)
            att_act(sc_e, "swa", sink=True)
            project_out(2, "ab_out", "swa")
            ffn_act("ffn0", "f0", ffn[0])

            project_in("cd_in", "x1", CD_C, CD_W)
            sc_e.wait_ge(cd_s["f_in"], 1)
            sc_e.activation(fox[:, 1, :], fox[:, 1, :], ACT.Exp, scale=-1.0).then_inc(cd_s["f_exp"], 1)
            sc_e.wait_ge(cd_s["f_exp"], 1)
            sc_e.activation(fox[:, 1, :], fox[:, 1, :], ACT.Ln, bias=1.0).then_inc(cd_s["f_ln"], 1)
            turn_act(sc_e, "cd_rot")
            high("cd_out", 0, 0, KT * OUT_W)
            att_act(sc_e, "fox")
            sc_e.wait_ge(att["outs"], att_base["fox"] + 8)
            att_act(sc_e, "ck")
            project_out(3, "cd_out", "ck")
            ffn_act("ffn1", "f1", ffn[1])

        @block.vector
        def _(dve):
            tl = Tally(dve, dve_step)
            done = tl.done
            TT, STT, TS = dve.tensor_tensor, dve.scalar_tensor_tensor, dve.tensor_scalar

            def note(signal):
                done(dve.tensor_copy(scm[:, 0:1], mv[:, 0, 0:1]), signal)

            def ada_sum(layer, raw, m, k0):
                w = raw[:, 0:KT * ADA_W].rearrange("p (k w) -> p k w", k=KT)
                part = acc[:, m % 2, :]
                done(TS(part, w[:, k0, :], csil[:, k0:k0 + 1], None, ALU.mult))
                for k in range(k0 + 1, KT):
                    done(STT(part, w[:, k, :], csil[:, k:k + 1], part, ALU.mult, ALU.add), ada[layer]["summed"] if k == KT - 1 else None)

            def ada_take(layer, m, parity, mod):
                dve.wait_ge(ada[layer]["full"], m + 1)
                at = m * ADA_W
                dst = mod[:, at:at + ADA_W] if isinstance(at, int) else mod[:, bass.ds(at, ADA_W)]
                done(TT(dst, dst, S[parity][:, 0:ADA_W], ALU.add), ada[layer]["taken"])

            def low(name, q, j, cols, stride=1):
                n, k = first[name] + j, split0[name] + j
                dve.wait_ge(hi_done, q * 2 + (part0[name] + j + 1))
                raw = ring[:, n % 2 if stride == 1 else 0, 0:cols]
                TT(wlo[k % 2][:, 0:cols], raw, whi[k % 2][:, 0:cols].bitcast(F32), ALU.subtract).then_inc(lo_done, 1)

            def moments(src, t, pieces, layer_norm, eps):
                for c, piece in enumerate(src):
                    done(dve.bn_stats(bstat[:, t, c, :], piece))
                done(dve.bn_aggr(mv[:, t, :], bstat[:, t, 0:pieces, :]))
                v, mean = var[:, t:t + 1], mv[:, t, 0:1]
                if layer_norm:
                    done(TS(v, mv[:, t, 1:2], eps, None, ALU.add), norm["var"])
                else:
                    done(STT(v, mean, mean, mv[:, t, 1:2], ALU.mult, ALU.add))
                    done(TS(v, v, eps, None, ALU.add), norm["var"])

            vec_n = [0]

            def next_vec():
                v = vec_n[0]
                vec_n[0] += 1
                dve.wait_ge(vec_loaded[v % 2], 16 * (v // 2 + 1))
                return vec[:, v % 2, :]

            def scale_gain(mod):
                scale, g = mod[:, D:2 * D], next_vec()
                done(STT(scale, scale, 1.0, g, ALU.add, ALU.mult), vec_used)

            def ada_norm(i, mod, t):
                done(TT(tok[:, t, :], x[:, t, :], mod[:, D:2 * D], ALU.mult))
                dve.wait_ge(norm["rstd"], 2 * i + t + 1)
                done(STT(tok[:, t, :], tok[:, t, :], rstd[:, t:t + 1], mod[:, 0:D], ALU.mult, ALU.add), norm["ready"])

            def layer_norm(i, g, b, pieces, t):
                moments([], t, pieces, True, EPS_LN)
                done(STT(x[:, t, :], x[:, t, :], mv[:, t, 0:1], g, ALU.subtract, ALU.mult))
                dve.wait_ge(norm["rstd"], 2 * i + t + 1)
                done(STT(x[:, t, :], x[:, t, :], rstd[:, t:t + 1], b, ALU.mult, ALU.add), norm["ready"])

            def set_head(col):
                def take(j, o, r):
                    done(TT(tok[:, :, (col + j) * DH:(col + j + 1) * DH], o, over(r, 2, DH), ALU.mult), att["outs"])
                return take

            def project_out(i, name, gatev, between, finish):
                turn_low(dve, f"o{i}")
                low(name, 0, 1, KT * OUT_W)
                for m in range(OUT_C):
                    for t in range(NT):
                        if t == 0:
                            dve.wait_ge(outp["full"], OUT_C * i + m + 1)
                        else:
                            dve.wait_ge(used, split0[name] + m + 1)
                        cols = slice(m * OUT_W, (m + 1) * OUT_W)
                        y, part = G[(m % 2) * 2 + t][:, 0:OUT_W], x[:, t, cols]
                        if gatev is None:
                            done(STT(part, part, ALPHA, y, ALU.mult, ALU.add), outp["taken"])
                        else:
                            done(TT(tmp[:, t, 0:OUT_W], y, gatev[:, cols], ALU.mult), outp["taken"])
                            done(TT(part, part, tmp[:, t, 0:OUT_W], ALU.add))
                        done(dve.bn_stats(bstat[:, t, m, :], part))
                        if m == OUT_C - 1:
                            finish(t)
                    if m < OUT_C - 2:
                        low(name, 1, m, KT * OUT_W)
                    elif m == OUT_C - 2:
                        between()

            gu, dn = slice(0, 2 * KT * P), slice(2 * KT * P, 3 * KT * P)

            def low_ffn(st, q, b, part, what):
                dve.wait_ge(st[what + "_hi"], q * 2 + b + 1)
                TT(wlo[b][:, part], ring[:, b, part], whi[b][:, part].bitcast(F32), ALU.subtract).then_inc(st[what + "_lo"], 1)

            def ffn_dve(i, name, turn_name):
                st = ffn[i]
                turn_low(dve, turn_name)
                low_ffn(st, 0, 1, gu, "gu")
                low_ffn(st, 0, 1, dn, "dn")

                def hidden(q, b):
                    dve.wait_ge(st["silu_done"], q * 2 + b + 1)
                    TT(act[:, b, :], S[b][:, T:2 * T], sil[:, b, :], ALU.mult).then_inc(st["hidden"], 1)
                    dve.wait_ge(st["high"], q * 2 + b + 1)
                    TT(actl[:, b, :], act[:, b, :], acth[:, b, :].bitcast(F32), ALU.subtract).then_inc(st["act_ready"], 1)

                hidden(0, 0)
                with dve.Fori(1, FF_STEPS // 2) as q:
                    low_ffn(st, q, 0, gu, "gu")
                    hidden(q - 1, 1)
                    low_ffn(st, q, 0, dn, "dn")
                    low_ffn(st, q, 1, gu, "gu")
                    hidden(q, 0)
                    low_ffn(st, q, 1, dn, "dn")
                hidden(FF_STEPS // 2 - 1, 1)

            def ffn_out(name, finish):
                dve.wait_ge(used, split0[name] + FF_STEPS)
                for t in range(NT):
                    for half in range(2):
                        part = x[:, t, half * 512:(half + 1) * 512]
                        done(STT(part, part, ALPHA, G[2 * t + half][:], ALU.mult, ALU.add))
                        done(dve.bn_stats(bstat[:, t, half, :], part))
                    finish(t)

            def attention(name, bias_of, scale, take, sink=None):
                att_dve(dve, tl, name, bias_of, scale, take, sink)

            dve.wait_ge(consts_set, 3)
            dve.wait_ge(c_ready, 1)
            for k in range(ADA_PE):
                done(TS(cb[:, k, :], ones[:], csil[:, k:k + 1], None, ALU.mult), cb_ready)
            dve.wait_ge(mod0_loaded, 16)
            for m in range(ADA_EARLY):
                wait_landed(dve, first["ada0"] + m)
                ada_sum(0, ring[:, m % 2, :], m, ADA_PE)
                if m == 0:
                    dve.wait_ge(x_loaded, 16)
                    for t in range(NT):
                        moments([x[:, t, c * 512:(c + 1) * 512] for c in range(2)], t, 2, False, EPS_RMS)
                else:
                    ada_take(0, m - 1, (m - 1) % 2, mod0)
            ada_take(0, ADA_EARLY - 1, (ADA_EARLY - 1) % 2, mod0)
            scale_gain(mod0)
            for t in range(NT):
                ada_norm(0, mod0, t)
            low("nsa_in", 0, 0, KT * NSA_W, 2)
            turn_low(dve, "h0")

            dve.wait_ge(mod1_loaded, 16)
            n1 = first["nsa_in"] + 1
            for m in range(2):
                if m == 1:
                    low("nsa_in", 0, m, KT * NSA_W, 2)
                wait_landed(dve, n1, m)
                ada_sum(1, ring[:, 1, :], m, 0)
            ada_take(1, 0, 0, mod1)
            with dve.Fori(1, NSA_C // 2) as i:
                tl.enter(i - 1, {dve_step: 2 * (KT - 1), ada[1]["summed"]: 2, ada[1]["taken"]: 2})
                for j in range(2):
                    low("nsa_in", i, j, KT * NSA_W, 2)
                    dve.wait_ge(landed[1], i * 32 + 16 * (n1 // 2 + j + 1))
                    ada_sum(1, ring[:, 1, :], j, 0)
                    ada_take(1, i * 2 + (j - 1), 1 - j, mod1)
            tl.leave(ADA_C // 2 - 1)
            ada_take(1, ADA_C - 1, 1, mod1)
            for m in range(ADA_EARLY, ADA_C):
                n = first["ada0_gate"] + m - ADA_EARLY
                wait_landed(dve, n)
                ada_sum(0, ring[:, n % 2, :], m, ADA_PE)
                ada_take(0, m, m % 2, mod0)

            dve.wait_ge(proj["nsa_in"]["taken"], 2 * NSA_C)
            dve.wait_ge(tab_loaded, 16)
            dve.wait_ge(small_loaded, 16 * SMALL_LOADS)
            for t in range(NT):
                ins = dve.tensor_copy(kcdup[:, t, :].rearrange("p (n two d) -> p n two d", n=4, two=2),
                                      over(u[:, t, 1024:1280].rearrange("p (n d) -> p n d", n=4), 2, 2))
                done(ins, nsa_s["kc_ready"] if t == 1 else None)
            flat = tmp[:].rearrange("p a b -> p (a b)")
            for t in range(NT):
                kd = kdup[:, t, :].rearrange("p (n two d) -> p n two d", n=4, two=2)
                for lo, n in ((1280, 0), (1536, 2)):
                    rotate(tl, kd[:, n:n + 2, 0, :], u[:, t, lo:lo + P].rearrange("p (g d) -> p g d", g=2), cos, sin, 2, HALF, t, flat)
                done(dve.tensor_copy(kd[:, :, 1, :], kd[:, :, 0, :]), nsa_s["keys_ready"])
            dve.wait_ge(nsa_s["gates_exp"], 1)
            done(TS(gate[:], gate[:], 1.0, None, ALU.add))
            done(dve.reciprocal(gate[:], gate[:]))
            dve.wait_ge(nsa_s["rot_ready"], NT)
            dve.wait_ge(*turned_all("nsa_kc"))
            for v in range(2):
                for g in range(2):
                    for far in range(2):
                        src = a2[:, v, g, 16 * far:16 * far + 240].rearrange("p (n b two) -> p b n two", two=2, b=8)[:, :, :, 0]
                        done(TT(blkT[:, v, far * 8:far * 8 + 8, g, :], src, over(peT[:, v, far * 8:far * 8 + 8], 2, NCMP), ALU.add), nsa_s["blocks"])
            scale_gain(mod1)
            done(TS(negsink[:], sinks, -1.0, None, ALU.mult))
            dve.wait_ge(nsa_s["hid_taken"], 1)
            for g in range(2):
                for mh in range(2):
                    done(dve.tensor_copy(hid8[:, g, mh, :].rearrange("p (r n) -> p r n", r=8),
                                         over(hid[:, 1, mh, g * NCMP:(g + 1) * NCMP], 1, 8)), nsa_s["hid8"])
            dve.wait_ge(nsa_s["kv_full"], 1)
            for g in range(2):
                for odd in range(2):
                    rows = slice(odd * DH, (odd + 1) * DH)
                    done(dve.tensor_copy(kc2[rows, g, odd * NCMP:(odd + 1) * NCMP], S[0][rows, g * NCMP:(g + 1) * NCMP]), nsa_s["kcT_ready"])
            dve.wait_ge(nsa_s["kv_full"], 2)
            for g in range(2):
                done(TT(vbd[:, g, :].rearrange("p (r d) -> p r d", r=8), over(S[1][0:8 * NCMP, g * DH:(g + 1) * DH], 1, 8),
                        bdmask[:].rearrange("p (r d) -> p r d", r=8), ALU.mult), nsa_s["vbd"])
            dve.wait_ge(nsa_s["scored"], 1)
            for t in range(NT):
                for g in range(2):
                    at = t * H + g * 8
                    done(STT(sc[:, at:at + 8, :].rearrange("p (r two) n -> p r (two n)", two=2),
                             G[2 * t + g][:].rearrange("p (r w) -> p r w", r=4)[:, :, 0:2 * NCMP], SCALE,
                             over(cneg[:, t, :], 1, 4), ALU.mult, ALU.add))
            done(dve.tensor_reduce(scm[:], sc[:], AX.X, ALU.max))
            done(TT(sc[:], sc[:], over(scm[:], 2, NCMP), ALU.subtract), nsa_s["cmp_sub"])
            dve.wait_ge(nsa_s["cmp_exp"], 1)
            for t in range(NT):
                part = sc[:, t * H:(t + 1) * H, :]
                done(TT(part, part, over(cone[:, t, :], 1, H), ALU.mult))
            done(dve.tensor_reduce(scm[:], sc[:], AX.X, ALU.add))
            done(TS(scm[:], scm[:], 1.0, None, ALU.max))
            done(dve.reciprocal(scm[:], scm[:]))
            done(TT(sc[:], sc[:], over(scm[:], 2, NCMP), ALU.mult), nsa_s["cmp_prob"])
            gates = gate[:].rearrange("p t (h b) -> p t h b", b=3)
            dve.wait_ge(*turned_all("nsa_rot"))
            for b in range(4):
                t, g = b // 2, b % 2
                dve.wait_ge(nsa_s["cmp_out"], b + 1)
                done(TT(tok[:, t, g * 512:(g + 1) * 512].rearrange("p (h d) -> p h d", h=8), G[b][:].rearrange("p (h d) -> p h d", h=8),
                        over(gates[:, t, g * 8:(g + 1) * 8, 0], 2, DH), ALU.mult), nsa_s["cmp_summed"])
            low("nsa_out", 0, 0, KT * OUT_W)

            def add_gated(j, o, r):
                h, branch = j % H, 1 + j // H
                done(TT(r, r, gates[:, :, h, branch], ALU.mult))
                for t in range(NT):
                    dst = tok[:, t, h * DH:(h + 1) * DH]
                    ins = STT(dst, o[:, t, :], r[:, t:t + 1], dst, ALU.mult, ALU.add)
                    tl.mark(ins, tl.own if t == 0 else att["outs"])

            attention("nsa", lambda i: table("causal"), SCALE, add_gated)
            dve.wait_ge(att["outs"], att_base["nsa"] + 2 * H)
            dve.wait_ge(nsa_s["silu"], 1)
            done(TT(tok[:], tok[:], u[:, :, 1792:2816], ALU.mult), out_ready)

            def norm_1(t):
                moments([], t, 4, False, EPS_RMS)
                ada_norm(1, mod1, t)

            project_out(0, "nsa_out", mod0[:, 2 * D:3 * D], lambda: low("dil_in", 0, 0, KT * DIL_W), norm_1)

            turn_low(dve, "h1")
            low("dil_in", 0, 1, KT * DIL_W)
            with dve.Fori(1, DIL_C // 2) as i:
                for j in range(2):
                    low("dil_in", i, j, KT * DIL_W)
            low("dil_out", 0, 0, KT * OUT_W)
            groups = (6, 5, 5)
            offs = (0, 6, 11, 16)
            group = [g for g, n in enumerate(groups) for _ in range(n)]
            dve.wait_ge(*turned_all("dil_rot"))
            attention("dil", lambda i: table(f"dil{group[i]}"), SCALE, set_head(0))
            done(dve.tensor_copy(lse[:, 0, :].rearrange("p (h t) -> p h t", t=NT), den[:, 0:H, :]), dil_s["lse_in"])
            dve.wait_ge(dil_s["lse_out"], 1)
            done(TT(lse[:, 1, :], lse[:, 0, :], negmax[:].rearrange("p h t -> p (h t)"), ALU.subtract))
            l1 = lse[:, 1, :].rearrange("p (h t) -> p t h", t=NT)
            l3 = lse[:, 3, :].rearrange("p (h t) -> p t h", t=NT)
            gl = [glse[:, k, 0:6].rearrange("p (t g) -> p t g", t=NT) for k in range(8)]
            for g in range(3):
                hs = slice(offs[g], offs[g + 1])
                done(dve.tensor_reduce(gl[0][:, :, g], l1[:, :, hs], AX.X, ALU.max))
                done(TT(l3[:, :, hs], l1[:, :, hs], over(gl[0][:, :, g], 2, groups[g]), ALU.subtract), dil_s["lse_in"] if g == 2 else None)
            dve.wait_ge(dil_s["lse_out"], 2)
            for g in range(3):
                hs = slice(offs[g], offs[g + 1])
                done(dve.tensor_reduce(gl[4][:, :, g], l3[:, :, hs], AX.X, ALU.add), dil_s["lse_in"] if g == 2 else None)
            dve.wait_ge(dil_s["lse_out"], 3)
            for g in range(3):
                done(STT(gl[1][:, :, g], gl[4][:, :, g], -float(np.log(groups[g])), gl[0][:, :, g], ALU.add, ALU.add))
            done(dve.tensor_reduce(glse[:, 6, 0:NT], gl[1], AX.X, ALU.max))
            done(TT(gl[5], gl[1], over(glse[:, 6, 0:NT], 2, 3), ALU.subtract), dil_s["lse_in"])
            dve.wait_ge(dil_s["lse_out"], 4)
            done(dve.tensor_reduce(glse[:, 6, 0:NT], gl[5], AX.X, ALU.add))
            done(dve.reciprocal(glse[:, 6, 0:NT], glse[:, 6, 0:NT]))
            done(TS(glse[:, 6, 0:NT], glse[:, 6, 0:NT], 3.0, None, ALU.mult))
            done(TT(gl[5], gl[5], over(glse[:, 6, 0:NT], 2, 3), ALU.mult))
            dve.wait_ge(dil_s["silu"], 1)
            for g in range(3):
                lo, hi = offs[g] * DH, offs[g + 1] * DH
                for t in range(NT):
                    done(STT(tok[:, t, lo:hi], tok[:, t, lo:hi], gl[5][:, t, g:g + 1], u[:, t, 3 * D + lo:3 * D + hi], ALU.mult, ALU.mult),
                         out_ready if (g, t) == (2, 1) else None)
            g_final = next_vec()

            def norm_2(t):
                moments([], t, 4, False, EPS_RMS)
                dve.wait_ge(norm["rstd"], 2 * 2 + t + 1)
                done(STT(x[:, t, :], x[:, t, :], rstd[:, t:t + 1], g_final, ALU.mult, ALU.mult), norm["ready"])

            project_out(1, "dil_out", mod1[:, 2 * D:3 * D], lambda: low("ab_in", 0, 0, KT * AB_W), norm_2)
            note(mod1_used)
            note(vec_used)

            turn_low(dve, "x0")
            low("ab_in", 0, 1, KT * AB_W)
            low("ab_in", 1, 0, KT * AB_W)
            low("ab_in", 1, 1, KT * AB_W)
            dve.wait_ge(proj["ab_in"]["taken"], 2 * 2)
            latents = ((0, 384, q_gain), (384, 256, kv_gain))
            for i, (lo, w, gain) in enumerate(latents):
                for t in range(NT):
                    moments([u[:, t, lo:lo + w]], t, 1, False, EPS_RMS)
                for t in range(NT):
                    dve.wait_ge(norm["rstd"], 2 * (3 + i) + t + 1)
                    ins = STT(tok[:, t, lo:lo + w], u[:, t, lo:lo + w], rstd[:, t:t + 1], gain, ALU.mult, ALU.mult)
                    done(ins, ab_s["c_ready"] if (i, t) == (1, 1) else None)
            for t in range(NT):
                rotate(tl, kr[:, t, :].rearrange("p (n d) -> p n d", n=1), u[:, t, 640:672].rearrange("p (n d) -> p n d", n=1),
                       cos_m, sin_m, 1, 16, t, flat)
                done(dve.tensor_copy(kcat[:, t, :].rearrange("p (h d) -> p h d", h=8)[:, :, DH:96], over(kr[:, t, :], 1, 8)))
            dve.wait_ge(proj["ab_in"]["taken"], 2 * AB_C)
            for t in range(NT):
                done(dve.tensor_copy(kswa[:, t, :].rearrange("p (g two d) -> p g two d", g=2, two=2),
                                     over(u[:, t, 1184:1312].rearrange("p (g d) -> p g d", g=2), 2, 2)))
            low("uq", 0, 0, 3 * 768)
            turn_low(dve, "ab_c")
            low("ukv", 0, 0, 2 * 1024)
            dve.wait_ge(proj["uq"]["taken"], 4)
            for t in range(NT):
                rotate(tl, qcat[:, t, :].rearrange("p (h d) -> p h d", h=8)[:, :, DH:96],
                       u[:, t, 1536:2304].rearrange("p (h d) -> p h d", h=8)[:, :, DH:96], cos_m, sin_m, 8, 16, t, flat,
                       ab_s["rot_ready"] if t == 1 else None)
            low("ab_out", 0, 0, KT * OUT_W)
            dve.wait_ge(*turned_all("ab_rot"))
            attention("mla", lambda i: table("chunk"), MLA_SCALE, set_head(0))
            dve.wait_ge(swa_loaded, 16)
            attention("swa", lambda i: bias8[:, i * SW:(i + 1) * SW], SCALE, set_head(8), sink=lambda i: negsink[:, i:i + 1])
            note(out_ready)
            note(swa_used)
            g5, b5 = next_vec(), next_vec()

            def before_ffn(i):
                def between():
                    low_ffn(ffn[i], 0, 0, gu, "gu")
                    low_ffn(ffn[i], 0, 0, dn, "dn")
                return between

            project_out(2, "ab_out", None, before_ffn(0), lambda t: layer_norm(5, g5, b5, 4, t))
            note(vec_used)
            note(vec_used)
            ffn_dve(0, "ffn0", "f0")
            low("cd_in", 0, 0, KT * CD_W)
            g6, b6 = next_vec(), next_vec()
            ffn_out("ffn0", lambda t: layer_norm(6, g6, b6, 2, t))
            note(vec_used)
            note(vec_used)

            turn_low(dve, "x1")
            low("cd_in", 0, 1, KT * CD_W)
            with dve.Fori(1, CD_C // 2) as i:
                for j in range(2):
                    low("cd_in", i, j, KT * CD_W)
            dve.wait_ge(proj["cd_in"]["taken"], 2 * 6)
            f = [fox[:, k, :].rearrange("p (t h) -> p t h", t=NT) for k in range(6)]
            done(TT(f[0], u[:, :, 1536:1544], over(forget, 1, NT), ALU.add))
            done(STT(f[1], f[0], -1.0, f[0], ALU.mult, ALU.max), cd_s["f_in"])
            done(TS(f[2], f[0], 0.0, None, ALU.min))
            qa = [qaug[:, t, :].rearrange("p (h d) -> p h d", h=8) for t in range(NT)]
            ka = [kaug[:, t, :].rearrange("p (h d) -> p h d", h=8) for t in range(NT)]
            for t in range(NT):
                done(dve.tensor_copy(qa[t][:, :, 0:DH], u[:, t, 0:512].rearrange("p (h d) -> p h d", h=8)))
                done(dve.tensor_copy(ka[t][:, :, 0:DH], u[:, t, 512:1024].rearrange("p (h d) -> p h d", h=8)))
                done(dve.memset(qa[t][:, :, DH + 1:DH + 2], 1.0))
                done(dve.memset(ka[t][:, :, DH:DH + 1], 1.0))
            for h in range(8):
                dve.wait_ge(cd_s["flipped"], h + 1)
                done(STT(bias8[:, h * SW:(h + 1) * SW], G[h % 4][:, 0:SW], 1.0 / SCALE, table("chunk"), ALU.mult, ALU.add), cd_s["bias_ready"])
            dve.wait_ge(cd_s["f_ln"], 1)
            done(TT(f[3], f[2], f[1], ALU.subtract), cd_s["f_ready"])
            dve.wait_ge(cd_s["cum"], 1)
            for t in range(NT):
                c = S[0][:, t * 8:(t + 1) * 8].unsqueeze(2)
                done(TS(qa[t][:, :, DH:DH + 1], c, 1.0 / SCALE, None, ALU.mult))
                done(TS(ka[t][:, :, DH + 1:DH + 2], c, -1.0 / SCALE, None, ALU.mult), cd_s["aug_ready"] if t == 1 else None)
            low("cd_out", 0, 0, KT * OUT_W)
            dve.wait_ge(*turned_all("cd_rot"))
            attention("fox", lambda i: table("causal"), SCALE, set_head(0))
            attention("ck", lambda i: bias8[:, i * SW:(i + 1) * SW], SCALE, set_head(8))
            note(out_ready)
            g7, b7 = next_vec(), next_vec()
            project_out(3, "cd_out", None, before_ffn(1), lambda t: layer_norm(7, g7, b7, 4, t))
            note(vec_used)
            note(vec_used)
            ffn_dve(1, "ffn1", "f1")
            g8, b8 = next_vec(), next_vec()
            ffn_out("ffn1", lambda t: layer_norm(8, g8, b8, 2, t))


def shape_tables():
    f = np.float32
    tab = np.zeros((P, TAB_W), f)

    def put(name, v):
        lo, hi = TAB[name]
        tab[:, lo:hi] = np.asarray(v, f).reshape(P, hi - lo)

    def by_token(v):
        return v.reshape(NT, P, -1).transpose(1, 0, 2)

    put("ident", np.eye(P))
    put("flip", np.eye(P)[::-1])
    put("tri", np.triu(np.ones((P, P))))
    for half, c, s, inv in ((HALF, "cos", "sin", f(10000.0) ** (-np.arange(HALF, dtype=f) / f(HALF))),
                            (16, "cos_m", "sin_m", f(10000.0) ** (-np.arange(0, 32, 2, dtype=f) / f(32)))):
        ang = np.arange(T, dtype=f)[:, None] * inv.astype(f)[None, :]
        put(c, by_token(np.cos(ang)))
        put(s, by_token(np.sin(ang)))
    q, k = np.arange(T)[:, None], np.arange(T)[None, :]

    def packed(m):
        return np.concatenate([m[0:P, 0:P], m[P:, 0:P], m[P:, P:]], axis=-1)

    def hidden(seen):
        return packed(np.where(seen, 0.0, -1e30))

    put("causal", hidden(k <= q))
    put("dil0", hidden((k <= q) & (q - k <= 128)))
    put("dil1", hidden((k <= q) & ((q - k) % 4 == 0)))
    put("dil2", hidden((k <= q) & ((q - k) % 16 == 0)))
    put("chunk", hidden(k // 64 <= q // 64))
    seen = (16 * np.arange(NCMP) + 31)[None, :] <= np.arange(T)[:, None]
    put("cneg", by_token(np.tile(np.where(seen, 0.0, -1e30), (1, 2))))
    put("cone", by_token(np.where(seen, 1.0, 0.0)))
    near = (k // 64 <= q // 64) & (k // 64 >= q // 64 - 2)
    slopes = np.exp2(-8.0 * np.arange(1, 9) / 8)
    swa = np.stack([packed(np.where(near, -s * np.abs(q - k) / SCALE, -1e30)) for s in slopes], axis=1).reshape(P, 8 * SW).astype(f)
    bd = np.kron(np.eye(8), np.ones((NCMP, DH))).astype(f)
    return {"tables": tab, "swa_bias": swa, "bdmask": bd}


def tiles(w, width):
    k, n = w.shape
    return np.ascontiguousarray(w.reshape(k // P, P, n // width, width).transpose(2, 1, 0, 3)).reshape(n // width, P, -1)


def ffn_steps(gate, up, down):
    return np.concatenate([tiles(gate, P), tiles(up, P), down.reshape(FF_STEPS, P, D)], axis=2)


def kernel(**inputs):
    import concourse.bacc as bacc
    from concourse.bass_utils import run_bass_kernel_spmd

    v = {k: np.asarray(w) for k, w in inputs.items()}
    rel = v["cd_rel_bias_2"][0]
    arrays = {
        "x": v["x"],
        "c": np.ascontiguousarray(v["c"].reshape(KT, P).T),
        "ada_w0": tiles(v["ada_w"][0], ADA_W), "ada_w1": tiles(v["ada_w"][1], ADA_W), "ada_b": v["ada_b"],
        "nsa_w_in": tiles(v["nsa_w_in"][0], NSA_W),
        "cmp_w1": np.stack([w[0].reshape(2, 8, P, 256).transpose(0, 2, 1, 3).reshape(2, P, 2048)
                            for w in (v["nsa_ck_w1"], v["nsa_cv_w1"])]).reshape(4, P, 2048),
        "cmp_w2": np.ascontiguousarray(np.stack([w[0].reshape(2, P, DH).transpose(1, 0, 2) for w in (v["nsa_ck_w2"], v["nsa_cv_w2"])], axis=1)),
        "pos": np.ascontiguousarray(np.stack([w[0].reshape(16, P) for w in (v["nsa_pe_k"], v["nsa_pe_v"])], axis=1)),
        "nsa_w_out": tiles(v["nsa_w_out"][0], OUT_W),
        "dil_w_in": tiles(v["dil_w_in"][0], DIL_W), "dil_w_out": tiles(v["dil_w_out"][0], OUT_W),
        "ab_w_in": tiles(v["ab_w_in_2"][0], AB_W), "ab_w_uq": tiles(v["ab_w_uq_2"][0], 768),
        "ab_w_ukv": tiles(v["ab_w_ukv_2"][0], 1024), "ab_w_out": tiles(v["ab_w_out_2"][0], OUT_W),
        "cd_w_in": tiles(v["cd_w_in_2"][0], CD_W), "cd_w_out": tiles(v["cd_w_out_2"][0], OUT_W),
        "ffn0": ffn_steps(v["ffn_w_gate_2"][0], v["ffn_w_up_2"][0], v["ffn_w_down_2"][0]),
        "ffn1": ffn_steps(v["ffn_w_gate_2"][1], v["ffn_w_up_2"][1], v["ffn_w_down_2"][1]),
        "vecs": np.stack([v["norm_g"][0], v["norm_g"][1], v["final_g"], v["ln1_g_2"][0], v["ln1_b_2"][0], v["ln2_g_2"][0],
                          v["ln2_b_2"][0], v["ln1_g_2"][1], v["ln1_b_2"][1], v["ln2_g_2"][1], v["ln2_b_2"][1]]),
        "q_norm": v["ab_q_norm_2"][0], "kv_norm": v["ab_kv_norm_2"][0], "sinks": v["ab_sinks_2"][0], "b_forget": v["cd_b_forget_2"][0],
        "rel_rev": np.pad(rel[318::-1].T, ((0, 0), (0, 512 - 319))),
        **shape_tables(),
    }
    arrays = {k: np.ascontiguousarray(w) for k, w in arrays.items()}
    nc = bacc.Bacc("TRN2", target_bir_lowering=False, num_devices=1)
    aps = {k: nc.dram_tensor(f"in_{k}", w.shape, mybir.dt.from_np(w.dtype), kind="ExternalInput").ap() for k, w in arrays.items()}
    out = nc.dram_tensor("out", v["x"].shape, F32, kind="ExternalOutput").ap()
    two_stacks(nc, aps, out)
    got = run_bass_kernel_spmd(nc, [{f"in_{k}": w for k, w in arrays.items()}], core_ids=[0])
    return got.results[0]["out"]
```

```python
from contextlib import ExitStack

import numpy as np

import concourse.bass as bass
from concourse import mybir

P = 128
D = 1024
T = 256
NT = T // P
KT = D // P
H = 16
DH = 64
HALF = DH // 2
SLOTS = 2
SLOT = 3072
ADA_C, ADA_W = 8, 384
ADA_EARLY = 6
ADA_PE = 4
NSA_C, NSA_W = 8, 358
DIL_C, DIL_W = 16, 256
AB_C, AB_W = 4, 360
CD_C, CD_W = 10, 308
OUT_C, OUT_W = 4, 256
LATE = 2 * ADA_C - ADA_EARLY
LATE_NSA = 8
NSA_Q = 768
FF_STEPS = 22
NCMP = 15
EPS_RMS = 1e-6
EPS_LN = 1e-5
ALPHA = 4.0 ** 0.25
SCALE = DH ** -0.5
MLA_SCALE = 96 ** -0.5
SW = 3 * P
FOXW = DH + 2

ALU = mybir.AluOpType
ACT = mybir.ActivationFunctionType
F32 = mybir.dt.float32
F32R = mybir.dt.float32r
AX = mybir.AxisListType

TAB = {}
_at = 0
for _name, _n in (("ident", P), ("flip", P), ("tri", P), ("cos", NT * HALF), ("sin", NT * HALF), ("cos_m", NT * 16),
                  ("sin_m", NT * 16), ("causal", SW), ("dil0", SW), ("dil1", SW), ("dil2", SW),
                  ("chunk", SW), ("cneg", NT * 2 * NCMP), ("cone", NT * NCMP)):
    TAB[_name] = (_at, _at + _n)
    _at += _n
TAB_W = _at

VECS = ("norm_g0", "norm_g1", "final_g", "ln1_g0", "ln1_b0", "ln2_g0", "ln2_b0", "ln1_g1", "ln1_b1", "ln2_g1", "ln2_b1")


class Tally:

    def __init__(self, eng, own):
        self.eng, self.own, self.n, self.turns = eng, own, {}, None

    def mark(self, ins, sem):
        ins.then_inc(sem, 1)
        self.n[sem.name] = self.n.get(sem.name, 0) + 1

    def done(self, ins, sem=None):
        sem = self.own if sem is None else sem
        self.mark(ins, sem)
        self.eng.wait_ge(sem, self.n[sem.name] + (0 if self.turns is None else self.turns * self.per[sem.name]))

    def enter(self, turns, per):
        self.turns, self.per = turns, {k.name: v for k, v in per.items()}

    def leave(self, times):
        for name, per in self.per.items():
            self.n[name] += per * (times - 1)
        self.turns = None


SMALL_LOADS = 9


class Signals:

    def __init__(self, ctx, nc, stage, names):
        self.s = {n: ctx.enter_context(nc.semaphore(f"{stage}_{n}")) for n in names.split()}

    def __getitem__(self, n):
        return self.s[n]


def over(ap, axis, n):
    a = ap.unsqueeze(axis)
    shape = list(a.shape)
    shape[axis] = n
    return a.broadcast_to(shape)


def two_stacks(nc, a, out):
    with ExitStack() as ctx:
        def sem(name):
            return ctx.enter_context(nc.semaphore(name))

        def stage(name, names):
            return Signals(ctx, nc, name, names)

        at_byte = [-(-nc.sbuf_base // 32) * 32]
        place = {}

        def sb(name, shape, dt=F32, over=None, skip=0):
            size = -(-4 * int(np.prod(shape[1:])) // 32) * 32
            if over is None:
                place[name] = at_byte[0]
                at_byte[0] += size
                assert at_byte[0] <= nc.sbuf_top, (name, at_byte[0], nc.sbuf_top)
            else:
                place[name] = place[over] + skip
            return nc.alloc_sbuf_tensor_at(name, list(shape), dt, offset=place[name])

        x = sb("x", [P, NT, D])
        tok = sb("tok", [P, NT, D])
        rotk = sb("rotk", [P, NT, D])
        hTh = sb("hTh", [P, KT, T], F32R)
        u = sb("u", [P, NT, 4 * D])
        qT = sb("qT", [P, 8, T])
        kT = sb("kT", [P, 8, T])
        q2T = sb("q2T", [P, 8, T])
        ring = sb("ring", [P, SLOTS, SLOT])
        whi = [sb("whi0", [P, SLOT], F32R), sb("whi1", [P, SLOT], F32R, over="qT")]
        wlo = [sb("wlo0", [P, SLOT], F32R), sb("wlo1", [P, SLOT], F32R, over="qT", skip=4 * SLOT)]
        scr = sb("scr", [P, 3, SW + 2])
        prob = sb("prob", [P, 3, SW + 2])
        probT = sb("probT", [P, 3, SW])
        hTl = sb("hTl", [P, KT, T], F32R, over="scr")
        acc = sb("acc", [P, 2, ADA_W], over="probT")
        hidr = sb("hidr", [2 * NCMP, 2, 256], over="probT")
        sil = sb("sil", [P, 2, T], over="u")
        act = sb("act", [P, 2, T], over="u", skip=4 * 2 * T)
        acth = sb("acth", [P, 2, T], F32R, over="u", skip=8 * 2 * T)
        actl = sb("actl", [P, 2, T], F32R, over="u", skip=12 * 2 * T)
        tab = sb("tab", [P, TAB_W])
        mod0 = sb("mod0", [P, 3 * D])
        bias8 = sb("bias8", [P, 8 * SW])
        vec = sb("vec", [P, 2, D])
        small = sb("small", [P, 384 + 256 + 8 + 8 + KT])
        cb = sb("cb", [P, ADA_PE, P], over="rotk")
        tmp = sb("tmp", [P, 2, 512])
        negmax = sb("negmax", [P, H, 2])
        den = sb("den", [P, 2 * H, 2])
        rden = sb("rden", [P, 2 * H, 2])
        gate = sb("gate", [P, NT, 48])
        bstat = sb("bstat", [P, NT, 4, 6])
        mv = sb("mv", [P, NT, 2])
        kr = sb("kr", [P, NT, 32])
        var = sb("var", [P, NT])
        rstd = sb("rstd", [P, NT])
        mhalf = sb("mhalf", [P, NT])
        ones = sb("ones", [P, P])
        peT = sb("peT", [P, 2, 16])
        pe_rows = sb("pe_rows", [16, 2, P])
        hid = sb("hid", [P, 2, 2, 2 * NCMP])
        hid8 = sb("hid8", [P, 2, 2, 8 * NCMP], over="tmp")
        w2 = sb("w2", [P, 2, 3 * DH])
        kc2 = sb("kc2", [P, 2, P])
        bdmask = sb("bdmask", [8 * NCMP, 8 * DH])
        scm = sb("scm", [P, NT * H])
        lse = sb("lse", [P, 1, NT * H], over="tmp")
        glse = sb("glse", [P, 8, NT * 3])
        fox = sb("fox", [P, 6, NT * 8])
        negsink = sb("negsink", [P, 8])

        G = [ctx.enter_context(nc.psum_tensor(f"G{i}", [P, 512], F32)) for i in range(4)]
        S = [ctx.enter_context(nc.psum_tensor(f"S{i}", [P, 512], F32)) for i in range(2)]
        TB = [ctx.enter_context(nc.psum_tensor(f"T{i}", [P, 512], F32)) for i in range(2)]

        def table(name):
            lo, hi = TAB[name]
            return tab[:, lo:hi]

        ident = table("ident")
        cos = table("cos").rearrange("p (t d) -> p t d", t=NT)
        sin = table("sin").rearrange("p (t d) -> p t d", t=NT)
        cos_m = table("cos_m").rearrange("p (t d) -> p t d", t=NT)
        sin_m = table("sin_m").rearrange("p (t d) -> p t d", t=NT)
        cneg = table("cneg").rearrange("p (t n) -> p t n", t=NT)
        cone = table("cone").rearrange("p (t n) -> p t n", t=NT)
        q_gain, kv_gain = small[:, 0:384], small[:, 384:640]
        sinks, forget = small[:, 640:648], small[:, 648:656]
        csil = small[:, 656:656 + KT]
        mod1 = bias8
        a2 = u[:, 0, 2864:2864 + 4 * T].rearrange("p (v g t) -> p v g t", v=2, g=2)
        blkT = u[:, 1, 2864:2864 + 960].rearrange("p (v c g n) -> p v c g n", v=2, c=16, g=2)

        vbd = rotk[0:8 * NCMP, :, 512:1024]
        sc = kT[:, 4:6, :].rearrange("p a t -> p (a t)")[:, 0:NT * H * NCMP].rearrange("p (h n) -> p h n", n=NCMP)
        pcT = kT[0:8 * NCMP, 6:8, :].rearrange("p a t -> p (a t)").rearrange("p (b c) -> p b c", b=4)

        flat = tmp[:].rearrange("p a b -> p (a b)")

        landed = [sem(f"slot{i}_landed") for i in range(SLOTS)]
        hi_done, lo_done = sem("hi_done"), sem("lo_done")
        used = sem("used")
        x_loaded, tab_loaded, small_loaded = sem("x_loaded"), sem("tab_loaded"), sem("small_loaded")
        ident_loaded = sem("ident_loaded")
        c_loaded, c_ready, cb_ready = sem("c_loaded"), sem("c_ready"), sem("cb_ready")
        mod0_loaded, mod1_loaded, swa_loaded, ck_loaded = (sem(n) for n in ("mod0_loaded", "mod1_loaded", "swa_loaded", "ck_loaded"))
        vec_loaded, vec_used = [sem("vec0_loaded"), sem("vec1_loaded")], sem("vec_used")
        consts_set, stored = sem("consts_set"), sem("stored")
        mod1_used, swa_used = sem("mod1_used"), sem("swa_used")
        dve_step, act_step, pool_step = sem("dve_step"), sem("act_step"), sem("pool_step")
        early_landed = [sem(f"early{m}_landed") for m in range(ADA_EARLY)]
        early, late = stage("ada_early", "summed full taken"), stage("ada_late", "begun summed full taken")
        norm = stage("norm", "var rstd ready")
        turn = stage("turn", "turned taken low")
        out_ready = sem("out_ready")
        proj = {n: stage(n, "full taken") for n in ("nsa_in", "dil_in", "ab_in", "uq", "ukv", "cd_in")}
        outp = stage("outp", "full taken")
        ffn = [stage(f"ffn{i}", "gu_hi gu_lo dn_hi dn_lo gu_full silu_done hidden high act_ready tile0") for i in range(2)]
        att = stage("att", "scores maxes probs turns turned pv outs")
        nsa_s = stage("nsa", "pos_turned pos_taken cmp_sub cmp_summed kc_ready blocks hidden hidden_act hid_turned hid_taken hid8 kv_full kcT_ready vbd scored cmp_exp cmp_prob cmp_turned cmp_taken cmp_out rot_ready keys_ready gates_exp silu")
        dil_s = stage("dil", "rot_ready lse_in lse_out silu")
        ab_s = stage("ab", "c_ready nope rot_ready")
        cd_s = stage("cd", "f_in f_exp f_ln f_ready cum aug_ready flipped bias_ready")

        first, n_items = {}, 0
        split0, part0 = {}, {}
        n_split = n_part = 0
        for name, count in (("nsa_in", NSA_C), ("w1", 2), ("late", LATE_NSA), ("nsa_out", OUT_C),
                            ("dil_in", DIL_C), ("late_gate", LATE - LATE_NSA), ("dil_out", OUT_C), ("ab_in", AB_C), ("uq", 1), ("ukv", 1),
                            ("ab_out", OUT_C), ("ffn0", FF_STEPS), ("cd_in", CD_C), ("cd_out", OUT_C), ("ffn1", FF_STEPS)):
            first[name] = n_items
            n_items += count
            if name not in ("w1", "late", "late_gate"):
                split0[name] = n_split
                n_split += count
                if not name.startswith("ffn"):
                    part0[name] = n_part
                    n_part += count

        late_item = [first["late"] + c for c in range(LATE_NSA)] + [first["late_gate"] + c for c in range(LATE - LATE_NSA)]
        w1_early = [u[:, :, 1792:2816].rearrange("p t (k w) -> p t k w", k=4), tok[:].rearrange("p t (k w) -> p t k w", k=4)]
        w1_early_landed = [sem("w1_0_landed"), sem("w1_1_landed")]
        early_raw = [ring[:, 0, :], ring[:, 1, :]] + [sb(f"early{i}", [P, SLOT], over=o, skip=s)[:]
                                                      for i, (o, s) in enumerate((("whi0", 0), ("wlo0", 0), ("qT", 0), ("qT", 4 * SLOT)))]

        def slot_of(n, cols):
            return ring[:, n % SLOTS, 0:cols]

        def tiles_of(n, k, w):
            return slot_of(n, k * w).rearrange("p (k w) -> p k w", k=k)

        def wait_landed(eng, n, more=0):
            eng.wait_ge(landed[n % SLOTS], more * 16 + 16 * (n // SLOTS + 1))

        def norm_ready(i):
            return 2 * (i + 1 if i < 3 else i - 1)

        block = ctx.enter_context(nc.Block())

        group_of = {}
        for name, n0 in first.items():
            for n in range(n0, n_items):
                group_of[n] = name

        def released(n):
            if n in late_item:
                return late["summed"], late_item.index(n) + 1
            name = group_of[n]
            m = n - first[name]
            if name == "w1":
                return nsa_s["hidden"], m + 3
            if name.startswith("ffn"):
                return ffn[int(name[3:])]["dn_lo"], m + 1
            return lo_done, part0[name] + m + 1

        LATE_BANK, LATE_DVE, LATE_BUFS = 3, 3, 5
        late_acc = [u[:, b // 3, 2864 + (b % 3) * ADA_W:2864 + (b % 3 + 1) * ADA_W] for b in range(LATE_BUFS + 1)]
        late_term = late_acc.pop()
        late_dst = ([mod0[:, m * ADA_W:(m + 1) * ADA_W] for m in range(ADA_EARLY, ADA_C)]
                    + [mod1[:, m * ADA_W:(m + 1) * ADA_W] for m in range(ADA_C)])

        def late_round(i, step, lag):
            c = (i - lag) // step
            return c if i >= lag and (i - lag) % step == 0 and c < LATE_NSA else None

        def late_parts(c):
            return late_acc[c % LATE_BUFS] if c < LATE_NSA else acc[:, c % 2, :]

        def late_sum(pe, c, bank):
            if c is None:
                return
            pe.wait_ge(late["summed"], c + 1)
            if c > 0:
                pe.wait_ge(late["taken"], c)
            pe.matmul(bank[:, 0:ADA_W], ones[:], late_parts(c), start=True, stop=True).then_inc(late["full"], 1)

        TILE_GROUPS = D // P // 4
        turns = {}
        turn_n = [0, 0, 0]

        def plan_turn(name, groups, split=False):
            turns[name] = (groups, *turn_n, split)
            turn_n[0] += len(groups)
            turn_n[1] += sum(len(takes) for _, takes in groups)
            turn_n[2] += len(groups) if split else 0

        def turned_all(name):
            groups, _, t0, l0, split = turns[name]
            return (turn["low"], l0 + len(groups)) if split else (turn["taken"], t0 + sum(len(takes) for _, takes in groups))

        def turned_tile(name, t):
            _, _, _, l0, _ = turns[name]
            return turn["low"], l0 + TILE_GROUPS * (t + 1)

        def of_tile(groups, t):
            return [(g, group) for g, group in enumerate(groups) if t is None or g // TILE_GROUPS == t]

        def turn_src(g, take):
            rows, cols, dst, n = take
            return TB[g % 2][rows[0]:rows[1], cols[0]:cols[1]].rearrange("p (n c) -> p n c", n=n)[:, :, P - dst.shape[2]:]

        def turn_pe(pe, name, ready=None, tile=None):
            groups, _, t0, l0, split = turns[name]
            for g, (srcs, takes) in of_tile(groups, tile):
                if ready is not None:
                    ready(g)
                if g >= 2:
                    pe.wait_ge(*((turn["low"], l0 + g - 1) if split else (turn["taken"], t0 + (g - 1) * len(takes))))
                for n, (src, width) in enumerate(srcs):
                    ins = pe.transpose(TB[g % 2][0:width, n * P:(n + 1) * P], src, ident)
                ins.then_inc(turn["turned"], 1)

        def turn_act(act_, name, tile=None):
            groups, g0 = turns[name][0:2]
            for g, (srcs, takes) in of_tile(groups, tile):
                act_.wait_ge(turn["turned"], g0 + g + 1)
                for take in takes:
                    act_.copy(take[2], turn_src(g, take)).then_inc(turn["taken"], 1)

        def turn_low(dve, name, tile=None):
            groups, _, t0, _, _ = turns[name]
            for g, (srcs, takes) in of_tile(groups, tile):
                dve.wait_ge(turn["taken"], t0 + g + 1)
                rows, cols, dst, n = takes[0]
                low = dst_low[name][g]
                dve.tensor_tensor(low, turn_src(g, takes[0]), dst.bitcast(F32), ALU.subtract).then_inc(turn["low"], 1)

        def rotate(tl, dst, src, c, s, n, half, t, scratch, ready=None):
            TT, done = tl.eng.tensor_tensor, tl.done
            x1, x2 = src[:, :, 0:half], src[:, :, half:2 * half]
            cb_, sb_ = over(c[:, t, :], 1, n), over(s[:, t, :], 1, n)
            ta = scratch[:, 0:n * half].rearrange("p (n d) -> p n d", n=n)
            tb = scratch[:, 512:512 + n * half].rearrange("p (n d) -> p n d", n=n)
            tl.mark(TT(ta, x1, cb_, ALU.mult), tl.own)
            done(TT(tb, x2, sb_, ALU.mult))
            done(TT(dst[:, :, 0:half], ta, tb, ALU.subtract))
            tl.mark(TT(ta, x2, cb_, ALU.mult), tl.own)
            done(TT(tb, x1, sb_, ALU.mult))
            done(TT(dst[:, :, half:2 * half], ta, tb, ALU.add), ready)

        def rows_to(dst, src, per=4, width=P, t_n=NT):
            groups = []
            for t in range(t_n):
                n_all = src[t].shape[1]
                for n in range(0, n_all, per):
                    m = min(per, n_all - n)
                    groups.append(([(src[t][:, n + j, :], width) for j in range(m)],
                                   [((0, width), (0, m * P), dst[0:width, n:n + m, t * P:(t + 1) * P], m)]))
            return groups

        def blocks_of(ap2, w=P):
            return [ap2[:, t, :].rearrange("p (n w) -> p n w", w=w) for t in range(NT)]

        turn_full = rows_to(hTh, blocks_of(tok))
        turn_resid = rows_to(hTh, blocks_of(x))
        low_full = [takes[0][2] for _, takes in rows_to(hTl, blocks_of(tok))]
        dst_low = {name: low_full for name in ("h0", "h1", "o0", "o1", "o2", "o3", "x0", "x1", "f0", "f1")}

        def att_pe(pe, name, between=None):
            jobs, b0 = att_jobs[name], att_base[name]
            n = len(jobs)
            for i in range(n + 3):
                if i < n:
                    q, k, _, _ = jobs[i]
                    if i >= 2:
                        pe.wait_ge(att["maxes"], 2 * (b0 + i - 1))
                    pe.matmul(S[i % 2][:, 0:P], q[:, 0:P], k[:, 0:P], start=True, stop=True)
                    pe.matmul(S[i % 2][:, P:SW], q[:, P:T], k[:, 0:T], start=True, stop=True).then_inc(att["scores"], 1)
                    if between is not None:
                        between(i)
                if 2 <= i < n + 2:
                    j = i - 2
                    pe.wait_ge(att["probs"], 2 * (b0 + j) + 2)
                    if j >= 2:
                        pe.wait_ge(att["turned"], b0 + j - 1)
                    for b in range(3):
                        ins = pe.transpose(TB[j % 2][:, b * P:(b + 1) * P], prob[:, j % 3, 1 + b * P:1 + (b + 1) * P], ident)
                    ins.then_inc(att["turns"], 1)
                if i >= 3:
                    j = i - 3
                    v = jobs[j][2]
                    pe.wait_ge(att["turned"], b0 + j + 1)
                    if j >= 3:
                        pe.wait_ge(att["outs"], b0 + j - 2)
                    o = G[j % 3]
                    pt = probT[:, j % 3, :]
                    pe.matmul(o[:, 0:P], pt[:, 0:P], v[0], start=True, stop=True)
                    pe.matmul(o[:, P:2 * P], pt[:, P:2 * P], v[0], start=True, stop=False)
                    pe.matmul(o[:, P:2 * P], pt[:, 2 * P:SW], v[1], start=False, stop=True).then_inc(att["pv"], 1)

        def att_dve(dve, tl, name, bias_of, scale_of, take, sink=None, between=None):
            jobs, b0 = att_jobs[name], att_base[name]
            n = len(jobs)
            for i in range(n + 4):
                if i < n:
                    dve.wait_ge(att["scores"], b0 + i + 1)
                    if i >= 3:
                        dve.wait_ge(att["probs"], 2 * (b0 + i) - 4)
                    s, bank, bias, h = scr[:, i % 3, :], S[i % 2], bias_of(i), i % H
                    if i >= H:
                        dve.wait_ge(att["probs"], 2 * (b0 + i - H) + 2)
                    least, scale = 3e38, scale_of(i)
                    if sink is not None and sink(i) is not None:
                        tl.mark(dve.tensor_copy(s[:, 0:SW + 2:SW + 1], sink(i).broadcast_to([P, 2])), tl.own)
                        least = sink(i)
                    tl.mark(dve.tensor_tensor_reduce(s[:, 1:1 + P], bank[:, 0:P], bias[:, 0:P], -scale, least, ALU.add, ALU.min,
                                                     negmax[:, h, 0:1]), att["maxes"])
                    tl.mark(dve.tensor_tensor_reduce(s[:, 1 + P:1 + SW], bank[:, P:SW], bias[:, P:SW], -scale, least, ALU.add, ALU.min,
                                                     negmax[:, h, 1:2]), att["maxes"])
                if between is not None:
                    between(i)
                if i >= 4:
                    j = i - 4
                    dve.wait_ge(att["pv"], b0 + j + 1)
                    tl.done(dve.reciprocal(rden[:, j, :], den[:, j, :]))
                    off = jobs[j][3]
                    take(j, G[j % 3][:, 0:2 * P].rearrange("p (t d) -> p t d", t=NT)[:, :, off:off + DH], rden[:, j, :])

        def att_act(act_, name, sink=lambda i: False, between=None):
            n, b0 = len(att_jobs[name]), att_base[name]
            for i in range(n + 2):
                if i < n:
                    lo, hi = (0, SW + 2) if sink(i) else (1, SW + 1)
                    act_.wait_ge(att["maxes"], 2 * (b0 + i) + 2)
                    if i >= 3:
                        act_.wait_ge(att["turns"], b0 + i - 2)
                    h, b = i % H, i % 3
                    act_.activation(prob[:, b, lo:1 + P], scr[:, b, lo:1 + P], ACT.Exp, bias=negmax[:, h, 0:1], scale=-1.0,
                                    accum_out=den[:, i, 0:1]).then_inc(att["probs"], 1)
                    act_.activation(prob[:, b, 1 + P:hi], scr[:, b, 1 + P:hi], ACT.Exp, bias=negmax[:, h, 1:2], scale=-1.0,
                                    accum_out=den[:, i, 1:2]).then_inc(att["probs"], 1)
                if between is not None:
                    between(i)
                if i >= 2:
                    j = i - 2
                    act_.wait_ge(att["turns"], b0 + j + 1)
                    if j >= 3:
                        act_.wait_ge(att["pv"], b0 + j - 2)
                    act_.copy(probT[:, j % 3, :], TB[j % 2][:, 0:SW]).then_inc(att["turned"], 1)

        def pair(tile, h):
            return tile[(h % 2) * DH:(h % 2) * DH + DH, h // 2, :]

        def v_of(lo, off):
            return [u[:, t, lo:lo + P] for t in range(NT)], off

        def twin(tile, h, g):
            return tile[(h % 2) * DH:(h % 2) * DH + DH, g, :]

        nsa_jobs = [(pair(qT, h), twin(kT, h, br * 2 + h // 8), *v_of(384 + 256 * br, DH * (h // 8)))
                    for br in range(2) for h in range(H)]
        dil_jobs = [(pair(qT, h), pair(kT, h), *v_of(2 * D + P * (h // 2), DH * (h % 2))) for h in range(H)]
        mla_jobs = [(qT[0:96, h, :], kT[0:96, h, :], *v_of(2560 + P * h, DH)) for h in range(8)]
        swa_jobs = [(pair(q2T, h), twin(q2T, h, 4 + h // 4), *v_of(1312, DH * (h // 4))) for h in range(8)]
        fox_jobs = [(qT[0:FOXW, h, :], kT[0:FOXW, h, :], *v_of(1024 + P * (h // 2), DH * (h % 2))) for h in range(8)]
        ck_jobs = [(pair(q2T, h), twin(q2T, h, 4 + h // 2), *v_of(2568 + P * (h // 2), DH * (h % 2))) for h in range(8)]
        att_jobs = {"nsa": nsa_jobs, "dil": dil_jobs, "ab": mla_jobs + swa_jobs, "cd": fox_jobs + ck_jobs}
        att_base, heads_n = {}, 0
        for name, jobs in att_jobs.items():
            att_base[name] = heads_n
            heads_n += len(jobs)

        nsa_plain = rows_to(q2T, blocks_of(u[:, :, NSA_Q:NSA_Q + D]))
        kdup = rotk[:, :, 0:512]
        kcdup = rotk[:, :, 512:1024]
        nsa_rot = rows_to(qT, blocks_of(tok)) + rows_to(kT, blocks_of(kdup))
        a2f = a2.rearrange("p v g t -> p (v g) t")
        nsa_kc = [([(kcdup[:, t, n * P:(n + 1) * P], P) for n in range(4)],
                   [((0, DH), (0, 4 * P), a2f[0:DH, :, t * P:(t + 1) * P], 4),
                    ((DH, P), (0, 4 * P), a2f[DH:P, :, max(t * P - 1, 0):(t + 1) * P - 1], 4)]) for t in range(NT)]
        dil_rot = rows_to(qT, blocks_of(tok)) + rows_to(kT, blocks_of(rotk))
        ab_c = rows_to(hTh, blocks_of(tok[:, :, 0:640]))
        dst_low["ab_c"] = [takes[0][2] for _, takes in rows_to(hTl, blocks_of(tok[:, :, 0:640]))]
        qcat = tok[:, :, 0:768]
        kcat = rotk[:, :, 0:768]
        kswa = tok[:, :, 768:1024]
        ab_rot = (rows_to(qT, blocks_of(qcat, 96), width=96) + rows_to(kT, blocks_of(kcat, 96), width=96)
                  + rows_to(q2T, blocks_of(u[:, :, 672:1184])) + rows_to(q2T[:, 4:6, :], blocks_of(kswa)))
        qaug = tok[:, :, 0:8 * FOXW]
        kaug = rotk[:, :, 0:8 * FOXW]
        cd_rot = (rows_to(qT, blocks_of(qaug, FOXW), width=FOXW) + rows_to(kT, blocks_of(kaug, FOXW), width=FOXW)
                  + rows_to(q2T, blocks_of(u[:, :, 1544:2056])) + rows_to(q2T[:, 4:8, :], blocks_of(u[:, :, 2056:2568])))

        for name, groups in (("h0", turn_full), ("nsa_kc", nsa_kc), ("nsa_plain", nsa_plain), ("nsa_rot", nsa_rot), ("o0", turn_full),
                             ("h1", turn_full), ("dil_rot", dil_rot), ("o1", turn_full), ("x0", turn_resid), ("ab_c", ab_c),
                             ("ab_rot", ab_rot), ("o2", turn_full), ("f0", turn_resid), ("x1", turn_resid), ("cd_rot", cd_rot),
                             ("o3", turn_full), ("f1", turn_resid)):
            plan_turn(name, groups, name in dst_low)

        @block.sync
        def _(sp):
            def fetch(n, src, cols):
                sp.wait_ge(*(released(n - SLOTS) if n >= SLOTS else (early["full"], n + 1)))
                sp.dma_start(slot_of(n, cols), src).then_inc(landed[n % SLOTS], 16)

            def group(name, srcs, cols):
                n0, count = first[name], srcs.shape[0]
                for j in range(min(SLOTS, count)):
                    fetch(n0 + j, srcs[j], cols)
                if count > 2 * SLOTS:
                    with sp.Fori(1, count // SLOTS) as i:
                        for j in range(SLOTS):
                            done, value = released(n0 + j)
                            sp.wait_ge(done, i * SLOTS + (value - SLOTS))
                            sp.dma_start(slot_of(n0 + j, cols), srcs[i * SLOTS + j]).then_inc(landed[(n0 + j) % SLOTS], 16)
                else:
                    for j in range(SLOTS, count):
                        fetch(n0 + j, srcs[j], cols)

            for m in range(ADA_EARLY):
                sp.dma_start(early_raw[m][:, 0:KT * ADA_W], a["ada_w0"][m]).then_inc(early_landed[m], 16)
                if m == 1:
                    sp.dma_start(x[:], a["x"].rearrange("b (t p) d -> p (b t) d", p=P)).then_inc(x_loaded, 16)
                if m == 2:
                    bias = a["ada_b"][0:1, 0:ADA_EARLY * ADA_W].rearrange("a d -> (a d)")
                    sp.dma_start(mod0[:, 0:ADA_EARLY * ADA_W], bias.partition_broadcast(P)).then_inc(mod0_loaded, 16)
            def fetch_w1(i):
                sp.dma_start(w1_early[i], a["cmp_w1"][i].rearrange("p (t k w) -> p t k w", t=2, k=4)).then_inc(w1_early_landed[i], 16)

            for n in range(NSA_C):
                fetch(n, a["nsa_w_in"][n], KT * NSA_W)
                if n == 2:
                    fetch_w1(0)
                if n == 3:
                    sp.wait_ge(*turned_all("h0"))
                    fetch_w1(1)
            for i in range(2):
                fetch(first["w1"] + i, a["cmp_w1"][2 + i], 2048)

            def fetch_late(c):
                fetch(late_item[c], a["ada_w0"][ADA_EARLY + c] if c < LATE - ADA_C else a["ada_w1"][c - (LATE - ADA_C)], KT * ADA_W)

            for c in range(LATE_NSA):
                fetch_late(c)
            group("nsa_out", a["nsa_w_out"], KT * OUT_W)
            group("dil_in", a["dil_w_in"], KT * DIL_W)
            for c in range(LATE_NSA, LATE):
                fetch_late(c)
            group("dil_out", a["dil_w_out"], KT * OUT_W)
            group("ab_in", a["ab_w_in"], KT * AB_W)
            group("uq", a["ab_w_uq"], 3 * 768)
            group("ukv", a["ab_w_ukv"], 2 * 1024)
            group("ab_out", a["ab_w_out"], KT * OUT_W)
            group("ffn0", a["ffn0"], 3072)
            group("cd_in", a["cd_w_in"], KT * CD_W)
            group("cd_out", a["cd_w_out"], KT * OUT_W)
            group("ffn1", a["ffn1"], 3072)
            for t in range(NT):
                sp.wait_ge(norm["ready"], norm_ready(8) - 1 + t)
                sp.dma_start(out[:, t * P:(t + 1) * P, :].rearrange("b p d -> p (b d)"), x[:, t, :]).then_inc(stored, 16)
            sp.wait_ge(stored, 16 * NT)

        @block.gpsimd
        def _(pool):
            pool.memset(mhalf[:], -0.5).then_inc(consts_set, 1)
            pool.memset(ones[:], 1.0).then_inc(consts_set, 1)
            pool.memset(kc2[:], 0.0).then_inc(consts_set, 1)
            pool.wait_ge(consts_set, 3)
            tl = Tally(pool, pool_step)

            def load_vec(v):
                if v >= 2:
                    pool.wait_ge(vec_used, v - 1)
                pool.dma_start(vec[:, v % 2, :], a["vecs"][v:v + 1, :].rearrange("a d -> (a d)").partition_broadcast(P)).then_inc(vec_loaded[v % 2], 16)

            def rstd_of(i):
                for t in range(NT):
                    pool.wait_ge(norm["var"], 2 * i + t + 1)
                    pool.tensor_tensor(rstd[:, t:t + 1], var[:, t:t + 1], mhalf[:, t:t + 1], ALU.pow).then_inc(norm["rstd"], 1)

            def rotate_all(dst, lo, scratch, ready):
                for t in range(NT):
                    rotate(tl, dst[:, t, :].rearrange("p (h d) -> p h d", h=H), u[:, t, lo:lo + D].rearrange("p (h d) -> p h d", h=H),
                           cos, sin, H, HALF, t, scratch, ready)

            load_vec(0)
            rstd_of(0)
            load_vec(1)
            load_vec(2)
            pool.wait_ge(tab_loaded, 16)
            pool.wait_ge(proj["nsa_in"]["taken"], 2 * -(-(NSA_Q + D) // NSA_W))
            pool.wait_ge(nsa_s["hidden"], 2)
            pool.wait_ge(nsa_s["keys_ready"], NT)
            for dst, src in ((mod1[:], a["ada_b"][1:2, :]), (mod0[:, ADA_EARLY * ADA_W:], a["ada_b"][0:1, ADA_EARLY * ADA_W:])):
                pool.dma_start(dst, src.rearrange("a d -> (a d)").partition_broadcast(P)).then_inc(mod1_loaded, 16)
            rotate_all(tok, NSA_Q, flat, nsa_s["rot_ready"])
            for c in range(LATE_NSA):
                pool.wait_ge(late["begun"], c + 1)
                n = late_item[c]
                wait_landed(pool, n)
                w, part = tiles_of(n, KT, ADA_W), late_parts(c)
                for k in range(LATE_DVE, KT):
                    tl.done(pool.tensor_tensor(late_term, w[:, k, :], csil[:, k:k + 1].broadcast_to([P, ADA_W]), ALU.mult))
                    tl.done(pool.tensor_tensor(part, part, late_term, ALU.add), late["summed"] if k == KT - 1 else None)
            rstd_of(1)
            for dst, lo in ((tok, 0), (rotk, D)):
                pool.wait_ge(proj["dil_in"]["taken"], 2 * ((lo + D) // DIL_W))
                rotate_all(dst, lo, flat, dil_s["rot_ready"])
            rstd_of(2)
            load_vec(3)
            load_vec(4)
            pool.wait_ge(mod1_used, 1)
            pool.dma_start(bias8[:], a["swa_bias"]).then_inc(swa_loaded, 16)
            rstd_of(3)
            rstd_of(4)
            rstd_of(5)
            load_vec(5)
            load_vec(6)
            pool.wait_ge(swa_used, 1)
            b8 = bias8[:].rearrange("p (h w) -> p h w", h=8)
            rev = a["rel_rev"]
            for lo, base in ((0, P), (P, 0), (2 * P, P)):
                pool.dma_start(b8[:, :, lo:lo + P], bass.AP(tensor=rev.tensor, offset=base, ap=[[1, P], [rev.shape[1], 8], [1, P]])).then_inc(ck_loaded, 16)
            rstd_of(6)
            load_vec(7)
            load_vec(8)
            rstd_of(7)
            load_vec(9)
            load_vec(10)
            rstd_of(8)

        @block.tensor
        def _(pe):
            def split_products(out_, act_h, act_l, w_h, w_l, first_, last_):
                pe.matmul(out_, act_h, w_h, start=first_, stop=False)
                pe.matmul(out_, act_h, w_l, start=False, stop=False)
                return pe.matmul(out_, act_l, w_h, start=False, stop=last_)

            def gemm_chunk(name, st, m, j, w, n_k=KT, before_tile=None):
                if before_tile is None:
                    pe.wait_ge(lo_done, m + (part0[name] + 1))
                wh, wl = (part[j % 2][:, 0:n_k * w].rearrange("p (k w) -> p k w", k=n_k) for part in (whi, wlo))
                for t in range(NT):
                    if before_tile is not None:
                        before_tile(t)
                    for k in range(n_k):
                        ins = split_products(G[(j % 2) * 2 + t][:, 0:w], hTh[:, k, t * P:(t + 1) * P], hTl[:, k, t * P:(t + 1) * P],
                                             wh[:, k, :], wl[:, k, :], k == 0, k == n_k - 1)
                    ins.then_inc(st["full"] if t == 0 else used, 1)

            def turn_first(name, turn_name, ready):
                def before_tile(t):
                    turn_pe(pe, turn_name, ready, t)
                    pe.wait_ge(*turned_tile(turn_name, t))
                    if t == 0:
                        pe.wait_ge(lo_done, part0[name] + 1)
                return before_tile

            def gemm(name, st, count, w, before, turn_name, ready):
                gemm_chunk(name, st, 0, 0, w, before_tile=turn_first(name, turn_name, ready))
                gemm_chunk(name, st, 1, 1, w)
                if count > 4:
                    with pe.Fori(1, count // 2) as i:
                        for j in range(2):
                            pe.wait_ge(st["taken"], i * 4 + (before + 2 * (j - 1)))
                            gemm_chunk(name, st, i * 2 + j, j, w)
                else:
                    for m in range(2, count):
                        pe.wait_ge(st["taken"], before + 2 * (m - 1))
                        gemm_chunk(name, st, m, m, w)

            def wide(name, st, k0, k_n, w):
                pe.wait_ge(lo_done, part0[name] + 1)
                slot = split0[name] % 2
                wh, wl = (part[slot][:, 0:k_n * 2 * w].rearrange("p (k w) -> p k w", k=k_n) for part in (whi, wlo))
                for t in range(NT):
                    for half in range(2):
                        cols = slice(half * w, (half + 1) * w)
                        for k in range(k_n):
                            ins = split_products(G[2 * t + half][:, 0:w], hTh[:, k0 + k, t * P:(t + 1) * P], hTl[:, k0 + k, t * P:(t + 1) * P],
                                                 wh[:, k, cols], wl[:, k, cols], k == 0, k == k_n - 1)
                        ins.then_inc(st["full"] if (t, half) != (1, 1) else used, 1)

            def ffn_pe(name, st):
                def gate_up(b, s):
                    pe.wait_ge(st["gu_lo"], s + 1)
                    for part in range(2):
                        bank = S[b][:, part * T:(part + 1) * T]
                        for k in range(KT):
                            at = slice((part * KT + k) * P, (part * KT + k + 1) * P)
                            pe.matmul(bank, whi[b][:, at], hTh[:, k, :], start=(k == 0), stop=False)
                            pe.matmul(bank, whi[b][:, at], hTl[:, k, :], start=False, stop=False)
                            ins = pe.matmul(bank, wlo[b][:, at], hTh[:, k, :], start=False, stop=(k == KT - 1))
                    ins.then_inc(st["gu_full"], 1)

                def down(b, s, start, stop):
                    pe.wait_ge(st["dn_lo"], s + 1)
                    pe.wait_ge(st["act_ready"], s + 1)
                    for t in range(NT):
                        for half in range(2):
                            at = slice(2 * KT * P + half * 512, 2 * KT * P + (half + 1) * 512)
                            ts = slice(t * P, (t + 1) * P)
                            ins = split_products(G[2 * t + half][:], acth[:, b, ts], actl[:, b, ts], whi[b][:, at], wlo[b][:, at], start, stop)
                        if t == 0 and stop:
                            ins.then_inc(st["tile0"], 1)
                    ins.then_inc(used, 1)

                gate_up(0, 0)
                gate_up(1, 1)
                down(0, 0, True, False)
                with pe.Fori(0, (FF_STEPS - 2) // 2) as i:
                    for j in range(2):
                        s = i * 2 + (1 + j)
                        pe.wait_ge(st["hidden"], s)
                        gate_up(j, s + 1)
                        down(1 - j, s, False, False)
                down((FF_STEPS - 1) % 2, FF_STEPS - 1, False, True)

            def norm_tiles(i, per_tile=2):
                def ready(g):
                    if g % per_tile == 0:
                        pe.wait_ge(norm["ready"], norm_ready(i) - 1 + g // per_tile)
                return ready

            pe.wait_ge(consts_set, 3)
            pe.wait_ge(cb_ready, ADA_PE)
            for m in range(ADA_EARLY):
                if m >= 2:
                    pe.wait_ge(early["taken"], m - 1)
                bank = S[m % 2][:, 0:ADA_W]
                pe.wait_ge(early_landed[m], 16)
                w = early_raw[m][:, 0:KT * ADA_W].rearrange("p (k w) -> p k w", k=KT)
                for k in range(ADA_PE):
                    pe.matmul(bank, cb[:, k, :], w[:, k, :], start=(k == 0), stop=False)
                pe.wait_ge(early["summed"], m + 1)
                pe.matmul(bank, ones[:], acc[:, m % 2, :], start=False, stop=True).then_inc(early["full"], 1)

            pe.wait_ge(ident_loaded, 16)
            st = proj["nsa_in"]
            for m in range(NSA_C):
                if m >= 2:
                    pe.wait_ge(st["taken"], 2 * (m - 1))
                gemm_chunk("nsa_in", st, m, m, NSA_W, before_tile=turn_first("nsa_in", "h0", norm_tiles(0)) if m == 0 else None)
                if m == 3:
                    pe.wait_ge(small_loaded, 16 * SMALL_LOADS)
                    for v in range(2):
                        ins = pe.transpose(TB[0][:, v * 16:(v + 1) * 16], pe_rows[:, v, :], ident[0:16, 0:16])
                    ins.then_inc(nsa_s["pos_turned"], 1)
                    pe.wait_ge(nsa_s["kc_ready"], 1)
                    pe.wait_ge(nsa_s["pos_taken"], 1)
                    turn_pe(pe, "nsa_kc")
                for i in {4: (0,), 5: (1,), 7: (2, 3)}.get(m, ()):
                    pe.wait_ge(nsa_s["blocks"], 8)
                    v, kh = i // 2, i % 2
                    if i < 2:
                        pe.wait_ge(w1_early_landed[i], 16)
                    else:
                        wait_landed(pe, first["w1"] + i - 2)
                    for c in range(8):
                        w1 = w1_early[i][:, c // 4, c % 4, :] if i < 2 else tiles_of(first["w1"] + i - 2, 8, 256)[:, c, :]
                        ins = pe.matmul(S[v][0:2 * NCMP, 0:256], blkT[:, v, kh * 8 + c, :, :], w1,
                                        start=(kh == 0 and c == 0), stop=(kh == 1 and c == 7))
                    ins.then_inc(nsa_s["hidden"], 1)

            pe.wait_ge(st["taken"], 2 * NSA_C)
            turn_pe(pe, "nsa_plain")
            pe.wait_ge(nsa_s["hidden_act"], 2)
            for v in range(2):
                for mh in range(2):
                    at = (2 * v + mh) * 2 * NCMP
                    ins = pe.transpose(G[3][:, at:at + 2 * NCMP], hidr[:, v, mh * P:(mh + 1) * P], ident[0:2 * NCMP, 0:2 * NCMP])
            ins.then_inc(nsa_s["hid_turned"], 1)
            pe.wait_ge(nsa_s["hid_taken"], 1)
            for mh in range(2):
                ins = pe.matmul(S[0][:, 0:2 * NCMP], w2[:, mh, 0:P], hid[:, 0, mh, :], start=(mh == 0), stop=(mh == 1))
            ins.then_inc(nsa_s["kv_full"], 1)
            pe.wait_ge(*turned_all("nsa_plain"))
            pe.wait_ge(nsa_s["kcT_ready"], 4)
            for t in range(NT):
                for pr in range(H // 2):
                    ins = pe.matmul(G[2 * t + pr // 4][:, (pr % 4) * P:(pr % 4 + 1) * P], q2T[:, pr, t * P:(t + 1) * P],
                                    kc2[:, pr // 4, :], start=True, stop=True)
            ins.then_inc(nsa_s["scored"], 1)
            pe.wait_ge(nsa_s["hid8"], 4)
            for g in range(2):
                for mh in range(2):
                    ins = pe.matmul(S[1][0:8 * NCMP, g * DH:(g + 1) * DH], hid8[:, g, mh, :], w2[:, mh, P:3 * DH],
                                    start=(mh == 0), stop=(mh == 1))
            ins.then_inc(nsa_s["kv_full"], 1)
            pe.wait_ge(nsa_s["rot_ready"], NT)
            pe.wait_ge(nsa_s["keys_ready"], NT)
            turn_pe(pe, "nsa_rot")
            pe.wait_ge(*turned_all("nsa_rot"))
            pe.wait_ge(nsa_s["cmp_prob"], 1)
            for b in range(4):
                ins = pe.transpose(TB[0][0:8 * NCMP, b * P:(b + 1) * P], sc[:, b * 8:(b + 1) * 8, :], ident)
            ins.then_inc(nsa_s["cmp_turned"], 1)
            pe.wait_ge(nsa_s["cmp_taken"], 1)
            pe.wait_ge(nsa_s["vbd"], 2)
            for b in range(4):
                pe.matmul(G[b][:], pcT[:, b, :], vbd[:, b % 2, :], start=True, stop=True).then_inc(nsa_s["cmp_out"], 1)
            pe.wait_ge(nsa_s["cmp_summed"], 4)
            att_pe(pe, "nsa", lambda i: late_sum(pe, late_round(i, 4, 1), G[LATE_BANK]))

            def project_out(i, name):
                gemm(name, outp, OUT_C, OUT_W, i * 2 * OUT_C, f"o{i}",
                     lambda g: pe.wait_ge(out_ready, 2 * i + g // 2 + 1) if g % 2 == 0 else None)

            project_out(0, "nsa_out")

            gemm("dil_in", proj["dil_in"], DIL_C, DIL_W, 0, "h1", norm_tiles(1))
            pe.wait_ge(proj["dil_in"]["taken"], 2 * DIL_C)
            turn_pe(pe, "dil_rot", lambda g: pe.wait_ge(dil_s["rot_ready"], g // 2 + 1))
            pe.wait_ge(*turned_all("dil_rot"))
            for c in range(LATE_NSA, LATE):
                late_sum(pe, c, S[c % 2])
            pe.wait_ge(late["taken"], LATE)
            att_pe(pe, "dil")
            project_out(1, "dil_out")

            gemm("ab_in", proj["ab_in"], AB_C, AB_W, 0, "x0", norm_tiles(2))
            pe.wait_ge(ab_s["c_ready"], 1)
            turn_pe(pe, "ab_c")
            pe.wait_ge(*turned_all("ab_c"))
            pe.wait_ge(proj["ab_in"]["taken"], 2 * AB_C)
            wide("uq", proj["uq"], 0, 3, 384)
            pe.wait_ge(proj["uq"]["taken"], 4)
            wide("ukv", proj["ukv"], 3, 2, 512)
            pe.wait_ge(ab_s["rot_ready"], 1)
            pe.wait_ge(ab_s["nope"], 4)
            pe.wait_ge(proj["ukv"]["taken"], 4)
            turn_pe(pe, "ab_rot")
            pe.wait_ge(*turned_all("ab_rot"))
            att_pe(pe, "ab")
            project_out(2, "ab_out")

            turn_pe(pe, "f0", norm_tiles(5))
            pe.wait_ge(*turned_all("f0"))
            ffn_pe("ffn0", ffn[0])

            gemm("cd_in", proj["cd_in"], CD_C, CD_W, 0, "x1", norm_tiles(6))
            pe.wait_ge(proj["cd_in"]["taken"], 2 * CD_C)
            pe.wait_ge(ck_loaded, 48)
            for h in range(8):
                if h >= 4:
                    pe.wait_ge(cd_s["bias_ready"], h - 3)
                pe.matmul(G[h % 4][:, 0:SW], table("flip"), bias8[:, h * SW:(h + 1) * SW], start=True, stop=True).then_inc(cd_s["flipped"], 1)
            pe.wait_ge(cd_s["f_ready"], 1)
            f = fox[:, 3, :]
            pe.matmul(S[0][:, 0:8], table("tri"), f[:, 0:8], start=True, stop=True)
            pe.matmul(S[0][:, 8:16], table("tri"), f[:, 8:16], start=True, stop=False)
            pe.matmul(S[0][:, 8:16], ones[:], f[:, 0:8], start=False, stop=True).then_inc(cd_s["cum"], 1)
            pe.wait_ge(cd_s["aug_ready"], 1)
            pe.wait_ge(proj["cd_in"]["taken"], 2 * CD_C)
            turn_pe(pe, "cd_rot")
            pe.wait_ge(*turned_all("cd_rot"))
            att_pe(pe, "cd")
            project_out(3, "cd_out")

            turn_pe(pe, "f1", norm_tiles(7))
            pe.wait_ge(*turned_all("f1"))
            ffn_pe("ffn1", ffn[1])

        @block.scalar
        def _(sc_e):
            tl = Tally(sc_e, act_step)
            sc_e.dma_start(csil, a["c"]).then_inc(c_loaded, 16)
            sc_e.dma_start(ident, a["tables"][:, 0:P]).then_inc(ident_loaded, 16)
            sc_e.wait_ge(c_loaded, 16)
            tl.done(sc_e.activation(csil, csil, ACT.Silu), c_ready)

            def high(name, q, j, cols):
                n0, k0 = first[name], split0[name]
                n = n0 + j
                sc_e.wait_ge(landed[n % 2], q * 16 + 16 * (n // 2 + 1))
                if not isinstance(q, int) or k0 + 2 * q + j >= 2:
                    sc_e.wait_ge(used, q * 2 + (k0 + j - 1))
                raw = ring[:, n % 2, 0:cols]
                sc_e.copy(whi[(k0 + j) % 2][:, 0:cols], raw).then_inc(hi_done, 1)

            def take_chunk(name, st, q, j, w):
                at = q * (2 * w) + j * w
                for t in range(NT):
                    if t == 0:
                        sc_e.wait_ge(st["full"], q * 2 + j + 1)
                    else:
                        sc_e.wait_ge(used, q * 2 + (split0[name] + j + 1))
                    dst = u[:, t, at:at + w] if isinstance(at, int) else u[:, t, bass.ds(at, w)]
                    sc_e.copy(dst, G[j * 2 + t][:, 0:w]).then_inc(st["taken"], 1)

            def project_in(name, turn_name, count, w, before_last=None):
                st = proj[name]
                high(name, 0, 0, KT * w)
                high(name, 0, 1, KT * w)
                turn_act(sc_e, turn_name)
                take_chunk(name, st, 0, 0, w)
                if count > 4:
                    with sc_e.Fori(1, count // 2) as q:
                        high(name, q, 0, KT * w)
                        take_chunk(name, st, q - 1, 1, w)
                        high(name, q, 1, KT * w)
                        take_chunk(name, st, q, 0, w)
                else:
                    for q in range(1, count // 2):
                        high(name, q, 0, KT * w)
                        take_chunk(name, st, q - 1, 1, w)
                        high(name, q, 1, KT * w)
                        take_chunk(name, st, q, 0, w)
                if before_last is not None:
                    before_last()
                take_chunk(name, st, count // 2 - 1, 1, w)

            def project_out(i, name, att_last):
                turn_act(sc_e, f"o{i}")
                sc_e.wait_ge(att["scores"], att_base[att_last] + len(att_jobs[att_last]))
                high(name, 0, 1, KT * OUT_W)
                high(name, 1, 0, KT * OUT_W)
                high(name, 1, 1, KT * OUT_W)

            def take_wide(name, st, at, w):
                for t in range(NT):
                    for half in range(2):
                        n = 2 * t + half
                        if n < 3:
                            sc_e.wait_ge(st["full"], n + 1)
                        else:
                            sc_e.wait_ge(used, split0[name] + 1)
                        sc_e.copy(u[:, t, at + half * w:at + (half + 1) * w], G[n][:, 0:w]).then_inc(st["taken"], 1)

            def ffn_act(name, turn_name, st):
                n0, k0 = first[name], split0[name]
                gu, dn = slice(0, 2 * KT * P), slice(2 * KT * P, 3 * KT * P)

                def high_gu(q, b, peeled=False):
                    sc_e.wait_ge(landed[b], q * 16 + 16 * (n0 // 2 + 1))
                    if peeled:
                        sc_e.wait_ge(used, k0 + b - 1)
                    else:
                        sc_e.wait_ge(st["gu_full"], q * 2 + (b - 1))
                    sc_e.copy(whi[b][:, gu], ring[:, b, gu]).then_inc(st["gu_hi"], 1)

                def high_dn(q, b):
                    sc_e.wait_ge(used, q * 2 + (k0 + b - 1))
                    sc_e.copy(whi[b][:, dn], ring[:, b, dn]).then_inc(st["dn_hi"], 1)

                def silu(q, b):
                    sc_e.wait_ge(st["gu_full"], q * 2 + b + 1)
                    sc_e.activation(sil[:, b, :], S[b][:, 0:T], ACT.Silu).then_inc(st["silu_done"], 1)

                def high_act(q, b):
                    sc_e.wait_ge(st["hidden"], q * 2 + b + 1)
                    sc_e.copy(acth[:, b, :], act[:, b, :]).then_inc(st["high"], 1)

                high_gu(0, 0, True)
                high_dn(0, 0)
                high_gu(0, 1, True)
                high_dn(0, 1)
                turn_act(sc_e, turn_name)
                silu(0, 0)
                high_act(0, 0)
                with sc_e.Fori(1, FF_STEPS // 2) as q:
                    high_gu(q, 0)
                    silu(q - 1, 1)
                    high_act(q - 1, 1)
                    high_dn(q, 0)
                    high_gu(q, 1)
                    silu(q, 0)
                    high_act(q, 0)
                    high_dn(q, 1)
                silu(FF_STEPS // 2 - 1, 1)
                high_act(FF_STEPS // 2 - 1, 1)

            def nsa_high(m):
                high("nsa_in", m // 2, m % 2, KT * NSA_W)

            def nsa_take(m):
                take_chunk("nsa_in", proj["nsa_in"], m // 2, m % 2, NSA_W)

            def hidden_act(v):
                sc_e.wait_ge(nsa_s["hidden"], 2 * v + 2)
                sc_e.activation(hidr[:, v, :], S[v][0:2 * NCMP, 0:256], ACT.Silu).then_inc(nsa_s["hidden_act"], 1)

            sc_e.wait_ge(early["full"], ADA_EARLY)
            nsa_high(0)
            sc_e.dma_start(tab[:, P:], a["tables"][:, P:]).then_inc(tab_loaded, 16)
            for dst, src in ((q_gain, a["q_norm"]), (kv_gain, a["kv_norm"]), (sinks, a["sinks"]), (forget, a["b_forget"])):
                sc_e.dma_start(dst, src.partition_broadcast(P)).then_inc(small_loaded, 16)
            sc_e.dma_start(bdmask[:], a["bdmask"]).then_inc(small_loaded, 16)
            sc_e.dma_start(pe_rows[:], a["pos"]).then_inc(small_loaded, 16)
            sc_e.dma_start(w2[:, :, 0:DH], a["cmp_w2"][:, 0]).then_inc(small_loaded, 16)
            sc_e.dma_start(w2[:, :, DH:P], a["cmp_w2"][:, 0]).then_inc(small_loaded, 16)
            sc_e.dma_start(w2[:, :, P:3 * DH], a["cmp_w2"][:, 1]).then_inc(small_loaded, 16)
            turn_act(sc_e, "h0", 0)
            nsa_high(1)
            turn_act(sc_e, "h0", 1)
            nsa_take(0)
            for m in range(1, 4):
                nsa_high(m + 1)
                nsa_take(m)
            sc_e.wait_ge(nsa_s["pos_turned"], 1)
            sc_e.copy(peT[:], TB[0][:, 0:32].rearrange("p (v c) -> p v c", v=2)).then_inc(nsa_s["pos_taken"], 1)
            turn_act(sc_e, "nsa_kc")
            nsa_high(5)
            nsa_take(4)
            nsa_high(6)
            nsa_take(5)
            nsa_high(7)
            hidden_act(0)
            nsa_take(6)
            nsa_take(7)
            turn_act(sc_e, "nsa_plain")
            hidden_act(1)
            sc_e.wait_ge(nsa_s["hid_turned"], 1)
            sc_e.copy(hid[:], G[3][:, 0:8 * NCMP].rearrange("p (v m n) -> p v m n", v=2, m=2)).then_inc(nsa_s["hid_taken"], 1)
            sc_e.wait_ge(proj["nsa_in"]["taken"], 2 * NSA_C)
            sc_e.activation(gate[:], u[:, :, 2816:2864], ACT.Exp, scale=-1.0).then_inc(nsa_s["gates_exp"], 1)
            sc_e.activation(u[:, :, 1792:2816], u[:, :, 1792:2816], ACT.Silu).then_inc(nsa_s["silu"], 1)
            turn_act(sc_e, "nsa_rot")
            sc_e.wait_ge(nsa_s["cmp_sub"], 1)
            sc_e.activation(sc[:], sc[:], ACT.Exp).then_inc(nsa_s["cmp_exp"], 1)
            sc_e.wait_ge(nsa_s["cmp_turned"], 1)
            sc_e.copy(pcT[:], TB[0][0:8 * NCMP, :].rearrange("p (b c) -> p b c", b=4)).then_inc(nsa_s["cmp_taken"], 1)
            att_act(sc_e, "nsa", between=lambda i: high("nsa_out", 0, 0, KT * OUT_W) if i == 2 * H - 3 else None)
            project_out(0, "nsa_out", "nsa")

            project_in("dil_in", "h1", DIL_C, DIL_W)
            sc_e.wait_ge(proj["dil_in"]["taken"], 2 * DIL_C)
            sc_e.activation(u[:, :, 3 * D:4 * D], u[:, :, 3 * D:4 * D], ACT.Silu).then_inc(dil_s["silu"], 1)
            turn_act(sc_e, "dil_rot")
            high("dil_out", 0, 0, KT * OUT_W)
            att_act(sc_e, "dil")
            sc_e.wait_ge(dil_s["lse_in"], 1)
            sc_e.activation(lse[:, 0, :], lse[:, 0, :], ACT.Exp).then_inc(dil_s["lse_out"], 1)
            project_out(1, "dil_out", "dil")

            project_in("ab_in", "x0", AB_C, AB_W, lambda: high("uq", 0, 0, 3 * 768))
            turn_act(sc_e, "ab_c")
            high("ukv", 0, 0, 2 * 1024)
            take_wide("uq", proj["uq"], 1536, 384)
            take_wide("ukv", proj["ukv"], 2560, 512)
            sc_e.wait_ge(proj["ukv"]["taken"], 4)
            for t in range(NT):
                sc_e.copy(qcat[:, t, :].rearrange("p (h d) -> p h d", h=8)[:, :, 0:DH],
                         u[:, t, 1536:2304].rearrange("p (h d) -> p h d", h=8)[:, :, 0:DH]).then_inc(ab_s["nope"], 1)
                sc_e.copy(kcat[:, t, :].rearrange("p (h d) -> p h d", h=8)[:, :, 0:DH],
                         u[:, t, 2560:3584].rearrange("p (h d) -> p h d", h=8)[:, :, 0:DH]).then_inc(ab_s["nope"], 1)
            high("ab_out", 0, 0, KT * OUT_W)
            turn_act(sc_e, "ab_rot")
            att_act(sc_e, "ab", sink=lambda i: i >= 8)
            project_out(2, "ab_out", "ab")
            ffn_act("ffn0", "f0", ffn[0])

            project_in("cd_in", "x1", CD_C, CD_W)
            sc_e.wait_ge(cd_s["f_in"], 1)
            sc_e.activation(fox[:, 1, :], fox[:, 1, :], ACT.Exp, scale=-1.0).then_inc(cd_s["f_exp"], 1)
            sc_e.wait_ge(cd_s["f_exp"], 1)
            sc_e.activation(fox[:, 1, :], fox[:, 1, :], ACT.Ln, bias=1.0).then_inc(cd_s["f_ln"], 1)
            high("cd_out", 0, 0, KT * OUT_W)
            turn_act(sc_e, "cd_rot")
            att_act(sc_e, "cd")
            project_out(3, "cd_out", "cd")
            ffn_act("ffn1", "f1", ffn[1])

        @block.vector
        def _(dve):
            tl = Tally(dve, dve_step)
            done = tl.done
            TT, STT, TS = dve.tensor_tensor, dve.scalar_tensor_tensor, dve.tensor_scalar

            def note(signal):
                done(dve.tensor_copy(scm[:, 0:1], mv[:, 0, 0:1]), signal)

            def ada_sum(raw, m):
                w = raw[:, 0:KT * ADA_W].rearrange("p (k w) -> p k w", k=KT)
                part = acc[:, m % 2, :]
                done(TS(part, w[:, ADA_PE, :], csil[:, ADA_PE:ADA_PE + 1], None, ALU.mult))
                for k in range(ADA_PE + 1, KT):
                    done(STT(part, w[:, k, :], csil[:, k:k + 1], part, ALU.mult, ALU.add), early["summed"] if k == KT - 1 else None)

            def ada_take(m):
                dve.wait_ge(early["full"], m + 1)
                dst = mod0[:, m * ADA_W:(m + 1) * ADA_W]
                done(TT(dst, dst, S[m % 2][:, 0:ADA_W], ALU.add), early["taken"])

            def low(name, q, j, cols):
                n, k = first[name] + j, split0[name] + j
                dve.wait_ge(hi_done, q * 2 + (part0[name] + j + 1))
                raw = ring[:, n % 2, 0:cols]
                TT(wlo[k % 2][:, 0:cols], raw, whi[k % 2][:, 0:cols].bitcast(F32), ALU.subtract).then_inc(lo_done, 1)

            def moments(src, t, pieces, layer_norm, eps):
                for c, piece in enumerate(src):
                    done(dve.bn_stats(bstat[:, t, c, :], piece))
                done(dve.bn_aggr(mv[:, t, :], bstat[:, t, 0:pieces, :]))
                v, mean = var[:, t:t + 1], mv[:, t, 0:1]
                if layer_norm:
                    done(TS(v, mv[:, t, 1:2], eps, None, ALU.add), norm["var"])
                else:
                    done(STT(v, mean, mean, mv[:, t, 1:2], ALU.mult, ALU.add))
                    done(TS(v, v, eps, None, ALU.add), norm["var"])

            vec_n = [0]

            def next_vec():
                v = vec_n[0]
                vec_n[0] += 1
                dve.wait_ge(vec_loaded[v % 2], 16 * (v // 2 + 1))
                return vec[:, v % 2, :]

            def scale_gain(mod):
                scale, g = mod[:, D:2 * D], next_vec()
                done(STT(scale, scale, 1.0, g, ALU.add, ALU.mult), vec_used)

            def ada_norm(i, mod, t):
                done(TT(tok[:, t, :], x[:, t, :], mod[:, D:2 * D], ALU.mult))
                dve.wait_ge(norm["rstd"], 2 * i + t + 1)
                done(STT(tok[:, t, :], tok[:, t, :], rstd[:, t:t + 1], mod[:, 0:D], ALU.mult, ALU.add), norm["ready"])

            def layer_norm(i, g, b, pieces, t):
                moments([], t, pieces, True, EPS_LN)
                done(STT(x[:, t, :], x[:, t, :], mv[:, t, 0:1], g, ALU.subtract, ALU.mult))
                dve.wait_ge(norm["rstd"], 2 * i + t + 1)
                done(STT(x[:, t, :], x[:, t, :], rstd[:, t:t + 1], b, ALU.mult, ALU.add), norm["ready"])

            def set_head(col):
                def take(j, o, r):
                    done(TT(tok[:, :, (col + j) * DH:(col + j + 1) * DH], o, over(r, 2, DH), ALU.mult), att["outs"])
                return take

            def project_out(i, name, gatev, between, finish, turn_name):
                turn_low(dve, f"o{i}")
                low(name, 0, 1, KT * OUT_W)
                for m in range(OUT_C):
                    for t in range(NT):
                        if t == 0:
                            dve.wait_ge(outp["full"], OUT_C * i + m + 1)
                        else:
                            dve.wait_ge(used, split0[name] + m + 1)
                        cols = slice(m * OUT_W, (m + 1) * OUT_W)
                        y, part = G[(m % 2) * 2 + t][:, 0:OUT_W], x[:, t, cols]
                        if gatev is None:
                            done(STT(part, part, ALPHA, y, ALU.mult, ALU.add), outp["taken"])
                        else:
                            done(TT(tmp[:, t, 0:OUT_W], y, gatev[:, cols], ALU.mult), outp["taken"])
                            done(TT(part, part, tmp[:, t, 0:OUT_W], ALU.add))
                        done(dve.bn_stats(bstat[:, t, m, :], part))
                        if m == OUT_C - 1:
                            if t == 1:
                                turn_low(dve, turn_name, 0)
                            finish(t)
                    if m < OUT_C - 2:
                        low(name, 1, m, KT * OUT_W)
                    elif m == OUT_C - 2:
                        between()

            gu, dn = slice(0, 2 * KT * P), slice(2 * KT * P, 3 * KT * P)

            def low_ffn(st, q, b, part, what):
                dve.wait_ge(st[what + "_hi"], q * 2 + b + 1)
                TT(wlo[b][:, part], ring[:, b, part], whi[b][:, part].bitcast(F32), ALU.subtract).then_inc(st[what + "_lo"], 1)

            def ffn_dve(i, name, turn_name):
                st = ffn[i]
                turn_low(dve, turn_name, 1)
                low_ffn(st, 0, 1, gu, "gu")
                low_ffn(st, 0, 1, dn, "dn")

                def hidden(q, b):
                    dve.wait_ge(st["silu_done"], q * 2 + b + 1)
                    TT(act[:, b, :], S[b][:, T:2 * T], sil[:, b, :], ALU.mult).then_inc(st["hidden"], 1)
                    dve.wait_ge(st["high"], q * 2 + b + 1)
                    TT(actl[:, b, :], act[:, b, :], acth[:, b, :].bitcast(F32), ALU.subtract).then_inc(st["act_ready"], 1)

                hidden(0, 0)
                with dve.Fori(1, FF_STEPS // 2) as q:
                    low_ffn(st, q, 0, gu, "gu")
                    hidden(q - 1, 1)
                    low_ffn(st, q, 0, dn, "dn")
                    low_ffn(st, q, 1, gu, "gu")
                    hidden(q, 0)
                    low_ffn(st, q, 1, dn, "dn")
                hidden(FF_STEPS // 2 - 1, 1)

            def ffn_out(i, name, finish, turn_name=None, between=None):
                for t in range(NT):
                    if t == 0:
                        dve.wait_ge(ffn[i]["tile0"], 1)
                    else:
                        dve.wait_ge(used, split0[name] + FF_STEPS)
                    for half in range(2):
                        part = x[:, t, half * 512:(half + 1) * 512]
                        done(STT(part, part, ALPHA, G[2 * t + half][:], ALU.mult, ALU.add))
                        done(dve.bn_stats(bstat[:, t, half, :], part))
                    finish(t)
                    if t == 0 and turn_name is not None:
                        between()
                        turn_low(dve, turn_name, 0)

            def attention(name, bias_of, take, scale=lambda i: SCALE, sink=None, between=None):
                att_dve(dve, tl, name, bias_of, scale, take, sink, between)

            dve.wait_ge(consts_set, 3)
            dve.wait_ge(c_ready, 1)
            for k in range(ADA_PE):
                done(TS(cb[:, k, :], ones[:], csil[:, k:k + 1], None, ALU.mult), cb_ready)
            for m in range(ADA_EARLY):
                dve.wait_ge(early_landed[m], 16)
                ada_sum(early_raw[m], m)
                if m == 1:
                    dve.wait_ge(x_loaded, 16)
                    for t in range(NT):
                        moments([x[:, t, c * 512:(c + 1) * 512] for c in range(2)], t, 2, False, EPS_RMS)
                    dve.wait_ge(mod0_loaded, 16)
                if m >= 1:
                    ada_take(m - 1)
            ada_take(ADA_EARLY - 1)
            scale_gain(mod0)
            def late_begin(c):
                n = late_item[c]
                wait_landed(dve, n)
                if c >= LATE_BUFS:
                    dve.wait_ge(late["full"], c - LATE_BUFS + 1)
                w, part, blocks = tiles_of(n, KT, ADA_W), late_parts(c), KT if c >= LATE_NSA else LATE_DVE
                done(TS(part, w[:, 0, :], csil[:, 0:1], None, ALU.mult))
                for k in range(1, blocks):
                    done(STT(part, w[:, k, :], csil[:, k:k + 1], part, ALU.mult, ALU.add),
                         None if k < blocks - 1 else late["summed" if c >= LATE_NSA else "begun"])

            def late_take(c, bank):
                dve.wait_ge(late["full"], c + 1)
                done(TT(late_dst[c], late_dst[c], bank[:, 0:ADA_W], ALU.add), late["taken"])

            def nsa_low(m):
                low("nsa_in", m // 2, m % 2, KT * NSA_W)

            ada_norm(0, mod0, 0)
            nsa_low(0)
            turn_low(dve, "h0", 0)
            ada_norm(0, mod0, 1)
            turn_low(dve, "h0", 1)
            nsa_low(1)
            nsa_low(2)
            nsa_low(3)
            dve.wait_ge(proj["nsa_in"]["taken"], 2 * 3)
            for t in range(NT):
                ins = dve.tensor_copy(kcdup[:, t, :].rearrange("p (n two d) -> p n two d", n=4, two=2),
                                      over(u[:, t, 0:256].rearrange("p (n d) -> p n d", n=4), 2, 2))
                done(ins, nsa_s["kc_ready"] if t == 1 else None)
            nsa_low(4)
            dve.wait_ge(tab_loaded, 16)
            dve.wait_ge(small_loaded, 16 * SMALL_LOADS)
            for t in range(NT):
                kd = kdup[:, t, :].rearrange("p (n two d) -> p n two d", n=4, two=2)
                for lo, n in ((256, 0), (512, 2)):
                    rotate(tl, kd[:, n:n + 2, 0, :], u[:, t, lo:lo + P].rearrange("p (g d) -> p g d", g=2), cos, sin, 2, HALF, t, flat)
                done(dve.tensor_copy(kd[:, :, 1, :], kd[:, :, 0, :]), nsa_s["keys_ready"])
            nsa_low(5)
            dve.wait_ge(*turned_all("nsa_kc"))
            for v in range(2):
                for g in range(2):
                    for far in range(2):
                        src = a2[:, v, g, 16 * far:16 * far + 240].rearrange("p (n b two) -> p b n two", two=2, b=8)[:, :, :, 0]
                        done(TT(blkT[:, v, far * 8:far * 8 + 8, g, :], src, over(peT[:, v, far * 8:far * 8 + 8], 2, NCMP), ALU.add), nsa_s["blocks"])
            nsa_low(6)
            nsa_low(7)
            done(TS(negsink[:], sinks, -1.0, None, ALU.mult))
            dve.wait_ge(nsa_s["hidden"], 4)
            late_begin(0)
            dve.wait_ge(nsa_s["kv_full"], 1)
            for g in range(2):
                for odd in range(2):
                    rows = slice(odd * DH, (odd + 1) * DH)
                    done(dve.tensor_copy(kc2[rows, g, odd * NCMP:(odd + 1) * NCMP], S[0][rows, g * NCMP:(g + 1) * NCMP]), nsa_s["kcT_ready"])
            dve.wait_ge(nsa_s["rot_ready"], NT)
            for g in range(2):
                for mh in range(2):
                    done(dve.tensor_copy(hid8[:, g, mh, :].rearrange("p (r n) -> p r n", r=8),
                                         over(hid[:, 1, mh, g * NCMP:(g + 1) * NCMP], 1, 8)), nsa_s["hid8"])
            dve.wait_ge(nsa_s["kv_full"], 2)
            for g in range(2):
                done(TT(vbd[:, g, :].rearrange("p (r d) -> p r d", r=8), over(S[1][0:8 * NCMP, g * DH:(g + 1) * DH], 1, 8),
                        bdmask[:].rearrange("p (r d) -> p r d", r=8), ALU.mult), nsa_s["vbd"])
            late_begin(1)
            dve.wait_ge(nsa_s["scored"], 1)
            for t in range(NT):
                for g in range(2):
                    at = t * H + g * 8
                    done(STT(sc[:, at:at + 8, :].rearrange("p (r two) n -> p r (two n)", two=2),
                             G[2 * t + g][:].rearrange("p (r w) -> p r w", r=4)[:, :, 0:2 * NCMP], SCALE,
                             over(cneg[:, t, :], 1, 4), ALU.mult, ALU.add))
            done(dve.tensor_reduce(scm[:], sc[:], AX.X, ALU.max))
            done(TT(sc[:], sc[:], over(scm[:], 2, NCMP), ALU.subtract), nsa_s["cmp_sub"])
            dve.wait_ge(nsa_s["cmp_exp"], 1)
            for t in range(NT):
                part = sc[:, t * H:(t + 1) * H, :]
                done(TT(part, part, over(cone[:, t, :], 1, H), ALU.mult))
            done(dve.tensor_reduce(scm[:], sc[:], AX.X, ALU.add))
            done(TS(scm[:], scm[:], 1.0, None, ALU.max))
            done(dve.reciprocal(scm[:], scm[:]))
            done(TT(sc[:], sc[:], over(scm[:], 2, NCMP), ALU.mult), nsa_s["cmp_prob"])
            dve.wait_ge(nsa_s["gates_exp"], 1)
            done(TS(gate[:], gate[:], 1.0, None, ALU.add))
            done(dve.reciprocal(gate[:], gate[:]))
            gates = gate[:].rearrange("p t (h b) -> p t h b", b=3)
            dve.wait_ge(*turned_all("nsa_rot"))
            for b in range(4):
                t, g = b // 2, b % 2
                dve.wait_ge(nsa_s["cmp_out"], b + 1)
                done(TT(tok[:, t, g * 512:(g + 1) * 512].rearrange("p (h d) -> p h d", h=8), G[b][:].rearrange("p (h d) -> p h d", h=8),
                        over(gates[:, t, g * 8:(g + 1) * 8, 0], 2, DH), ALU.mult), nsa_s["cmp_summed"])

            def add_gated(j, o, r):
                h, branch = j % H, 1 + j // H
                done(TT(r, r, gates[:, :, h, branch], ALU.mult))
                for t in range(NT):
                    dst = tok[:, t, h * DH:(h + 1) * DH]
                    ins = STT(dst, o[:, t, :], r[:, t:t + 1], dst, ALU.mult, ALU.add)
                    tl.mark(ins, tl.own if t == 0 else att["outs"])

            GATED = (H - 4) * DH

            def late_steps(i):
                c = late_round(i, 5, 2)
                if c is not None and c + 3 < LATE_NSA:
                    late_begin(c + 3)
                c = late_round(i - 1, 4, 1)
                if c is not None:
                    late_take(c, G[LATE_BANK])
                if c == LATE_NSA - 1:
                    scale_gain(mod1)
                if i == 2 * H:
                    low("nsa_out", 0, 0, KT * OUT_W)
                    dve.wait_ge(att["outs"], att_base["nsa"] + 2 * H - 4)
                    dve.wait_ge(nsa_s["silu"], 1)
                    for t in range(NT):
                        done(TT(tok[:, t, 0:GATED], tok[:, t, 0:GATED], u[:, t, 1792:1792 + GATED], ALU.mult))

            dve.wait_ge(mod1_loaded, 32)
            late_begin(2)
            attention("nsa", lambda i: table("causal"), add_gated, between=late_steps)
            dve.wait_ge(att["outs"], att_base["nsa"] + 2 * H)
            for t in range(NT):
                done(TT(tok[:, t, GATED:], tok[:, t, GATED:], u[:, t, 1792 + GATED:2816], ALU.mult), out_ready)

            def norm_1(t):
                moments([], t, 4, False, EPS_RMS)
                ada_norm(1, mod1, t)

            project_out(0, "nsa_out", mod0[:, 2 * D:3 * D], lambda: low("dil_in", 0, 0, KT * DIL_W), norm_1, "h1")

            turn_low(dve, "h1", 1)
            low("dil_in", 0, 1, KT * DIL_W)
            with dve.Fori(1, DIL_C // 2) as i:
                for j in range(2):
                    low("dil_in", i, j, KT * DIL_W)
            tl.n[late["summed"].name] = LATE_NSA
            for c in range(LATE_NSA, LATE):
                late_begin(c)
                if c > LATE_NSA:
                    late_take(c - 1, S[(c - 1) % 2])
            late_take(LATE - 1, S[(LATE - 1) % 2])
            low("dil_out", 0, 0, KT * OUT_W)
            groups = (6, 5, 5)
            offs = (0, 6, 11, 16)
            group = [g for g, n in enumerate(groups) for _ in range(n)]
            dve.wait_ge(*turned_all("dil_rot"))
            top, share = glse[:, 6, 0:NT], glse[:, 5, 0:6].rearrange("p (t g) -> p t g", t=NT)

            def group_weights(i):
                if i == H + 1:
                    dve.wait_ge(att["probs"], 2 * (att_base["dil"] + H))
                    done(dve.tensor_reduce(top, negmax[:].rearrange("p h t -> p t h"), AX.X, ALU.min))
                    done(TT(lse[:, 0, :].rearrange("p (h t) -> p h t", t=NT), over(top, 1, H), negmax[:], ALU.subtract), dil_s["lse_in"])

            attention("dil", lambda i: table(f"dil{group[i]}"), set_head(0), between=group_weights)
            dve.wait_ge(dil_s["lse_out"], 1)
            done(TT(lse[:, 0, :].rearrange("p (h t) -> p h t", t=NT), lse[:, 0, :].rearrange("p (h t) -> p h t", t=NT), den[:, 0:H, :], ALU.mult))
            by_head = lse[:, 0, :].rearrange("p (h t) -> p t h", t=NT)
            for g in range(3):
                done(dve.tensor_reduce(share[:, :, g], by_head[:, :, offs[g]:offs[g + 1]], AX.X, ALU.add))
            for g in range(3):
                done(TS(share[:, :, g], share[:, :, g], 1.0 / groups[g], None, ALU.mult))
            done(dve.tensor_reduce(top, share, AX.X, ALU.add))
            done(dve.reciprocal(top, top))
            done(STT(share, share, 3.0, over(top, 2, 3), ALU.mult, ALU.mult))
            dve.wait_ge(dil_s["silu"], 1)
            for t in range(NT):
                for g in range(3):
                    lo, hi = offs[g] * DH, offs[g + 1] * DH
                    done(STT(tok[:, t, lo:hi], tok[:, t, lo:hi], share[:, t, g:g + 1], u[:, t, 3 * D + lo:3 * D + hi], ALU.mult, ALU.mult),
                         out_ready if g == 2 else None)
            g_final = next_vec()

            def norm_2(t):
                moments([], t, 4, False, EPS_RMS)
                dve.wait_ge(norm["rstd"], 2 * 2 + t + 1)
                done(STT(x[:, t, :], x[:, t, :], rstd[:, t:t + 1], g_final, ALU.mult, ALU.mult), norm["ready"])

            project_out(1, "dil_out", mod1[:, 2 * D:3 * D], lambda: low("ab_in", 0, 0, KT * AB_W), norm_2, "x0")
            note(mod1_used)
            note(vec_used)

            turn_low(dve, "x0", 1)
            low("ab_in", 0, 1, KT * AB_W)
            low("ab_in", 1, 0, KT * AB_W)
            low("ab_in", 1, 1, KT * AB_W)
            dve.wait_ge(proj["ab_in"]["taken"], 2 * 2)
            latents = ((0, 384, q_gain), (384, 256, kv_gain))
            for i, (lo, w, gain) in enumerate(latents):
                for t in range(NT):
                    moments([u[:, t, lo:lo + w]], t, 1, False, EPS_RMS)
                for t in range(NT):
                    dve.wait_ge(norm["rstd"], 2 * (3 + i) + t + 1)
                    ins = STT(tok[:, t, lo:lo + w], u[:, t, lo:lo + w], rstd[:, t:t + 1], gain, ALU.mult, ALU.mult)
                    done(ins, ab_s["c_ready"] if (i, t) == (1, 1) else None)
            low("uq", 0, 0, 3 * 768)
            for t in range(NT):
                rotate(tl, kr[:, t, :].rearrange("p (n d) -> p n d", n=1), u[:, t, 640:672].rearrange("p (n d) -> p n d", n=1),
                       cos_m, sin_m, 1, 16, t, flat)
                done(dve.tensor_copy(kcat[:, t, :].rearrange("p (h d) -> p h d", h=8)[:, :, DH:96], over(kr[:, t, :], 1, 8)))
            dve.wait_ge(proj["ab_in"]["taken"], 2 * AB_C)
            for t in range(NT):
                done(dve.tensor_copy(kswa[:, t, :].rearrange("p (g two d) -> p g two d", g=2, two=2),
                                     over(u[:, t, 1184:1312].rearrange("p (g d) -> p g d", g=2), 2, 2)))
            turn_low(dve, "ab_c")
            low("ukv", 0, 0, 2 * 1024)
            dve.wait_ge(proj["uq"]["taken"], 4)
            for t in range(NT):
                rotate(tl, qcat[:, t, :].rearrange("p (h d) -> p h d", h=8)[:, :, DH:96],
                       u[:, t, 1536:2304].rearrange("p (h d) -> p h d", h=8)[:, :, DH:96], cos_m, sin_m, 8, 16, t, flat,
                       ab_s["rot_ready"] if t == 1 else None)
            low("ab_out", 0, 0, KT * OUT_W)
            dve.wait_ge(*turned_all("ab_rot"))
            dve.wait_ge(swa_loaded, 16)
            attention("ab", lambda i: table("chunk") if i < 8 else bias8[:, (i - 8) * SW:(i - 7) * SW], set_head(0),
                      scale=lambda i: MLA_SCALE if i < 8 else SCALE, sink=lambda i: negsink[:, i - 8:i - 7] if i >= 8 else None)
            for t in range(NT):
                note(out_ready)
            note(swa_used)
            g5, b5 = next_vec(), next_vec()

            def before_ffn(i):
                def between():
                    low_ffn(ffn[i], 0, 0, gu, "gu")
                    low_ffn(ffn[i], 0, 0, dn, "dn")
                return between

            project_out(2, "ab_out", None, before_ffn(0), lambda t: layer_norm(5, g5, b5, 4, t), "f0")
            note(vec_used)
            note(vec_used)
            ffn_dve(0, "ffn0", "f0")
            g6, b6 = next_vec(), next_vec()
            ffn_out(0, "ffn0", lambda t: layer_norm(6, g6, b6, 2, t), "x1", lambda: low("cd_in", 0, 0, KT * CD_W))
            note(vec_used)
            note(vec_used)

            turn_low(dve, "x1", 1)
            low("cd_in", 0, 1, KT * CD_W)
            with dve.Fori(1, CD_C // 2) as i:
                for j in range(2):
                    low("cd_in", i, j, KT * CD_W)
            dve.wait_ge(proj["cd_in"]["taken"], 2 * 6)
            f = [fox[:, k, :].rearrange("p (t h) -> p t h", t=NT) for k in range(6)]
            done(TT(f[0], u[:, :, 1536:1544], over(forget, 1, NT), ALU.add))
            done(STT(f[1], f[0], -1.0, f[0], ALU.mult, ALU.max), cd_s["f_in"])
            done(TS(f[2], f[0], 0.0, None, ALU.min))
            qa = [qaug[:, t, :].rearrange("p (h d) -> p h d", h=8) for t in range(NT)]
            ka = [kaug[:, t, :].rearrange("p (h d) -> p h d", h=8) for t in range(NT)]
            for t in range(NT):
                done(dve.tensor_copy(qa[t][:, :, 0:DH], u[:, t, 0:512].rearrange("p (h d) -> p h d", h=8)))
                done(dve.tensor_copy(ka[t][:, :, 0:DH], u[:, t, 512:1024].rearrange("p (h d) -> p h d", h=8)))
                done(dve.memset(qa[t][:, :, DH + 1:DH + 2], 1.0))
                done(dve.memset(ka[t][:, :, DH:DH + 1], 1.0))
            for h in range(8):
                dve.wait_ge(cd_s["flipped"], h + 1)
                done(STT(bias8[:, h * SW:(h + 1) * SW], G[h % 4][:, 0:SW], 1.0 / SCALE, table("chunk"), ALU.mult, ALU.add), cd_s["bias_ready"])
            dve.wait_ge(cd_s["f_ln"], 1)
            done(TT(f[3], f[2], f[1], ALU.subtract), cd_s["f_ready"])
            dve.wait_ge(cd_s["cum"], 1)
            for t in range(NT):
                c = S[0][:, t * 8:(t + 1) * 8].unsqueeze(2)
                done(TS(qa[t][:, :, DH:DH + 1], c, 1.0 / SCALE, None, ALU.mult))
                done(TS(ka[t][:, :, DH + 1:DH + 2], c, -1.0 / SCALE, None, ALU.mult), cd_s["aug_ready"] if t == 1 else None)
            low("cd_out", 0, 0, KT * OUT_W)
            dve.wait_ge(*turned_all("cd_rot"))
            attention("cd", lambda i: table("causal") if i < 8 else bias8[:, (i - 8) * SW:(i - 7) * SW], set_head(0))
            for t in range(NT):
                note(out_ready)
            g7, b7 = next_vec(), next_vec()
            project_out(3, "cd_out", None, before_ffn(1), lambda t: layer_norm(7, g7, b7, 4, t), "f1")
            note(vec_used)
            note(vec_used)
            ffn_dve(1, "ffn1", "f1")
            g8, b8 = next_vec(), next_vec()
            ffn_out(1, "ffn1", lambda t: layer_norm(8, g8, b8, 2, t))


def shape_tables():
    f = np.float32
    tab = np.zeros((P, TAB_W), f)

    def put(name, v):
        lo, hi = TAB[name]
        tab[:, lo:hi] = np.asarray(v, f).reshape(P, hi - lo)

    def by_token(v):
        return v.reshape(NT, P, -1).transpose(1, 0, 2)

    put("ident", np.eye(P))
    put("flip", np.eye(P)[::-1])
    put("tri", np.triu(np.ones((P, P))))
    for half, c, s, inv in ((HALF, "cos", "sin", f(10000.0) ** (-np.arange(HALF, dtype=f) / f(HALF))),
                            (16, "cos_m", "sin_m", f(10000.0) ** (-np.arange(0, 32, 2, dtype=f) / f(32)))):
        ang = np.arange(T, dtype=f)[:, None] * inv.astype(f)[None, :]
        put(c, by_token(np.cos(ang)))
        put(s, by_token(np.sin(ang)))
    q, k = np.arange(T)[:, None], np.arange(T)[None, :]

    def packed(m):
        return np.concatenate([m[0:P, 0:P], m[P:, 0:P], m[P:, P:]], axis=-1)

    def hidden(seen):
        return packed(np.where(seen, 0.0, -1e30))

    put("causal", hidden(k <= q))
    put("dil0", hidden((k <= q) & (q - k <= 128)))
    put("dil1", hidden((k <= q) & ((q - k) % 4 == 0)))
    put("dil2", hidden((k <= q) & ((q - k) % 16 == 0)))
    put("chunk", hidden(k // 64 <= q // 64))
    seen = (16 * np.arange(NCMP) + 31)[None, :] <= np.arange(T)[:, None]
    put("cneg", by_token(np.tile(np.where(seen, 0.0, -1e30), (1, 2))))
    put("cone", by_token(np.where(seen, 1.0, 0.0)))
    near = (k // 64 <= q // 64) & (k // 64 >= q // 64 - 2)
    slopes = np.exp2(-8.0 * np.arange(1, 9) / 8)
    swa = np.stack([packed(np.where(near, -s * np.abs(q - k) / SCALE, -1e30)) for s in slopes], axis=1).reshape(P, 8 * SW).astype(f)
    bd = np.kron(np.eye(8), np.ones((NCMP, DH))).astype(f)
    return {"tables": tab, "swa_bias": swa, "bdmask": bd}


def tiles(w, width):
    k, n = w.shape
    return np.ascontiguousarray(w.reshape(k // P, P, n // width, width).transpose(2, 1, 0, 3)).reshape(n // width, P, -1)


def ffn_steps(gate, up, down):
    return np.concatenate([tiles(gate, P), tiles(up, P), down.reshape(FF_STEPS, P, D)], axis=2)


def kernel(**inputs):
    import concourse.bacc as bacc
    from concourse.bass_utils import run_bass_kernel_spmd

    v = {k: np.asarray(w) for k, w in inputs.items()}
    rel = v["cd_rel_bias_2"][0]
    arrays = {
        "x": v["x"],
        "c": np.ascontiguousarray(v["c"].reshape(KT, P).T),
        "ada_w0": tiles(v["ada_w"][0], ADA_W), "ada_w1": tiles(v["ada_w"][1], ADA_W), "ada_b": v["ada_b"],
        "nsa_w_in": tiles(np.concatenate([v["nsa_w_in"][0][:, D:D + NSA_Q], v["nsa_w_in"][0][:, 0:D], v["nsa_w_in"][0][:, D + NSA_Q:]], axis=1), NSA_W),
        "cmp_w1": np.stack([w[0].reshape(2, 8, P, 256).transpose(0, 2, 1, 3).reshape(2, P, 2048)
                            for w in (v["nsa_ck_w1"], v["nsa_cv_w1"])]).reshape(4, P, 2048),
        "cmp_w2": np.ascontiguousarray(np.stack([w[0].reshape(2, P, DH).transpose(1, 0, 2) for w in (v["nsa_ck_w2"], v["nsa_cv_w2"])], axis=1)),
        "pos": np.ascontiguousarray(np.stack([w[0].reshape(16, P) for w in (v["nsa_pe_k"], v["nsa_pe_v"])], axis=1)),
        "nsa_w_out": tiles(v["nsa_w_out"][0], OUT_W),
        "dil_w_in": tiles(v["dil_w_in"][0], DIL_W), "dil_w_out": tiles(v["dil_w_out"][0], OUT_W),
        "ab_w_in": tiles(v["ab_w_in_2"][0], AB_W), "ab_w_uq": tiles(v["ab_w_uq_2"][0], 768),
        "ab_w_ukv": tiles(v["ab_w_ukv_2"][0], 1024), "ab_w_out": tiles(v["ab_w_out_2"][0], OUT_W),
        "cd_w_in": tiles(v["cd_w_in_2"][0], CD_W), "cd_w_out": tiles(v["cd_w_out_2"][0], OUT_W),
        "ffn0": ffn_steps(v["ffn_w_gate_2"][0], v["ffn_w_up_2"][0], v["ffn_w_down_2"][0]),
        "ffn1": ffn_steps(v["ffn_w_gate_2"][1], v["ffn_w_up_2"][1], v["ffn_w_down_2"][1]),
        "vecs": np.stack([v["norm_g"][0], v["norm_g"][1], v["final_g"], v["ln1_g_2"][0], v["ln1_b_2"][0], v["ln2_g_2"][0],
                          v["ln2_b_2"][0], v["ln1_g_2"][1], v["ln1_b_2"][1], v["ln2_g_2"][1], v["ln2_b_2"][1]]),
        "q_norm": v["ab_q_norm_2"][0], "kv_norm": v["ab_kv_norm_2"][0], "sinks": v["ab_sinks_2"][0], "b_forget": v["cd_b_forget_2"][0],
        "rel_rev": np.pad(rel[318::-1].T, ((0, 0), (0, 512 - 319))),
        **shape_tables(),
    }
    arrays = {k: np.ascontiguousarray(w) for k, w in arrays.items()}
    nc = bacc.Bacc("TRN2", target_bir_lowering=False, num_devices=1)
    aps = {k: nc.dram_tensor(f"in_{k}", w.shape, mybir.dt.from_np(w.dtype), kind="ExternalInput").ap() for k, w in arrays.items()}
    out = nc.dram_tensor("out", v["x"].shape, F32, kind="ExternalOutput").ap()
    two_stacks(nc, aps, out)
    got = run_bass_kernel_spmd(nc, [{f"in_{k}": w for k, w in arrays.items()}], core_ids=[0])
    return got.results[0]["out"]
```
